# Optimizing a Trainium2 kernel written in Bass

```python
import math
import jax, jax.numpy as jnp
from jax import lax
import numpy as np

D_MODEL = 1024
BATCH = 1
SEQ = 1024
DEPTH = 1

DN_HEAD_DIM = 128
DN_WIDTH = D_MODEL // 2
DN_HEADS = DN_WIDTH // DN_HEAD_DIM
SHORT_CONV = 4
GLA_VAL_DIM = 128
GLA_WIDTH = D_MODEL - DN_WIDTH
GLA_HEADS = GLA_WIDTH // GLA_VAL_DIM
GLA_KEY_DIM = GLA_VAL_DIM // 2
GLA_GATE_RANK = 16
GLA_TAU = 16.0
MIX_WIDTH = DN_WIDTH + GLA_WIDTH
IN_SPLITS = (DN_WIDTH, DN_WIDTH, DN_WIDTH, DN_WIDTH, DN_HEADS, DN_HEADS,
             GLA_HEADS * GLA_KEY_DIM, GLA_HEADS * GLA_KEY_DIM, GLA_WIDTH, GLA_WIDTH, GLA_GATE_RANK)
IN_WIDTH = sum(IN_SPLITS)
CHUNK = 64
D_FF = 2816
FFN_CONV = 3
ALPHA = (2.0 * DEPTH) ** 0.25
BETA_INIT = (8.0 * DEPTH) ** -0.25
EPS = 1e-6


def layer_norm(x, g, b):
    xf = x.astype(jnp.float32)
    mu = xf.mean(-1, keepdims=True)
    var = jnp.square(xf - mu).mean(-1, keepdims=True)
    return ((xf - mu) * lax.rsqrt(var + EPS) * g.astype(jnp.float32) + b.astype(jnp.float32)).astype(x.dtype)

def rms_norm(x, g):
    xf = x.astype(jnp.float32)
    return (xf * lax.rsqrt(jnp.mean(xf * xf, -1, keepdims=True) + EPS) * g.astype(jnp.float32)).astype(x.dtype)

def l2_norm(x):
    return x * lax.rsqrt(jnp.sum(x * x, -1, keepdims=True) + EPS)

def causal_dwconv(x, w):
    k_w, ch = w.shape
    return lax.conv_general_dilated(x, w[:, None, :].astype(x.dtype), window_strides=(1,),
                                    padding=[(k_w - 1, 0)], dimension_numbers=('NWC', 'WIO', 'NWC'),
                                    feature_group_count=ch)

def to_chunks(x):
    b, t, h, d = x.shape
    return x.reshape(b, t // CHUNK, CHUNK, h, d).transpose(1, 0, 3, 2, 4)

def from_chunks(x):
    n, b, h, c, d = x.shape
    return x.transpose(1, 0, 3, 2, 4).reshape(b, n * c, h, d)

def gated_delta_rule(q, k, v, log_a, beta):
    dt = v.dtype
    q, k, v, log_a, beta = (a.astype(jnp.float32) for a in (q, k, v, log_a, beta))
    bsz, _, nh, dk = q.shape
    dv = v.shape[-1]
    qc, kc, vc = to_chunks(q * dk ** -0.5), to_chunks(k), to_chunks(v)
    G = jnp.cumsum(to_chunks(log_a[..., None])[..., 0], axis=-1)
    bc = to_chunks(beta[..., None])[..., 0]
    causal = jnp.tril(jnp.ones((CHUNK, CHUNK), dtype=bool))
    strict = jnp.tril(jnp.ones((CHUNK, CHUNK), dtype=bool), -1)
    decay = jnp.exp(jnp.where(causal, G[..., :, None] - G[..., None, :], -jnp.inf))
    kb = kc * bc[..., None]
    m_low = jnp.where(strict, jnp.einsum('nbhid,nbhjd->nbhij', kb, kc) * decay, 0.0)
    lhs = m_low + jnp.eye(CHUNK, dtype=jnp.float32)
    rhs = jnp.concatenate([vc * bc[..., None], kb * jnp.exp(G)[..., None]], axis=-1)
    sol = lax.linalg.triangular_solve(lhs, rhs, left_side=True, lower=True, unit_diagonal=True)
    u, w = sol[..., :dv], sol[..., dv:]
    attn = jnp.einsum('nbhid,nbhjd->nbhij', qc, kc) * decay
    q_dec = qc * jnp.exp(G)[..., None]
    k_dec = kc * jnp.exp(G[..., -1:] - G)[..., None]
    g_last = jnp.exp(G[..., -1])

    def step(S, inp):
        u_i, w_i, attn_i, qd_i, kd_i, gl_i = inp
        v_new = u_i - jnp.einsum('bhcd,bhde->bhce', w_i, S)
        o = jnp.einsum('bhcd,bhde->bhce', qd_i, S) + jnp.einsum('bhij,bhje->bhie', attn_i, v_new)
        S = S * gl_i[..., None, None] + jnp.einsum('bhcd,bhce->bhde', kd_i, v_new)
        return S, o

    S0 = jnp.zeros((bsz, nh, dk, dv), jnp.float32)
    _, o = lax.scan(step, S0, (u, w, attn, q_dec, k_dec, g_last))
    return from_chunks(o).astype(dt)

def gla_attention(q, k, v, log_alpha):
    dt = v.dtype
    q, k, v, log_alpha = (a.astype(jnp.float32) for a in (q, k, v, log_alpha))
    bsz, _, nh, dk = q.shape
    dv = v.shape[-1]
    qc, kc, vc = to_chunks(q * dk ** -0.5), to_chunks(k), to_chunks(v)
    b = jnp.cumsum(to_chunks(log_alpha), axis=-2)
    causal = jnp.tril(jnp.ones((CHUNK, CHUNK), dtype=bool))
    q_dec = qc * jnp.exp(b)
    attn = jnp.where(causal, jnp.einsum('nbhid,nbhjd->nbhij', q_dec, kc * jnp.exp(-b)), 0.0)
    o_intra = jnp.einsum('nbhij,nbhje->nbhie', attn, vc)
    k_dec = kc * jnp.exp(b[..., -1:, :] - b)
    g_last = jnp.exp(b[..., -1, :])

    def step(S, inp):
        qd_i, kd_i, v_i, oi_i, gl_i = inp
        o = jnp.einsum('bhcd,bhde->bhce', qd_i, S) + oi_i
        S = S * gl_i[..., :, None] + jnp.einsum('bhcd,bhce->bhde', kd_i, v_i)
        return S, o

    S0 = jnp.zeros((bsz, nh, dk, dv), jnp.float32)
    _, o = lax.scan(step, S0, (q_dec, k_dec, vc, o_intra, g_last))
    return from_chunks(o).astype(dt)

def hybrid_mixer(h, w_in, dn_conv, dn_a_log, dn_dt_bias, dn_norm_g, gla_w_gate2, gla_b_gate, gla_norm_g, w_o):
    bsz, t, _ = h.shape
    proj = h @ w_in
    offsets, acc = [], 0
    for s in IN_SPLITS[:-1]:
        acc += s
        offsets.append(acc)
    (dn_q, dn_k, dn_v, dn_z, dn_a, dn_b, gl_q, gl_k, gl_v, gl_g, gl_r) = jnp.split(proj, offsets, axis=-1)
    qkv = jax.nn.silu(causal_dwconv(jnp.concatenate([dn_q, dn_k, dn_v], -1), dn_conv))
    q, k, v = (a.reshape(bsz, t, DN_HEADS, DN_HEAD_DIM) for a in jnp.split(qkv, 3, axis=-1))
    log_a = -jnp.exp(dn_a_log) * jax.nn.softplus(dn_a + dn_dt_bias)
    beta = jax.nn.sigmoid(dn_b)
    o_dn = gated_delta_rule(l2_norm(q), l2_norm(k), v, log_a, beta)
    o_dn = rms_norm(o_dn, dn_norm_g) * jax.nn.silu(dn_z.reshape(bsz, t, DN_HEADS, DN_HEAD_DIM))
    log_alpha = jax.nn.log_sigmoid(gl_r @ gla_w_gate2 + gla_b_gate) / GLA_TAU
    o_gla = gla_attention(gl_q.reshape(bsz, t, GLA_HEADS, GLA_KEY_DIM),
                          gl_k.reshape(bsz, t, GLA_HEADS, GLA_KEY_DIM),
                          gl_v.reshape(bsz, t, GLA_HEADS, GLA_VAL_DIM),
                          log_alpha.reshape(bsz, t, GLA_HEADS, GLA_KEY_DIM))
    o_gla = rms_norm(o_gla, gla_norm_g) * jax.nn.silu(gl_g.reshape(bsz, t, GLA_HEADS, GLA_VAL_DIM))
    o = jnp.concatenate([o_dn.reshape(bsz, t, DN_WIDTH), o_gla.reshape(bsz, t, GLA_WIDTH)], axis=-1)
    return o @ w_o

def conv_ffn(h, w_up, conv_w, conv_b, w_down):
    u = causal_dwconv(h @ w_up, conv_w) + conv_b
    gate, val = jnp.split(u, 2, axis=-1)
    return (jax.nn.silu(gate) * val) @ w_down

def first_inputs(seed: int = 0) -> dict:
    key = jax.random.key(seed)
    ks = jax.random.split(key, 24)
    nrm = lambda k, shape, s: jax.random.normal(k, shape, jnp.float32) * s
    L, D = DEPTH, D_MODEL
    dt = jnp.exp(jax.random.uniform(ks[9], (L, DN_HEADS), jnp.float32, math.log(1e-3), math.log(1e-1)))
    return {
        "x": nrm(ks[0], (BATCH, SEQ, D), 1.0),
        "c": nrm(ks[1], (BATCH, D), 1.0),
        "ln0_g": 1.0 + nrm(ks[2], (D,), 0.02),
        "ln0_b": nrm(ks[3], (D,), 0.02),
        "w_ada": nrm(ks[4], (L, D, 6 * D), 0.1 * D ** -0.5),
        "b_ada": nrm(ks[5], (L, 6 * D), 0.01),
        "w_in": nrm(ks[6], (L, D, IN_WIDTH), D ** -0.5),
        "dn_conv": nrm(ks[7], (L, SHORT_CONV, 3 * DN_WIDTH), SHORT_CONV ** -0.5),
        "dn_a_log": jnp.log(jax.random.uniform(ks[8], (L, DN_HEADS), jnp.float32, 1.0, 16.0)),
        "dn_dt_bias": dt + jnp.log(-jnp.expm1(-dt)),
        "dn_norm_g": 1.0 + nrm(ks[10], (L, DN_HEAD_DIM), 0.02),
        "gla_w_gate2": nrm(ks[11], (L, GLA_GATE_RANK, GLA_HEADS * GLA_KEY_DIM), GLA_GATE_RANK ** -0.5),
        "gla_b_gate": nrm(ks[12], (L, GLA_HEADS * GLA_KEY_DIM), 0.01),
        "gla_norm_g": 1.0 + nrm(ks[13], (L, GLA_VAL_DIM), 0.02),
        "w_o": nrm(ks[14], (L, MIX_WIDTH, D), MIX_WIDTH ** -0.5 * BETA_INIT),
        "ln1_g": 1.0 + nrm(ks[15], (L, D), 0.02),
        "ln1_b": nrm(ks[16], (L, D), 0.02),
        "ffn_w_up": nrm(ks[17], (L, D, 2 * D_FF), D ** -0.5),
        "ffn_conv": nrm(ks[18], (L, FFN_CONV, 2 * D_FF), FFN_CONV ** -0.5),
        "ffn_conv_b": nrm(ks[19], (L, 2 * D_FF), 0.02),
        "ffn_w_down": nrm(ks[20], (L, D_FF, D), D_FF ** -0.5 * BETA_INIT),
        "ln2_g": 1.0 + nrm(ks[21], (L, D), 0.02),
        "ln2_b": nrm(ks[22], (L, D), 0.02),
    }

def first_block(x, c, ln0_g, ln0_b, w_ada, b_ada, w_in, dn_conv, dn_a_log, dn_dt_bias, dn_norm_g,
              gla_w_gate2, gla_b_gate, gla_norm_g, w_o, ln1_g, ln1_b, ffn_w_up, ffn_conv, ffn_conv_b,
              ffn_w_down, ln2_g, ln2_b):
    x = layer_norm(x, ln0_g, ln0_b)
    cond = jax.nn.silu(c)
    for l in range(DEPTH):
        mod = cond @ w_ada[l] + b_ada[l]
        sh_a, sc_a, gt_a, sh_f, sc_f, gt_f = jnp.split(mod[:, None, :], 6, axis=-1)
        h = x * (1.0 + sc_a) + sh_a
        y = hybrid_mixer(h, w_in[l], dn_conv[l], dn_a_log[l], dn_dt_bias[l], dn_norm_g[l],
                         gla_w_gate2[l], gla_b_gate[l], gla_norm_g[l], w_o[l])
        x = layer_norm(ALPHA * x + (1.0 + gt_a) * y, ln1_g[l], ln1_b[l])
        h = x * (1.0 + sc_f) + sh_f
        y = conv_ffn(h, ffn_w_up[l], ffn_conv[l], ffn_conv_b[l], ffn_w_down[l])
        x = layer_norm(ALPHA * x + (1.0 + gt_f) * y, ln2_g[l], ln2_b[l])
    return x


_first_inputs = first_inputs


def first_inputs(seed=0):
    import zlib

    import numpy as np

    out = dict(_first_inputs(seed))
    spreads = {}
    factors = {'b_ada': 5.024,
     'dn_norm_g': 8.0,
     'gla_b_gate': 8.0,
     'gla_norm_g': 8.0,
     'ln1_g': 2.74,
     'ln1_b': 2.749,
     'ffn_conv_b': 7.006,
     'ln2_g': 2.742,
     'ln2_b': 2.828}
    for name, (base, spread) in spreads.items():
        noise = np.random.default_rng([zlib.crc32(name.encode()), seed]).standard_normal(out[name].shape)
        drawn = base * np.exp(spread * noise) if base else spread * noise
        out[name] = __import__('jax').numpy.asarray(drawn.astype(out[name].dtype))
    for name, factor in factors.items():
        out[name] = (out[name] * factor).astype(out[name].dtype)
    return out


_narrow_inputs = first_inputs


def first_inputs(seed=0):

    out = dict(_narrow_inputs(seed))
    wider = {'dn_norm_g': 3.54, 'gla_norm_g': 3.88, 'ln2_g': 3.06, 'ln2_b': 3.08}
    for name, times in wider.items():
        mean = out[name].mean()
        out[name] = (mean + times * (out[name] - mean)).astype(out[name].dtype)
    return out


N_ATTN_HEADS = 8
HEAD_DIM = 64
ATTN_WIDTH = N_ATTN_HEADS * HEAD_DIM
N_RG_BLOCKS = 8
RG_WIDTH = 512
RG_BLOCK = RG_WIDTH // N_RG_BLOCKS
MIX_WIDTH_2 = ATTN_WIDTH + RG_WIDTH
IN_COLS = 3 * ATTN_WIDTH + 2 * RG_WIDTH
DILATED_PATTERNS = ((128, 1), (512, 4), (2048, 16))
BAND_BLOCK = 64
ROPE_THETA = 10000.0
CONV_WIDTH = 4
CONV_PAD_LEFT = 2
CONV_PAD_RIGHT = 1
RG_C = 8.0
N_MEM = 256
N_CROSS_HEADS = 4
CROSS_HEAD_DIM = 128
CROSS_WIDTH = N_CROSS_HEADS * CROSS_HEAD_DIM
D_FF_2 = 4 * D_MODEL
NORM_EPS = 1e-6
NEG_BIG = -1e30


def rmsnorm(x, g):
    xf = x.astype(jnp.float32)
    return xf * lax.rsqrt(jnp.mean(xf * xf, axis=-1, keepdims=True) + NORM_EPS) * g.astype(jnp.float32)

def rope(t, positions):
    half = t.shape[-1] // 2
    inv_freq = ROPE_THETA ** (-jnp.arange(half, dtype=jnp.float32) / half)
    ang = positions.astype(jnp.float32)[..., None] * inv_freq
    cos = jnp.cos(ang)[:, :, None, :]
    sin = jnp.sin(ang)[:, :, None, :]
    t1, t2 = t[..., :half], t[..., half:]
    return jnp.concatenate([t1 * cos - t2 * sin, t1 * sin + t2 * cos], axis=-1)

def banded_window_attention(q, k, v, radius):
    L, dh = q.shape[-2], q.shape[-1]
    blk = BAND_BLOCK
    nb = -(-L // blk)
    Lp = nb * blk
    lead = q.shape[:-2]
    nlead = len(lead)
    qb = jnp.pad(q, [(0, 0)] * nlead + [(0, Lp - L), (0, 0)]).reshape(*lead, nb, blk, dh)
    pad_both = [(0, 0)] * nlead + [(blk, Lp - L + blk), (0, 0)]
    kb = jnp.pad(k, pad_both).reshape(*lead, nb + 2, blk, dh)
    vb = jnp.pad(v, pad_both).reshape(*lead, nb + 2, blk, dh)
    kn = jnp.concatenate([kb[..., :-2, :, :], kb[..., 1:-1, :, :], kb[..., 2:, :, :]], axis=-2)
    vn = jnp.concatenate([vb[..., :-2, :, :], vb[..., 1:-1, :, :], vb[..., 2:, :, :]], axis=-2)
    s = jnp.einsum('...nqd,...nkd->...nqk', qb, kn) * (dh ** -0.5)
    qpos = jnp.arange(nb)[:, None] * blk + jnp.arange(blk)[None, :]
    kpos = (jnp.arange(nb)[:, None] - 1) * blk + jnp.arange(3 * blk)[None, :]
    dist = qpos[:, :, None] - kpos[:, None, :]
    valid = (jnp.abs(dist) <= radius) & (kpos[:, None, :] >= 0) & (kpos[:, None, :] < L)
    s = jnp.where(valid, s, NEG_BIG)
    m = jnp.max(s, axis=-1, keepdims=True)
    p = jnp.exp(s - m)
    denom = jnp.sum(p, axis=-1, keepdims=True)
    o = jnp.einsum('...nqk,...nkd->...nqd', p, vn) / denom
    lse = (m + jnp.log(denom))[..., 0]
    o = o.reshape(*lead, Lp, dh)[..., :L, :]
    lse = lse.reshape(*lead, Lp)[..., :L]
    return o, lse

def dilated_mixture_attention(q, k, v):
    B, S, H, dh = q.shape
    outs, lses = [], []
    for window, dil in DILATED_PATTERNS:
        L = S // dil

        def to_classes(t):
            return t.reshape(B, L, dil, H, dh).transpose(0, 2, 3, 1, 4)

        o, lse = banded_window_attention(to_classes(q), to_classes(k), to_classes(v), window // (2 * dil))
        outs.append(o.transpose(0, 3, 1, 2, 4).reshape(B, S, H, dh))
        lses.append(lse.transpose(0, 3, 1, 2).reshape(B, S, H))
    w = jax.nn.softmax(jnp.stack(lses, axis=0), axis=0)
    return jnp.sum(w[..., None] * jnp.stack(outs, axis=0), axis=0)

def centred_depthwise_conv(u, w, b):
    out = lax.conv_general_dilated(
        u, w[:, None, :].astype(u.dtype), window_strides=(1,),
        padding=[(CONV_PAD_LEFT, CONV_PAD_RIGHT)],
        dimension_numbers=('NWC', 'WIO', 'NWC'),
        feature_group_count=u.shape[-1])
    return out + b

def _linear_recurrence_combine(c1, c2):
    a1, b1 = c1
    a2, b2 = c2
    return a1 * a2, a2 * b1 + b2

def bidirectional_rglru(u, a_w, a_b, x_w, x_b, lam):
    B, S, _ = u.shape
    ug = u.reshape(B, S, N_RG_BLOCKS, RG_BLOCK)
    r = jax.nn.sigmoid(jnp.einsum('bsgi,zgij->zbsgj', ug, a_w) + a_b[:, None, None]).reshape(2, B, S, RG_WIDTH)
    i = jax.nn.sigmoid(jnp.einsum('bsgi,zgij->zbsgj', ug, x_w) + x_b[:, None, None]).reshape(2, B, S, RG_WIDTH)
    log_a = -RG_C * r * jax.nn.softplus(-lam.astype(jnp.float32))[:, None, None, :]
    a = jnp.exp(log_a)
    b = jnp.sqrt(-jnp.expm1(2.0 * log_a)) * (i * u[None])
    _, h_f = lax.associative_scan(_linear_recurrence_combine, (a[0], b[0]), axis=1)
    _, h_b = lax.associative_scan(_linear_recurrence_combine, (a[1], b[1]), axis=1, reverse=True)
    return h_f + h_b

def memory_cross_attention(xn, memn, wq, wk, wv, wo):
    B, S, _ = xn.shape
    M = memn.shape[1]
    q = (xn @ wq).reshape(B, S, N_CROSS_HEADS, CROSS_HEAD_DIM)
    k = (memn @ wk).reshape(B, M, N_CROSS_HEADS, CROSS_HEAD_DIM)
    v = (memn @ wv).reshape(B, M, N_CROSS_HEADS, CROSS_HEAD_DIM)
    s = jnp.einsum('bshd,bmhd->bhsm', q, k) * (CROSS_HEAD_DIM ** -0.5)
    p = jax.nn.softmax(s, axis=-1)
    o = jnp.einsum('bhsm,bmhd->bshd', p, v).reshape(B, S, CROSS_WIDTH)
    return o @ wo

def second_inputs(seed: int = 0) -> dict:
    key = jax.random.key(seed)
    ks = jax.random.split(key, 24)
    f32 = jnp.float32

    def nrm(k, shape, scale):
        return jax.random.normal(k, shape, f32) * scale

    def gain(k, shape):
        return 1.0 + 0.05 * jax.random.normal(k, shape, f32)

    lam_u = jax.random.uniform(ks[11], (DEPTH, 2, RG_WIDTH), f32, minval=0.9, maxval=0.999)
    a0 = lam_u ** (1.0 / RG_C)
    rg_lambda = jnp.log(a0) - jnp.log1p(-a0)
    return {
        "x": nrm(ks[0], (BATCH, SEQ, D_MODEL), 1.0),
        "mem": nrm(ks[1], (BATCH, N_MEM, D_MODEL), 1.0),
        "positions": jnp.broadcast_to(jnp.arange(SEQ, dtype=jnp.int32), (BATCH, SEQ)),
        "norm_mix_g": gain(ks[2], (DEPTH, D_MODEL)),
        "w_in": nrm(ks[3], (DEPTH, D_MODEL, IN_COLS), D_MODEL ** -0.5),
        "conv_w": nrm(ks[4], (DEPTH, CONV_WIDTH, RG_WIDTH), CONV_WIDTH ** -0.5),
        "conv_b": nrm(ks[5], (DEPTH, RG_WIDTH), 0.01),
        "rg_a_w": nrm(ks[6], (DEPTH, 2, N_RG_BLOCKS, RG_BLOCK, RG_BLOCK), RG_BLOCK ** -0.5),
        "rg_a_b": nrm(ks[7], (DEPTH, 2, N_RG_BLOCKS, RG_BLOCK), 0.01),
        "rg_x_w": nrm(ks[8], (DEPTH, 2, N_RG_BLOCKS, RG_BLOCK, RG_BLOCK), RG_BLOCK ** -0.5),
        "rg_x_b": nrm(ks[9], (DEPTH, 2, N_RG_BLOCKS, RG_BLOCK), 0.01),
        "rg_lambda": rg_lambda,
        "w_out": nrm(ks[10], (DEPTH, MIX_WIDTH_2, D_MODEL), MIX_WIDTH_2 ** -0.5),
        "norm_cross_g": gain(ks[12], (DEPTH, D_MODEL)),
        "norm_mem_g": gain(ks[13], (DEPTH, D_MODEL)),
        "w_cq": nrm(ks[14], (DEPTH, D_MODEL, CROSS_WIDTH), D_MODEL ** -0.5),
        "w_ck": nrm(ks[15], (DEPTH, D_MODEL, CROSS_WIDTH), D_MODEL ** -0.5),
        "w_cv": nrm(ks[16], (DEPTH, D_MODEL, CROSS_WIDTH), D_MODEL ** -0.5),
        "w_co": nrm(ks[17], (DEPTH, CROSS_WIDTH, D_MODEL), CROSS_WIDTH ** -0.5),
        "norm_mlp_g": gain(ks[18], (DEPTH, D_MODEL)),
        "w_mlp_in": nrm(ks[19], (DEPTH, D_MODEL, D_FF_2), D_MODEL ** -0.5),
        "w_mlp_out": nrm(ks[20], (DEPTH, D_FF_2, D_MODEL), D_FF_2 ** -0.5),
        "norm_final_g": gain(ks[21], (D_MODEL,)),
    }

def second_block(x, mem, positions, norm_mix_g, w_in, conv_w, conv_b, rg_a_w, rg_a_b, rg_x_w, rg_x_b,
              rg_lambda, w_out, norm_cross_g, norm_mem_g, w_cq, w_ck, w_cv, w_co,
              norm_mlp_g, w_mlp_in, w_mlp_out, norm_final_g):
    B, S, _ = x.shape
    h = x.astype(jnp.float32)
    memf = mem.astype(jnp.float32)
    for l in range(DEPTH):
        xn = rmsnorm(h, norm_mix_g[l])
        proj = xn @ w_in[l]
        q, k, v, u, y = jnp.split(proj, [ATTN_WIDTH, 2 * ATTN_WIDTH, 3 * ATTN_WIDTH,
                                         3 * ATTN_WIDTH + RG_WIDTH], axis=-1)
        q = rope(q.reshape(B, S, N_ATTN_HEADS, HEAD_DIM), positions)
        k = rope(k.reshape(B, S, N_ATTN_HEADS, HEAD_DIM), positions)
        v = v.reshape(B, S, N_ATTN_HEADS, HEAD_DIM)
        attn = dilated_mixture_attention(q, k, v).reshape(B, S, ATTN_WIDTH)
        uc = centred_depthwise_conv(u, conv_w[l], conv_b[l])
        rec = bidirectional_rglru(uc, rg_a_w[l], rg_a_b[l], rg_x_w[l], rg_x_b[l], rg_lambda[l]) * jax.nn.gelu(y)
        h = h + jnp.concatenate([attn, rec], axis=-1) @ w_out[l]
        h = h + memory_cross_attention(rmsnorm(h, norm_cross_g[l]), rmsnorm(memf, norm_mem_g[l]),
                                       w_cq[l], w_ck[l], w_cv[l], w_co[l])
        hid = jnp.square(jax.nn.relu(rmsnorm(h, norm_mlp_g[l]) @ w_mlp_in[l]))
        h = h + hid @ w_mlp_out[l]
    return rmsnorm(h, norm_final_g).astype(x.dtype)


def setup_inputs(seed=0):
    out = dict(first_inputs(seed))
    for name, value in second_inputs(seed + 1).items():
        if name != "x":
            out[name + "_2"] = value
    return out


def reference(
    x, c, ln0_g, ln0_b, w_ada, b_ada, w_in, dn_conv, dn_a_log, dn_dt_bias, dn_norm_g,
    gla_w_gate2, gla_b_gate, gla_norm_g, w_o, ln1_g, ln1_b, ffn_w_up, ffn_conv, ffn_conv_b,
    ffn_w_down, ln2_g, ln2_b, mem_2, positions_2, norm_mix_g_2, w_in_2, conv_w_2, conv_b_2,
    rg_a_w_2, rg_a_b_2, rg_x_w_2, rg_x_b_2, rg_lambda_2, w_out_2, norm_cross_g_2, norm_mem_g_2,
    w_cq_2, w_ck_2, w_cv_2, w_co_2, norm_mlp_g_2, w_mlp_in_2, w_mlp_out_2, norm_final_g_2,
):
    x = first_block(
        x, c, ln0_g, ln0_b, w_ada, b_ada, w_in, dn_conv, dn_a_log, dn_dt_bias, dn_norm_g,
        gla_w_gate2, gla_b_gate, gla_norm_g, w_o, ln1_g, ln1_b, ffn_w_up, ffn_conv, ffn_conv_b,
        ffn_w_down, ln2_g, ln2_b,
    )
    return second_block(
        x, mem_2, positions_2, norm_mix_g_2, w_in_2, conv_w_2, conv_b_2, rg_a_w_2, rg_a_b_2,
        rg_x_w_2, rg_x_b_2, rg_lambda_2, w_out_2, norm_cross_g_2, norm_mem_g_2, w_cq_2, w_ck_2,
        w_cv_2, w_co_2, norm_mlp_g_2, w_mlp_in_2, w_mlp_out_2, norm_final_g_2,
    )


_drawn_inputs = setup_inputs


def setup_inputs(seed=0):
    import zlib

    import numpy as np

    out = dict(_drawn_inputs(seed))
    spreads = {}
    factors = {'norm_mix_g_2': 2.737,
     'conv_b_2': 3.43,
     'rg_a_b_2': 8.0,
     'rg_x_b_2': 8.0,
     'norm_cross_g_2': 8.0,
     'norm_mem_g_2': 8.0,
     'norm_mlp_g_2': 8.0}
    for name, (base, spread) in spreads.items():
        noise = np.random.default_rng([zlib.crc32(name.encode()), seed]).standard_normal(out[name].shape)
        drawn = base * np.exp(spread * noise) if base else spread * noise
        out[name] = __import__('jax').numpy.asarray(drawn.astype(out[name].dtype))
    for name, factor in factors.items():
        out[name] = (out[name] * factor).astype(out[name].dtype)
    return out
```

```python
import math
from contextlib import ExitStack, contextmanager

import concourse.bass as bass
from concourse import mybir

F32 = mybir.dt.float32
I32 = mybir.dt.int32
ALU = mybir.AluOpType
ACT = mybir.ActivationFunctionType
AX = mybir.AxisListType.X

P = 128
BANK = 512
D = 1024
KD = D // P
T = 1024
NT = T // P
HALVES = T // BANK
EPS = 1e-6
ALPHA = 2.0 ** 0.25
DN_HEADS, GLA_HEADS = 4, 4
DN_W, GLA_W, GLA_K = 512, 512, 64
O_Q, O_K, O_V, O_Z, O_A = 0, 512, 1024, 1536, 2048
O_GQ, O_GK, O_GV, O_GG, O_GR = 2056, 2312, 2568, 3080, 3592
RANK = 16
TAU = 16.0
GC = 64
NGC = T // GC
FF = 2816
NFF = FF // P
HEADS, HD = 8, 64
RADIUS = 64
MEM = 256
CROSS = 4
FF2 = 4096
NFF2 = FF2 // P
PANEL = 2048
SLOTS = 4


class Mark:

    def __init__(self, counter, count, loop, back=0):
        self.counter, self.count, self.loop, self.back = counter, count, loop, back

    def value(self, program):
        if self.loop is None:
            return self.count * self.counter.step
        per = self.loop.per(self.counter)
        if program.loop is self.loop:
            return program.loop.i * (per * self.counter.step) + (self.count - self.back * per) * self.counter.step
        return (self.count + (self.loop.n - 1) * per) * self.counter.step


class Counter:
    def __init__(self, program, name, step=1):
        self.sem = program.stack.enter_context(program.nc.semaphore(name))
        self.program, self.name, self.step, self.count = program, name, step, 0
        program.counters.append(self)

    def inc(self, ins):
        ins.then_inc(self.sem, self.step)
        self.count += 1
        return Mark(self, self.count, self.program.loop)


class Queue:

    def __init__(self, program, engine, name, chain):
        self.program, self.engine, self.name, self.chain, self.last = program, engine, name, chain, None
        self.done = Counter(program, f"{name}_done")
        self.passed = {}

    def wait(self, *marks):
        need = {}
        for m in marks:
            here = m.loop is not None and m.loop is self.program.loop
            order = (1, -m.back, m.count) if here else (0, 0, m.value(self.program))
            if m.counter.name not in need or need[m.counter.name][0] < order:
                need[m.counter.name] = (order, m)
        need = {name: m for name, (_, m) in need.items()}
        for m in need.values():
            v = m.value(self.program)
            if self.program.loop is None:
                if self.passed.get(m.counter.name, 0) >= v:
                    continue
                self.passed[m.counter.name] = v
            self.engine.wait_ge(m.counter.sem, v)

    def __call__(self, f, *args, after=(), chain=None, **kw):
        own = [self.last] if (self.chain if chain is None else chain) and self.last is not None else []
        self.wait(*after, *own)
        self.last = self.done.inc(f(*args, **kw))
        return self.last


class Loop:
    def __init__(self, program, name, n, i):
        self.program, self.name, self.n, self.i = program, name, n, i
        self.start = {s.name: s.count for s in program.counters}

    def per(self, signal):
        return self.program.plan.get(self.name, {}).get("per", {}).get(signal.name, 0)


class Program:

    def __init__(self, nc, plan, stack):
        self.nc, self.plan, self.stack = nc, plan, stack
        self.counters, self.loop, self.free, self.new_plan = [], None, {}, {}
        self.pe = Queue(self, nc.tensor, "pe", False)
        self.v = Queue(self, nc.vector, "dve", True)
        self.a = Queue(self, nc.scalar, "act", True)
        self.g = Queue(self, nc.gpsimd, "pool", True)
        self.sp = Queue(self, nc.sync, "sp", False)
        self.engines = [self.pe, self.v, self.a, self.g]

    def barrier(self):
        marks = [Mark(q.done, q.done.count, None) for q in self.engines if q.done.count]
        for q in self.engines:
            q.wait(*marks)
            q.last = None

    @contextmanager
    def repeat(self, name, n):
        self.barrier()
        carried = self.plan.get(name, {}).get("free", {})
        for key in carried:
            if key.startswith("slot"):
                self.sp.wait(*self.free.get(key, ()))
        before = dict(self.free)
        with self.nc.Fori(0, n) as i:
            loop = Loop(self, name, n, i)
            self.loop = loop
            by_name = {s.name: s for s in self.counters}
            for key, marks in carried.items():
                self.free[key] = [Mark(by_name[s], loop.start[s] + k, loop, 1) for s, k in marks]
            for q in self.engines:
                q.last = self.free.get(f"last_{q.name}", [None])[0]
            yield i
            for q in self.engines:
                if q.last is not None:
                    self.free[f"last_{q.name}"] = [q.last]
            per = {s.name: s.count - loop.start.get(s.name, 0) for s in self.counters}
            free = {key: [(m.counter.name, m.count - loop.start[m.counter.name]) for m in marks]
                    for key, marks in self.free.items()
                    if any(m.loop is loop and not m.back for m in marks) and marks is not before.get(key)}
            self.new_plan[name] = {"per": per, "free": free}
            self.loop = None
        for s in self.counters:
            if s.name in loop.start:
                s.count = loop.start[s.name] + n * per[s.name]
        for q in self.engines + [self.sp]:
            q.passed = {}
            q.last = None
        self.barrier()


def build(nc, dram, plan):
    with ExitStack() as stack:
        program = Program(nc, plan, stack)
        emit(nc, program, stack, dram)
        return program.new_plan


def softplus(x, out, one, A, V, act, dve, after):
    V(dve.tensor_scalar, out[:], x[:], 0.0, None, ALU.max)
    m = V(dve.scalar_tensor_tensor, x[:], out[:], -2.0, x[:], ALU.mult, ALU.add)
    A(act.activation, x[:], x[:], ACT.Exp, after=[m])
    m = A(act.activation, x[:], x[:], ACT.Ln, bias=one[:], scale=1.0)
    return V(dve.tensor_tensor, out[:], out[:], x[:], ALU.add, after=[m])


def emit(nc, pr, stack, dram):
    PE, V, A, G, SP = pr.pe, pr.v, pr.a, pr.g, pr.sp
    te, dve, act, pool = nc.tensor, nc.vector, nc.scalar, nc.gpsimd
    debug = dram.get("debug", {})

    times = {}

    def sb(name, shape, dt=F32, where=None):
        times[name] = times.get(name, 0) + 1
        name = name if times[name] == 1 else f"{name}_{times[name]}"
        return (where or stack).enter_context(nc.sbuf_tensor(name, shape, dt))

    def spread(ap, axis, n):
        a = ap.unsqueeze(axis)
        shape = list(a.shape)
        shape[axis] = n
        return a.broadcast_to(shape)

    def loads(name):
        return Counter(pr, f"{name}_loaded", 16)

    vectors_loaded = loads("vectors")

    banks = [stack.enter_context(nc.psum_tensor(f"bank{n}", [P, BANK], F32)) for n in range(8)]
    turn = [0]

    def bank():
        n = turn[0] % 8
        turn[0] += 1
        PE.wait(*pr.free.get(f"bank{n}", ()))
        return n, banks[n]

    def emptied(n, *marks):
        pr.free[f"bank{n}"] = list(marks)

    panels = [sb(f"panel{n}", [P, PANEL]) for n in range(SLOTS)]
    arrived = [Counter(pr, f"panel{n}_arrived", 16) for n in range(SLOTS)]
    slot_turn = [0]

    def load_panel(*sources):
        n = slot_turn[0] % SLOTS
        slot_turn[0] += 1
        SP.wait(*pr.free.get(f"slot{n}", ()))
        a, b, c = sources[0].shape[1], len(sources), sources[0].shape[2]
        view = panels[n][:, 0:a * b * c].rearrange("p (a b c) -> p a b c", a=a, b=b)
        for g, src in enumerate(sources):
            mark = arrived[n].inc(nc.sync.dma_start(view[:, :, g, :], src))
        return n, view.rearrange("p a b c -> p a (b c)"), mark

    def used(n, mark):
        pr.free[f"slot{n}"] = [mark]

    def rows_of(w, r0, nr, c0, ncol):
        return w[bass.ds(r0, nr) if not isinstance(r0, int) else slice(r0, r0 + nr),
                 bass.ds(c0, ncol) if not isinstance(c0, int) else slice(c0, c0 + ncol)].rearrange(
                     "(k p) c -> p k c", p=P)

    def dump(name, ap):
        if name in debug:
            pr.barrier()
            SP.wait(*[Mark(q.done, q.done.count, None) for q in pr.engines if q.done.count])
            m = loads("dump_" + name).inc(nc.sync.dma_start(debug[name], ap))
            for q in pr.engines:
                q.wait(m)

    ident = sb("ident", [P, P])
    ones = sb("ones", [P, P])
    upper = sb("upper", [P, P])
    m_ones = G(pool.memset, ones[:], 1.0)
    G(pool.affine_select, out=ident[:], in_=ones[:], compare_op=ALU.is_equal, fill=0.0, base=0,
      pattern=[[-1, P]], channel_multiplier=1)
    G(pool.affine_select, out=upper[:], in_=ones[:], compare_op=ALU.is_ge, fill=0.0, base=0,
      pattern=[[1, P]], channel_multiplier=-1)

    vectors = [("c", dram["c"]), ("ln0_g", dram["ln0_g"]), ("ln0_b", dram["ln0_b"]), ("b_ada", dram["b_ada"]),
               ("dn_conv", dram["dn_conv"]), ("ln1_g", dram["ln1_g"]), ("ln1_b", dram["ln1_b"]),
               ("dn_norm_g", dram["dn_norm_g"]), ("gla_norm_g", dram["gla_norm_g"]),
               ("gla_b_gate", dram["gla_b_gate"]), ("ffn_conv", dram["ffn_conv"]),
               ("ffn_conv_b", dram["ffn_conv_b"]), ("norm_mix_g", dram["norm_mix_g_2"]),
               ("norm_cross_g", dram["norm_cross_g_2"]), ("norm_mem_g", dram["norm_mem_g_2"]),
               ("norm_mlp_g", dram["norm_mlp_g_2"]), ("conv_w", dram["conv_w_2"]),
               ("conv_b", dram["conv_b_2"]), ("rg_a_b", dram["rg_a_b_2"]), ("rg_x_b", dram["rg_x_b_2"]),
               ("rg_lambda", dram["rg_lambda_2"])]
    first_col, n_rows = {}, 0
    for name, ap in vectors:
        first_col[name] = n_rows
        n_rows += ap.size() // P
    n_vt = -(-n_rows // P)
    cols = sb("cols", [P, n_vt * P])
    vr = ExitStack()
    vec_rows = sb("vec_rows", [P, n_vt, P], where=vr)
    m_zero = V(dve.memset, vec_rows[:], 0.0)
    SP.wait(m_zero)
    for name, ap in vectors:
        flat = ap
        while len(flat.shape) > 1:
            names = " ".join("abcdef"[:len(flat.shape)])
            flat = flat.rearrange(f"{names} -> ({names})")
        flat = flat.rearrange("(r p) -> r p", p=P)
        at, n = first_col[name], ap.size() // P
        done = 0
        while done < n:
            tile, row = divmod(at + done, P)
            take = min(n - done, P - row)
            m_vec = vectors_loaded.inc(nc.sync.dma_start(vec_rows[row:row + take, tile, :], flat[done:done + take, :]))
            done += take

    def col(name, n=0, count=1):
        return cols[:, first_col[name] + n:first_col[name] + n + count]

    PE.wait(m_vec, G.last)
    for n in range(n_vt):
        b, ps = bank()
        m = PE(te.transpose, ps[:, 0:P], vec_rows[:, n, :], ident[:])
        emptied(b, V(dve.tensor_copy, cols[:, n * P:(n + 1) * P], ps[:, 0:P], after=[m]))
    cols_ready = V.last
    pr.barrier()
    vr.close()

    resid = sb("resid", [P, NT, D])
    ft = sb("ft", [P, KD, T])

    def rsqrt(out, in_, bias_tile, scale, after=()):
        A(act.activation, out, in_, ACT.Ln, bias=bias_tile, scale=scale, after=after)
        return A(act.activation, out, out, ACT.Exp, scale=-0.5)

    eps_col = sb("eps_col", [P, 1])
    V(dve.memset, eps_col[:], EPS)
    eps_q = sb("eps_q", [P, 1])
    V(dve.memset, eps_q[:], EPS * P)
    stats = sb("stats", [P, 2, 6])
    moments = sb("moments", [P, 2])
    held = sb("held", [P, 1])
    rstd = sb("rstd", [P, 1])

    def to_features(src, dst, tok0, n_tok, scale, bias, after):
        for q in range(KD // 4):
            b, ps = bank()
            PE.wait(*after)
            for k in range(4):
                m = te.transpose(ps[:, k * P:k * P + n_tok], src[0:n_tok, (4 * q + k) * P:(4 * q + k + 1) * P],
                                 ident[0:n_tok, 0:n_tok])
            m = PE.done.inc(m)
            ends = []
            for k in range(4):
                kk = 4 * q + k
                o = dst[:, kk, bass.ds(tok0, n_tok)]
                if q == 0:
                    e = V(dve.tensor_scalar, o, ps[:, k * P:k * P + n_tok], scale(kk),
                          bias(kk) if bias else None, ALU.mult, ALU.add if bias else ALU.bypass,
                          after=[m], chain=False)
                elif bias:
                    e = A(act.activation, o, ps[:, k * P:k * P + n_tok], ACT.Identity, scale=scale(kk),
                          bias=bias(kk), after=[m], chain=False)
                else:
                    e = A(act.activation, o, ps[:, k * P:k * P + n_tok], ACT.Copy, scale=scale(kk), after=[m],
                          chain=False)
                ends.append(e)
            emptied(b, ends[-1])
        pr.free["xhat"] = [m]
        return ends[-1]

    def rms_heads(ps, m, tmp, out, gain):
        flat = tmp[:].rearrange("p a b -> p (a b)")
        m = A(act.activation, flat, ps[:], ACT.Square, after=[m, *pr.free.get("sq", ())])
        b, ps2 = bank()
        m = PE(te.matmul, ps2[:], ones[:], flat, start=True, stop=True, after=[m])
        A(act.activation, flat, ps2[:], ACT.Ln, bias=eps_col[:], scale=1.0 / P, after=[m])
        emptied(b, A.last)
        m = A(act.activation, flat, flat, ACT.Exp, scale=-0.5)
        m = V(dve.scalar_tensor_tensor, out, ps[:].rearrange("p (h c) -> p h c", h=4), gain, tmp[:], ALU.mult,
              ALU.mult, after=[m])
        pr.free["sq"] = [m]
        return m

    def layer_norm_tile(x, row_g, row_b, after=()):
        for n in range(2):
            V(dve.bn_stats, stats[:, n, :], x[:, n * BANK:(n + 1) * BANK], after=after)
        V(dve.memset, held[:], 0.0)
        V(dve.bn_aggr, moments[:], stats[:].rearrange("p a b -> p (a b)"), chain=False)
        m = rsqrt(rstd[:], moments[:, 1:2], eps_col[:], 1.0, after=[V.last])
        n = V(dve.tensor_scalar, xhat[:], x, moments[:, 0:1], rstd[:], ALU.subtract, ALU.mult,
              after=[m, *pr.free.get("xhat", ())])
        V(dve.tensor_tensor, x, xhat[:], row_g, ALU.mult)
        V(dve.tensor_tensor, x, x, row_b, ALU.add)
        return n

    square, xhat, norm_rows = None, None, None

    @contextmanager
    def norm_space():
        nonlocal square, xhat, norm_rows
        pr.barrier()
        with ExitStack() as ph:
            norm_rows = sb("norm_rows", [P, 2, D], where=ph)
            xhat = sb("xhat", [P, D], where=ph)
            square = sb("square", [P, D], where=ph)
            yield ph
            pr.barrier()

    def rms_norm_tile(x, out, after=()):
        A(act.activation, square[:], x, ACT.Square, accum_out=moments[:, 0:1], after=after)
        m = rsqrt(rstd[:], moments[:, 0:1], eps_col[:], 1.0 / D, after=pr.free.get("rstd", ()))
        m = V(dve.tensor_scalar, out, x, rstd[:], None, ALU.mult, after=[m, *pr.free.get("xhat", ())])
        pr.free["rstd"] = [m]
        return m

    b1 = ExitStack()
    gate_row = sb("gate_row", [P, 2, D])
    in_scale = sb("in_scale", [P, 2, KD])
    in_bias = sb("in_bias", [P, 2, KD])
    mod_row = sb("mod_row", [P, 6, D], where=b1)
    with ExitStack() as ph:
        cond = sb("cond", [P, KD], where=ph)
        cond_b = sb("cond_b", [P, KD, P], where=ph)
        A(act.activation, cond[:], col("c", 0, KD), ACT.Silu, after=[cols_ready])
        m_cond = V(dve.tensor_copy, cond_b[:], spread(cond[:], 2, P), after=[A.last])
        w_ada = dram["w_ada"][0]
        m_b = loads("b_ada").inc(nc.sync.dma_start(mod_row[:].rearrange("p a b -> p (a b)"),
                                               dram["b_ada"][0].partition_broadcast(P)))
        PE.wait(m_cond)
        V.wait(m_b)
        with pr.repeat("ada", 6) as i:
            for n in range(2):
                b, ps = bank()
                for h in range(2):
                    s, w, m = load_panel(rows_of(w_ada, 0, D, i * D + (2 * n + h) * 256, 256))
                    PE.wait(m)
                    for k in range(KD):
                        mm = te.matmul(ps[:, h * 256:(h + 1) * 256], cond_b[:, k, :], w[:, k, :],
                                       start=(k == 0), stop=(k == KD - 1))
                    mm = PE.done.inc(mm)
                    used(s, mm)
                o = mod_row[:, bass.ds(i, 1), n * BANK:(n + 1) * BANK].rearrange("p a b -> p (a b)")
                emptied(b, V(dve.tensor_tensor, o, ps[:], o, ALU.add, after=[mm]))
    dump("mod", mod_row[0:1, :, :].rearrange("p a b -> p (a b)"))
    SH_A, SC_A, GT_A, SH_F, SC_F, GT_F = range(6)

    mod_col = sb("mod_col", [P, 4, KD], where=b1)
    square = sb("mod_diagonal", [P, D], where=b1)
    for n, part in enumerate((SH_A, SC_A, SH_F, SC_F)):
        for k in range(KD):
            V(dve.tensor_tensor, square[:, k * P:(k + 1) * P], mod_row[:, part, k * P:(k + 1) * P], ident[:],
              ALU.mult, chain=k == 0)
        V(dve.tensor_reduce, mod_col[:, n, :], square[:].rearrange("p (k c) -> p k c", k=KD), AX, ALU.add)
    for n, (g, b) in enumerate((("ln0_g", "ln0_b"), ("ln1_g", "ln1_b"))):
        V(dve.tensor_scalar, mod_col[:, 2 * n + 1, :], mod_col[:, 2 * n + 1, :], 1.0, None, ALU.add)
        V(dve.tensor_tensor, in_scale[:, n, :], mod_col[:, 2 * n + 1, :], col(g, 0, KD), ALU.mult)
        V(dve.tensor_tensor, in_bias[:, n, :], mod_col[:, 2 * n + 1, :], col(b, 0, KD), ALU.mult)
        V(dve.tensor_tensor, in_bias[:, n, :], in_bias[:, n, :], mod_col[:, 2 * n, :], ALU.add)
    for n, part in enumerate((GT_A, GT_F)):
        V(dve.tensor_scalar, gate_row[:, n, :], mod_row[:, part, :], 1.0, None, ALU.add)

    pr.barrier()
    b1.close()

    def load_norm_rows(g, b=None):
        SP.wait(*[Mark(q.done, q.done.count, None) for q in (V, A) if q.done.count])
        sig = loads(f"rows_{g}")
        m = sig.inc(nc.sync.dma_start(norm_rows[:, 0, :], vector_of(g).partition_broadcast(P)))
        if b:
            m = sig.inc(nc.sync.dma_start(norm_rows[:, 1, :], vector_of(b).partition_broadcast(P)))
        return m

    def vector_of(name):
        v = dram[name]
        return v[0] if len(v.shape) == 2 else v

    nsp = norm_space()
    nsp.__enter__()
    m_rows = load_norm_rows("ln0_g", "ln0_b")
    m_x = loads("x").inc(nc.sync.dma_start(resid[:], dram["x"][0].rearrange("(n p) d -> p n d", p=P)))
    V.wait(m_x, m_rows)
    with pr.repeat("norm0", NT) as i:
        x = resid[:, bass.ds(i, 1), :].rearrange("p a b -> p (a b)")
        m = layer_norm_tile(x, norm_rows[:, 0, :], norm_rows[:, 1, :])
        to_features(xhat, ft, i * P, P, lambda k: in_scale[:, 0, k:k + 1], lambda k: in_bias[:, 0, k:k + 1], [m])
    nsp.__exit__(None, None, None)
    dump("x0", resid[:])
    dump("h0", ft[:])

    def project(w, c0, n_cols, done, width=None):
        for base in range(0, n_cols, 256):
            n_here = min(256, n_cols - base)
            s, wt, m = load_panel(rows_of(w, 0, D, c0 + base, n_here))
            PE.wait(m)
            for c in range(0, n_here, P):
                cw = min(P, n_here - c)
                for h in range(HALVES):
                    b, ps = bank()
                    for k in range(KD):
                        mm = te.matmul(ps[0:cw, :], wt[:, k, c:c + cw], ft[:, k, h * BANK:(h + 1) * BANK],
                                       start=(k == 0), stop=(k == KD - 1))
                    mm = PE.done.inc(mm)
                    emptied(b, done((base + c) // P, h, ps[0:cw, :], mm))
            used(s, mm)

    def project_tokens(src, n_k, w, r0, take):
        for h in range(2):
            parts = [load_panel(rows_of(w, r0 + 4 * P * n, 4 * P, h * BANK, BANK)) for n in range(n_k // 4)]
            PE.wait(*[m for _, _, m in parts])
            for n in range(NT):
                b, ps = bank()
                for k in range(n_k):
                    m = te.matmul(ps[:], src(k, n), parts[k // 4][1][:, k % 4, :], start=(k == 0),
                                  stop=(k == n_k - 1))
                m = PE.done.inc(m)
                emptied(b, take(h, n, ps, m))
            for s, _, _ in parts:
                used(s, m)

    w_in = dram["w_in"][0]
    mixed_space = ExitStack()
    mixed = sb("mixed", [P, 8, T], where=mixed_space)
    mx = ExitStack()

    v_feat = sb("v_feat", [P, 4, T], where=mx)
    cv = ExitStack()
    pre = [sb(f"conv_in{n}", [P, 3 + T], where=cv) for n in range(2)]
    conv = [sb(f"conv_out{n}", [P, T], where=cv) for n in range(2)]
    taps = sb("taps", [P, 12, 4], where=cv)
    tap_now = sb("tap_now", [P, 4, 4], where=cv)
    V(dve.tensor_copy, taps[:], col("dn_conv", 0, 48).rearrange("p (j c) -> p c j", j=4))
    for n in range(2):
        V(dve.memset, pre[n][:, 0:3], 0.0)

    def causal_conv(buf, n, w, n_taps, bias=None, conv=conv):
        lead = 3 - (n_taps - 1)
        V(dve.tensor_scalar, conv[n][:], buf[:, lead:lead + T], w(0), bias, ALU.mult,
          ALU.add if bias is not None else ALU.bypass, after=pr.free.get(f"conv{n}", ()))
        for j in range(1, n_taps):
            V(dve.scalar_tensor_tensor, conv[n][:], buf[:, lead + j:lead + j + T], w(j), conv[n][:], ALU.mult,
              ALU.add)
        return V.last

    def qkv_chunks(dst, i, c0):
        V(dve.tensor_copy, tap_now[:], taps[:, bass.ds(i * 4, 4), :])
        taps_ready = V.last

        def done(c, h, ps, m):
            n = c % 2
            m = A(act.copy, pre[n][:, 3 + h * BANK:3 + (h + 1) * BANK], ps,
                  after=[m, *(pr.free.get(f"pre{n}", ()) if h == 0 else ())], chain=False)
            if h == HALVES - 1:
                V.wait(m)
                r = causal_conv(pre[n], n, lambda j: tap_now[:, c, j:j + 1], 4)
                pr.free[f"pre{n}"] = [r]
                pr.free[f"conv{n}"] = [A(act.activation, dst(c), conv[n][:], ACT.Silu, after=[r], chain=False)]
            return m
        project(w_in, c0, 512, done)

    with pr.repeat("qk", 2) as i:
        qkv_chunks(lambda c: mixed[:, bass.ds(i * 4 + c, 1), :].rearrange("p a b -> p (a b)"), i, i * 512)
    qkv_chunks(lambda c: v_feat[:, c, :], 2, O_V)
    pr.barrier()
    cv.close()
    dump("q", mixed[:, 0:4, :])
    dump("kv", mixed[:, 4:8, :])

    log_a = sb("log_a", [P, NT, 4], where=mx)
    beta = sb("beta", [P, NT, 4], where=mx)
    with ExitStack() as ph:
        w_ab = sb("w_ab", [P, KD, 8], where=ph)
        heads = sb("heads", [P, 2, 4], where=ph)
        ab = sb("ab", [P, NT, 8], where=ph)
        tmp = sb("ab_tmp", [P, NT, 4], where=ph)
        one = sb("one_col", [P, 1], where=ph)
        SP.wait(Mark(V.done, V.done.count, None), Mark(A.done, A.done.count, None))
        sig = loads("ab")
        sig.inc(nc.sync.dma_start(w_ab[:], rows_of(w_in, 0, D, O_A, 8)))
        sig.inc(nc.sync.dma_start(heads[:, 0, :], dram["dn_a_log"][0].partition_broadcast(P)))
        m_ab = sig.inc(nc.sync.dma_start(heads[:, 1, :], dram["dn_dt_bias"][0].partition_broadcast(P)))
        V(dve.memset, one[:], 1.0)
        PE.wait(m_ab)
        b, ps = bank()
        for n in range(NT):
            for k in range(KD):
                m = te.matmul(ps[:, n * 8:n * 8 + 8], ft[:, k, n * P:(n + 1) * P], w_ab[:, k, :],
                              start=(k == 0), stop=(k == KD - 1))
        m = PE.done.inc(m)
        emptied(b, V(dve.tensor_copy, ab[:], ps[:, 0:NT * 8].rearrange("p (n c) -> p n c", c=8), after=[m, m_ab]))
        A(act.activation, heads[:, 0, :], heads[:, 0, :], ACT.Exp, after=[m_ab])
        m = V(dve.tensor_tensor, tmp[:], ab[:, :, 0:4], spread(heads[:, 1, :], 1, NT), ALU.add)
        softplus(tmp, log_a, one, A, V, act, dve, m)
        V(dve.tensor_tensor, log_a[:], log_a[:], spread(heads[:, 0, :], 1, NT), ALU.mult, after=[A.last])
        V(dve.tensor_scalar, log_a[:], log_a[:], -1.0, None, ALU.mult)
        A(act.activation, beta[:], ab[:, :, 4:8], ACT.Sigmoid, after=[V.last])
        pr.barrier()
    dump("log_a", log_a[:])
    dump("beta", beta[:])

    SCALE_Q = DN_W // DN_HEADS
    dn = ExitStack()
    H4 = DN_HEADS

    def four(name):
        return sb(name, [P, H4, P], where=dn)

    def words(t):
        return t[:].rearrange("p a b -> p (a b)")

    masks = sb("masks", [P, 7, P], where=dn)
    strict = sb("strict", [P, P], where=dn)
    for lv in range(7):
        s = 1 << lv
        G(pool.memset, masks[:, lv, :], 0.0)
        view = masks[:, lv, :].rearrange("p (n h c) -> p n h c", h=2, c=s)[:, :, 1, :]
        ones_v = ones[:].rearrange("p (n h c) -> p n h c", h=2, c=s)[:, :, 1, :]
        G(pool.affine_select, out=view, in_=ones_v, compare_op=ALU.is_ge, fill=0.0, base=0,
          pattern=[[-2 * s, P // (2 * s)], [0, s]], channel_multiplier=1)
        G(pool.affine_select, out=view, in_=view, compare_op=ALU.is_ge, fill=0.0, base=s - 1,
          pattern=[[2 * s, P // (2 * s)], [0, s]], channel_multiplier=-1)
    G(pool.affine_select, out=strict[:], in_=ones[:], compare_op=ALU.is_gt, fill=0.0, base=0,
      pattern=[[1, P]], channel_multiplier=-1)
    la_t, be_t = sb("la_t", [P, H4], where=dn), sb("be_t", [P, H4], where=dn)
    g_row, b_row = four("g_row"), four("b_row")
    g_col = sb("g_col", [P, 4, H4], where=dn)
    decay = four("decay")
    qn, kn, qd, vt = four("qn"), four("kn"), four("qd"), four("vt")
    sq = four("sq")
    lt, ltm, at = four("lt"), four("ltm"), four("at")
    inv, inv_t, prod = four("inv"), four("inv_t"), four("prod")
    vtok, ktok, vnew, rhs = four("vtok"), four("ktok"), four("vnew"), four("rhs")
    state = four("state")
    la_b, be_b = lt, rhs
    V(dve.memset, state[:], 0.0)

    def per_head(ps, lhs, rhs_of, after, start=True, stop=True):
        PE.wait(*after)
        for h in range(H4):
            m = te.matmul(ps[:, h * P:(h + 1) * P], lhs(h), rhs_of(h), start=start, stop=stop)
        return PE.done.inc(m)

    ID4 = spread(ident[:], 1, H4)
    with pr.repeat("delta", NT) as i:
        tok = bass.ds(i * P, P)
        m_la = V(dve.tensor_copy, la_t[:], log_a[:, bass.ds(i, 1), :].rearrange("p a b -> p (a b)"), chain=False)
        V(dve.tensor_copy, be_t[:], beta[:, bass.ds(i, 1), :].rearrange("p a b -> p (a b)"), chain=False)
        V(dve.tensor_copy, la_b[:], spread(la_t[:], 2, P))
        m_b = V(dve.tensor_copy, be_b[:], spread(be_t[:], 2, P))
        b0, ps = bank()
        m = per_head(ps, lambda h: la_b[:, h, :], lambda h: upper[:], [m_b])
        m_g = A(act.copy, words(g_row), ps[:], after=[m])
        emptied(b0, m_g)
        b0, ps = bank()
        m = PE(te.matmul, ps[:, 0:H4], upper[:], la_t[:], start=True, stop=True)
        m = V(dve.tensor_copy, g_col[:, 0, :], ps[:, 0:H4], after=[m])
        emptied(b0, m)
        b0, ps = bank()
        m = per_head(ps, lambda h: be_b[:, h, :], lambda h: ident[:], [])
        m_br = V(dve.tensor_copy, words(b_row), ps[:], after=[m])
        emptied(b0, m_br)
        V(dve.tensor_tensor, decay[:], g_row[:], spread(g_col[:, 0, :], 2, P), ALU.subtract, after=[m_g])
        m = V(dve.tensor_scalar, decay[:], decay[:], 0.0, None, ALU.min)
        A(act.activation, decay[:], decay[:], ACT.Exp, after=[m])
        g_end = g_row[:, :, P - 1]
        m = V(dve.tensor_tensor, g_col[:, 2, :], g_end, g_col[:, 0, :], ALU.subtract)
        A(act.activation, g_col[:, 1, :], g_col[:, 0, :], ACT.Exp)
        A(act.activation, g_col[:, 2, :], g_col[:, 2, :], ACT.Exp, after=[m])
        m_e = A(act.activation, g_col[:, 3, :], g_end, ACT.Exp)
        m_er = A(act.activation, g_row[:], g_row[:], ACT.Exp)
        m_dec = V(dve.tensor_tensor, decay[:], decay[:], spread(upper[:], 1, H4), ALU.mult, after=[m_e])
        for src, dst, factor in ((mixed[:, 0:4, tok], qn, float(SCALE_Q)), (mixed[:, 4:8, tok], kn, 1.0)):
            m = G(pool.tensor_tensor, sq[:], src, src, ALU.mult, after=pr.free.get("sq", ()))
            b0, ps = bank()
            PE.wait(m)
            m = PE(te.matmul, ps[:], ones[:], words(sq), start=True, stop=True)
            A(act.activation, words(sq), ps[:], ACT.Ln, bias=eps_q[:] if factor != 1.0 else eps_col[:],
              scale=factor, after=[m])
            emptied(b0, A.last)
            m = A(act.activation, words(sq), words(sq), ACT.Exp, scale=-0.5)
            m_n = V(dve.tensor_tensor, dst[:], src, sq[:], ALU.mult, after=[m])
            pr.free["sq"] = [m_n]
        m_qd = V(dve.tensor_tensor, qd[:], qn[:], g_row[:], ALU.mult, after=[m_er])
        m_v = G(pool.tensor_copy, vt[:], v_feat[:, :, tok])
        b0, ps = bank()
        m = per_head(ps, lambda h: kn[:, h, :], lambda h: kn[:, h, :], [m_n])
        V(dve.tensor_tensor, words(lt), ps[:], words(decay), ALU.mult, after=[m])
        emptied(b0, V.last)
        b1_, ps = bank()
        m = per_head(ps, lambda h: kn[:, h, :], lambda h: qn[:, h, :], [])
        m_at = V(dve.tensor_tensor, words(at), ps[:], words(decay), ALU.mult, after=[m])
        emptied(b1_, m_at)
        V(dve.tensor_tensor, lt[:], lt[:], b_row[:], ALU.mult)
        m_lt = V(dve.tensor_tensor, lt[:], lt[:], spread(strict[:], 1, H4), ALU.mult)
        for src, dst, w in ((kn, ktok, m_n), (vt, vtok, m_v)):
            b0, ps = bank()
            PE.wait(w)
            for h in range(H4):
                m = te.transpose(ps[:, h * P:(h + 1) * P], src[:, h, :], ident[:])
            m = PE.done.inc(m)
            emptied(b0, A(act.copy, words(dst), ps[:], after=[m]))
        m_tok = A.last
        m = V(dve.tensor_tensor, ltm[:], lt[:], spread(masks[:, 0, :], 1, H4), ALU.mult)
        b0, ps = bank()
        PE.wait(m)
        for h in range(H4):
            mm = te.transpose(ps[:, h * P:(h + 1) * P], ltm[:, h, :], ident[:])
        mm = PE.done.inc(mm)
        m_xt = V(dve.tensor_tensor, inv_t[:], ID4, ltm[:], ALU.subtract)
        m_x = V(dve.tensor_tensor, inv[:], ID4, ps[:].rearrange("p (h c) -> p h c", h=H4), ALU.subtract, after=[mm])
        emptied(b0, m_x)
        for lv in range(1, 7):
            m = G(pool.tensor_tensor, ltm[:], lt[:], spread(masks[:, lv, :], 1, H4), ALU.mult,
                  after=[m_lt, mm, m_xt])
            b0, ps = bank()
            mm = per_head(ps, lambda h: ltm[:, h, :], lambda h: inv[:, h, :], [m, m_x])
            m = A(act.copy, words(prod), ps[:], after=[mm])
            emptied(b0, m)
            b1_, ps1 = bank()
            m1 = per_head(ps1, lambda h: prod[:, h, :], lambda h: inv_t[:, h, :], [m, m_xt])
            m0 = m1
            if lv < 6:
                b2_, ps2 = bank()
                m0 = per_head(ps2, lambda h: inv_t[:, h, :], lambda h: prod[:, h, :], [])
            m_xt = V(dve.tensor_tensor, words(inv_t), words(inv_t), ps1[:], ALU.subtract, after=[m0])
            emptied(b1_, m_xt)
            if lv < 6:
                m_x = V(dve.tensor_tensor, words(inv), words(inv), ps2[:], ALU.subtract, after=[m0])
                emptied(b2_, m_x)
            A.wait(m0)
        b0, ps = bank()
        m = per_head(ps, lambda h: kn[:, h, :], lambda h: state[:, h, :], pr.free.get("state", ()))
        V(dve.tensor_tensor, rhs[:], ps[:].rearrange("p (h c) -> p h c", h=H4), spread(g_col[:, 1, :], 2, P),
          ALU.mult, after=[m])
        emptied(b0, V.last)
        V(dve.tensor_tensor, rhs[:], vtok[:], rhs[:], ALU.subtract, after=[m_tok])
        m = V(dve.tensor_tensor, rhs[:], rhs[:], spread(be_t[:], 2, P), ALU.mult)
        b0, ps = bank()
        m = per_head(ps, lambda h: inv_t[:, h, :], lambda h: rhs[:, h, :], [m, m_xt])
        m_vn = A(act.copy, words(vnew), ps[:], after=[m])
        emptied(b0, m_vn)
        b0, ps = bank()
        PE.wait(m_qd, m_vn, m_at)
        for h in range(H4):
            te.matmul(ps[:, h * P:(h + 1) * P], state[:, h, :], qd[:, h, :], start=True, stop=False)
            m = te.matmul(ps[:, h * P:(h + 1) * P], vnew[:, h, :], at[:, h, :], start=False, stop=True)
        m_o = PE.done.inc(m)
        m = V(dve.tensor_tensor, ktok[:], ktok[:], spread(g_col[:, 2, :], 2, P), ALU.mult)
        b1_, ps1 = bank()
        m = per_head(ps1, lambda h: ktok[:, h, :], lambda h: vnew[:, h, :], [m])
        V(dve.tensor_tensor, state[:], state[:], spread(g_col[:, 3, :], 2, P), ALU.mult, after=[m_o])
        V(dve.tensor_tensor, words(state), words(state), ps1[:], ALU.add, after=[m])
        emptied(b1_, V.last)
        pr.free["state"] = [V.last]
        emptied(b0, rms_heads(ps, m_o, sq, mixed[:, 0:4, tok], col("dn_norm_g")))
    dn.close()
    dump("o_dn", mixed[:, 0:4, :])
    mx.close()

    gl = ExitStack()
    g_qk = sb("g_qk", [P, 4, T], where=gl)
    k_dec = sb("k_dec", [P, 2, T], where=gl)
    g_v = sb("g_v", [P, NT, GLA_W], where=gl)
    g_last = sb("g_last", [P, 2, NGC], where=gl)

    def gqk_done(c, h, ps, m):
        return A(act.mul, g_qk[:, c, h * BANK:(h + 1) * BANK], ps, GLA_K ** -0.5 if c < 2 else 1.0, after=[m],
                 chain=False)
    project(w_in, O_GQ, 512, gqk_done)
    halves = [load_panel(rows_of(w_in, 4 * P * n, 4 * P, O_GV, GLA_W)) for n in range(2)]
    PE.wait(*[m for _, _, m in halves])
    for n in range(NT):
        b, ps = bank()
        for k in range(KD):
            m = te.matmul(ps[:], ft[:, k, n * P:(n + 1) * P], halves[k // 4][1][:, k % 4, :], start=(k == 0),
                          stop=(k == KD - 1))
        m = PE.done.inc(m)
        emptied(b, V(dve.tensor_copy, g_v[:, n, :], ps[:], after=[m], chain=False))
    for s, _, _ in halves:
        used(s, m)

    with ExitStack() as ph:
        w_r = sb("w_r", [P, KD, RANK], where=ph)
        w_g2 = sb("w_g2", [RANK, 2 * P], where=ph)
        r_feat = sb("r_feat", [RANK, T], where=ph)
        cum = sb("cum", [P, 2, T], where=ph)
        tmp = sb("cum_tmp", [P, 2, T], where=ph)
        keep = sb("keep", [P, T], where=ph)
        one = sb("one_col2", [P, 1], where=ph)
        SP.wait(Mark(V.done, V.done.count, None), Mark(A.done, A.done.count, None))
        sig = loads("gate")
        sig.inc(nc.sync.dma_start(w_r[:], rows_of(w_in, 0, D, O_GR, RANK)))
        m_r = sig.inc(nc.sync.dma_start(w_g2[:], dram["gla_w_gate2"][0]))
        V(dve.memset, one[:], 1.0)
        V(dve.memset, keep[:], 1.0)
        m_keep = V(dve.memset, keep[:].rearrange("p (n c) -> p n c", c=GC)[:, :, 0:1], 0.0)
        PE.wait(m_r)
        for h in range(HALVES):
            b, ps = bank()
            for k in range(KD):
                m = te.matmul(ps[0:RANK, :], w_r[:, k, :], ft[:, k, h * BANK:(h + 1) * BANK], start=(k == 0),
                              stop=(k == KD - 1))
            m = PE.done.inc(m)
            emptied(b, A(act.copy, r_feat[:, h * BANK:(h + 1) * BANK], ps[0:RANK, :], after=[m]))
        for c in range(2):
            for h in range(HALVES):
                b, ps = bank()
                m = PE(te.matmul, ps[:], w_g2[:, c * P:(c + 1) * P], r_feat[:, h * BANK:(h + 1) * BANK],
                       start=True, stop=True, after=[A.last])
                emptied(b, V(dve.tensor_scalar, tmp[:, c, h * BANK:(h + 1) * BANK], ps[:],
                             col("gla_b_gate", c), -1.0, ALU.add, ALU.mult, after=[m]))
        softplus(tmp, cum, one, A, V, act, dve, V.last)
        for c in range(2):
            V(dve.tensor_tensor_scan, tmp[:, c, :], keep[:], cum[:, c, :], 0.0, ALU.mult, ALU.add)
        b_sum = tmp
        ends = b_sum[:].rearrange("p c (n t) -> p c n t", t=GC)[:, :, :, GC - 1]
        m = V(dve.tensor_tensor, k_dec[:].rearrange("p c (n t) -> p c n t", t=GC),
              b_sum[:].rearrange("p c (n t) -> p c n t", t=GC), spread(ends, 3, GC), ALU.subtract)
        A(act.activation, k_dec[:], k_dec[:], ACT.Exp, scale=1.0 / TAU, after=[m])
        A(act.activation, g_last[:], ends, ACT.Exp, scale=-1.0 / TAU)
        m = A(act.activation, cum[:], b_sum[:], ACT.Exp, scale=-1.0 / TAU)
        V(dve.tensor_tensor, g_qk[:, 0:2, :], g_qk[:, 0:2, :], cum[:], ALU.mult, after=[m])
        V(dve.tensor_tensor, k_dec[:], k_dec[:], g_qk[:, 2:4, :], ALU.mult)
        m = A(act.activation, cum[:], b_sum[:], ACT.Exp, scale=1.0 / TAU, after=[V.last])
        V(dve.tensor_tensor, g_qk[:, 2:4, :], g_qk[:, 2:4, :], cum[:], ALU.mult, after=[m])
        pr.barrier()

    def gls(name, shape):
        return sb(name, shape, where=gl)
    k_inv = gls("k_inv", [P, 4, P])
    kd_t = gls("kd_t", [P, 2, P])
    kd_tok = gls("kd_tok", [P, 2, 2, P])
    v_t = gls("v_t", [P, GLA_W])
    at_g = gls("at_g", [P, 4, P])
    sq_g = gls("sq_g", [P, 4, P])
    st_g = gls("st_g", [P, 4, P])
    gl_t = gls("gl_t", [P, 2, 2])
    chunk_mask = gls("chunk_mask", [P, P])
    G(pool.tensor_copy, chunk_mask[:], upper[:])
    G(pool.memset, chunk_mask[0:GC, GC:P], 0.0)
    for t in (k_inv, kd_tok, st_g):
        G(pool.memset, t[:], 0.0)
    pr.free.pop("sq", None)
    with pr.repeat("gla", NT) as i:
        tok = bass.ds(i * P, P)
        m_k = None
        for hb in range(2):
            rows = slice(hb * GLA_K, (hb + 1) * GLA_K)
            m_k = G(pool.tensor_copy, k_inv[rows].rearrange("p (a b) t -> p a b t", b=2)[:, :, hb, :],
                    g_qk[rows, 2:4, tok], after=pr.free.get("k_inv", ()))
        m_kd = G(pool.tensor_copy, kd_t[:], k_dec[:, :, tok], after=pr.free.get("kd_t", ()))
        m_v = A(act.copy, v_t[:], g_v[:, bass.ds(i, 1), :].rearrange("p a b -> p (a b)"),
                after=pr.free.get("v_t", ()))
        m_gl = V(dve.tensor_copy, gl_t[:], g_last[:, :, bass.ds(i * 2, 2)])
        b0, ps = bank()
        PE.wait(m_k)
        for h in range(GLA_HEADS):
            m = te.matmul(ps[:, h * P:(h + 1) * P], k_inv[:, h, :], g_qk[:, h // 2, tok], start=True, stop=True)
        m = PE.done.inc(m)
        pr.free["k_inv"] = [m]
        m_at = V(dve.tensor_tensor, at_g[:], ps[:].rearrange("p (h c) -> p h c", h=4), spread(chunk_mask[:], 1, 4),
                 ALU.mult, after=[m, *pr.free.get("at_g", ())])
        emptied(b0, m_at)
        b0, ps = bank()
        PE.wait(m_kd)
        for p in range(2):
            m = te.transpose(ps[:, p * P:(p + 1) * P], kd_t[:, p, :], ident[:])
        m = PE.done.inc(m)
        pr.free["kd_t"] = [m]
        for c in range(2):
            rows = slice(c * GC, (c + 1) * GC)
            m_kt = A(act.copy, kd_tok[rows, c, :, :], ps[rows, 0:2 * P].rearrange("p (a b) -> p a b", a=2),
                     after=[m, *pr.free.get("kd_tok", ())])
        emptied(b0, m_kt)
        b0, ps = bank()
        PE.wait(m_at, m_v)
        for h in range(GLA_HEADS):
            te.matmul(ps[:, h * P:(h + 1) * P], v_t[:, h * P:(h + 1) * P], at_g[:, h, :], start=(h == 0), stop=False)
        for c in range(2):
            PE.wait(*pr.free.get("st_g", ()))
            for h in range(GLA_HEADS):
                m = te.matmul(ps[:, h * P + c * GC:h * P + (c + 1) * GC], st_g[:, h, :],
                              g_qk[:, h // 2, bass.ds(i * P + c * GC, GC)], start=False, stop=(h == 3 and c == 1))
            m_o = PE.done.inc(m)
            b1_, ps1 = bank()
            PE.wait(m_kt)
            for p in range(2):
                m = te.matmul(ps1[:, p * 2 * P:(p + 1) * 2 * P], kd_tok[:, c, p, :], v_t[:, p * 2 * P:(p + 1) * 2 * P],
                              start=True, stop=True)
            m = PE.done.inc(m)
            for h in range(GLA_HEADS):
                rows = slice((h % 2) * GLA_K, (h % 2 + 1) * GLA_K)
                V(dve.scalar_tensor_tensor, st_g[rows, h, :], st_g[rows, h, :], gl_t[rows, h // 2, c:c + 1],
                  ps1[rows, h * P:(h + 1) * P], ALU.mult, ALU.add, after=[m, m_o, m_gl], chain=True)
            emptied(b1_, V.last)
            pr.free["st_g"] = [V.last]
        pr.free["kd_tok"] = pr.free["v_t"] = [m]
        pr.free["at_g"] = [m_o]
        emptied(b0, rms_heads(ps, m_o, sq_g, mixed[:, 4:8, tok], col("gla_norm_g")))
    gl.close()
    dump("o_gla", mixed[:, 4:8, :])

    with ExitStack() as ph:
        gate = [sb(f"gate{n}", [P, BANK], where=ph) for n in range(2)]
        with pr.repeat("gates", 2) as i:
            def gate_done(c, h, ps, m):
                n = h % 2
                m = A(act.activation, gate[n][:], ps, ACT.Silu, after=[m, *pr.free.get(f"gate{n}", ())], chain=False)
                o = mixed[:, bass.ds(i * 4 + c, 1), h * BANK:(h + 1) * BANK].rearrange("p a b -> p (a b)")
                pr.free[f"gate{n}"] = [V(dve.tensor_tensor, o, o, gate[n][:], ALU.mult, after=[m], chain=False)]
                return m
            project(w_in, i * (O_GG - O_Z) + O_Z, 512, gate_done)
        dump("o_mix", mixed[:])

        def residual(h, n, ps, m):
            g = gate[n % 2]
            r = resid[:, n, h * BANK:(h + 1) * BANK]
            e = V(dve.tensor_tensor, g[:], ps[:], gate_row[:, 0, h * BANK:(h + 1) * BANK], ALU.mult, after=[m])
            V(dve.scalar_tensor_tensor, r, r, ALPHA, g[:], ALU.mult, ALU.add)
            return e
        project_tokens(lambda k, n: mixed[:, k, n * P:(n + 1) * P], 8, dram["w_o"][0], 0, residual)
        pr.barrier()
    mixed_space.close()

    with norm_space():
        m_rows = load_norm_rows("ln1_g", "ln1_b")
        V.wait(m_rows)
        with pr.repeat("norm1", NT) as i:
            x = resid[:, bass.ds(i, 1), :].rearrange("p a b -> p (a b)")
            m = layer_norm_tile(x, norm_rows[:, 0, :], norm_rows[:, 1, :])
            to_features(xhat, ft, i * P, P, lambda k: in_scale[:, 1, k:k + 1], lambda k: in_bias[:, 1, k:k + 1], [m])
    dump("x1", resid[:])
    dump("h1", ft[:])

    with ExitStack() as ph:
        y_acc = sb("y_acc", [P, NT, D], where=ph)
        pre = [sb(f"ffn_in{n}", [P, 3 + T], where=ph) for n in range(2)]
        conv = [sb(f"ffn_conv{n}", [P, T], where=ph) for n in range(2)]
        hid = [sb(f"ffn_hid{n}", [P, T], where=ph) for n in range(2)]
        taps = sb("ffn_taps", [P, 2, NFF, 4], where=ph)
        tap_now = sb("ffn_tap_now", [P, 2, 2, 4], where=ph)
        V(dve.tensor_copy, taps[:, :, :, 0:3],
          col("ffn_conv", 0, 3 * 2 * NFF).rearrange("p (j g c) -> p g c j", j=3, g=2))
        V(dve.tensor_copy, taps[:, :, :, 3:4],
          col("ffn_conv_b", 0, 2 * NFF).rearrange("p (g c j) -> p g c j", g=2, j=1))
        for n in range(2):
            V(dve.memset, pre[n][:, 0:3], 0.0)
        G(pool.memset, y_acc[:], 0.0)
        w_up, w_down = dram["ffn_w_up"][0], dram["ffn_w_down"][0]

        def project_down(n_units, hidden, w, row_of, acc):
            for u in range(n_units):
                s, wt, m = load_panel(rows_of(w, row_of(u), P, 0, D))
                PE.wait(m, *hidden[u][1])
                for n in range(NT):
                    for h in range(2):
                        b, ps = bank()
                        m = PE(te.matmul, ps[:], hidden[u][0][:, n * P:(n + 1) * P],
                               wt[:, 0, h * BANK:(h + 1) * BANK], start=True, stop=True)
                        o = acc[:, n, h * BANK:(h + 1) * BANK]
                        emptied(b, V(dve.tensor_tensor, o, o, ps[:], ALU.add, after=[m], chain=False))
                used(s, m)
                pr.free[f"hid{u}"] = [m]

        with pr.repeat("ffn", NFF // 2) as i:
            m_taps = V(dve.tensor_copy, tap_now[:], taps[:, :, bass.ds(i * 2, 2), :])
            hidden = []
            for u in range(2):
                s, wt, m = load_panel(*[rows_of(w_up, 0, D, (i * 2 + u) * P + g * FF, P) for g in range(2)])
                PE.wait(m)
                for g in range(2):
                    for h in range(HALVES):
                        b, ps = bank()
                        for k in range(KD):
                            mm = te.matmul(ps[:], wt[:, k, g * P:(g + 1) * P], ft[:, k, h * BANK:(h + 1) * BANK],
                                           start=(k == 0), stop=(k == KD - 1))
                        mm = PE.done.inc(mm)
                        m = A(act.copy, pre[g][:, 3 + h * BANK:3 + (h + 1) * BANK], ps[:],
                              after=[mm, *(pr.free.get(f"pre{g}", ()) if h == 0 else ())], chain=False)
                        emptied(b, m)
                    V.wait(m, *pr.free.get(f"fconv{g}", ()))
                    r = causal_conv(pre[g], g, lambda j: tap_now[:, g, u, j:j + 1], 3, tap_now[:, g, u, 3:4], conv)
                    pr.free[f"pre{g}"] = [r]
                used(s, mm)
                m0 = A(act.activation, hid[u][:], conv[0][:], ACT.Silu, after=[r, *pr.free.get(f"hid{u}", ())],
                       chain=False)
                m1 = G(pool.tensor_tensor, hid[u][:], hid[u][:], conv[1][:], ALU.mult, after=[m0])
                pr.free["fconv0"], pr.free["fconv1"] = [m0], [m1]
                hidden.append((hid[u], [m1]))
            project_down(2, hidden, w_down, lambda u: (i * 2 + u) * P, y_acc)
        dump("ffn", y_acc[:])
        with pr.repeat("ffn_out", NT) as i:
            x = resid[:, bass.ds(i, 1), :].rearrange("p a b -> p (a b)")
            y = y_acc[:, bass.ds(i, 1), :].rearrange("p a b -> p (a b)")
            V(dve.tensor_tensor, y, y, gate_row[:, 1, :], ALU.mult)
            V(dve.scalar_tensor_tensor, x, x, ALPHA, y, ALU.mult, ALU.add)

    with norm_space():
        m_rows = load_norm_rows("ln2_g", "ln2_b")
        V.wait(m_rows)
        with pr.repeat("norm2", NT) as i:
            x = resid[:, bass.ds(i, 1), :].rearrange("p a b -> p (a b)")
            layer_norm_tile(x, norm_rows[:, 0, :], norm_rows[:, 1, :])
            m = rms_norm_tile(x, xhat[:], after=[V.last])
            to_features(xhat, ft, i * P, P, lambda k: col("norm_mix_g", k), None, [m])
    dump("x2", resid[:])
    dump("xn", ft[:])


    w_in2 = dram["w_in_2"][0]
    O2_U = 3 * HEADS * HD
    mix2 = sb("mix2", [P, 8, T])

    with ExitStack() as ph:
        def rg(name, shape):
            return sb(name, shape, where=ph)
        gates_w = rg("gates_w", [P, 4, 4, P])
        gw_now = rg("gw_now", [P, 4, P])
        params = rg("params", [P, 4, 11])
        par = rg("par", [P, 11])
        npar = rg("npar", [P, 2])
        one = rg("one_col", [P, 1])
        lam = rg("lam", [P, 8])
        lam_sp = rg("lam_sp", [P, 8])
        pre = rg("u_in", [P, 3 + T])
        uc = rg("uc", [P, T])
        ra, ri, th, a_, h_f = (rg(n, [P, T]) for n in ("gate_a", "gate_x", "th", "a_coef", "h_fwd"))
        m = G(pool.memset, gates_w[:], 0.0)
        SP.wait(m)
        sig = loads("gates_w")
        for ty, w in enumerate((dram["rg_a_w_2"][0], dram["rg_x_w_2"][0])):
            for z in range(2):
                for g in range(2):
                    m_gw = sig.inc(nc.sync.dma_start(
                        gates_w[g * 64:(g + 1) * 64, :, ty * 2 + z, g * 64:(g + 1) * 64],
                        w[z].rearrange("(c g) i j -> g i c j", g=2)[g]))
        V(dve.memset, one[:], 1.0)
        V(dve.tensor_copy, params[:, :, 0:4], col("conv_w", 0, 16).rearrange("p (j c) -> p c j", c=4))
        V(dve.tensor_copy, params[:, :, 4:5], col("conv_b", 0, 4).rearrange("p (j c) -> p c j", c=4))
        V(dve.tensor_copy, params[:, :, 5:7], col("rg_a_b", 0, 8).rearrange("p (j c) -> p c j", c=4))
        V(dve.tensor_copy, params[:, :, 7:9], col("rg_x_b", 0, 8).rearrange("p (j c) -> p c j", c=4))
        V(dve.tensor_scalar, lam[:], col("rg_lambda", 0, 8), -1.0, None, ALU.mult)
        softplus(lam, lam_sp, one, A, V, act, dve, V.last)
        V(dve.tensor_scalar, params[:, :, 9:11], lam_sp[:].rearrange("p (j c) -> p c j", c=4), -8.0, None, ALU.mult)
        V(dve.memset, pre[:, 0:2], 0.0)
        V(dve.memset, pre[:, 2 + T:3 + T], 0.0)
        G.wait(m_gw)
        with pr.repeat("rglru", 4) as i:
            m_par = V(dve.tensor_copy, par[:], params[:, bass.ds(i, 1), :].rearrange("p a b -> p (a b)"))
            V(dve.tensor_scalar, npar[:], par[:, 9:11], -1.0, None, ALU.mult)
            m_par = V.last
            m_gwn = G(pool.tensor_copy, gw_now[:], gates_w[:, bass.ds(i, 1), :, :].rearrange("p a b c -> p (a b) c"),
                      after=pr.free.get("gw_now", ()))
            s, wt, m = load_panel(*[rows_of(w_in2, 0, D, i * P + (O2_U + g * 512), P) for g in range(2)])
            PE.wait(m)
            y = mix2[:, bass.ds(i + 4, 1), :].rearrange("p a b -> p (a b)")
            for g in range(2):
                for h in range(HALVES):
                    hs = slice(h * BANK, (h + 1) * BANK)
                    b, ps = bank()
                    for k in range(KD):
                        mm = te.matmul(ps[:], wt[:, k, g * P:(g + 1) * P], ft[:, k, hs], start=(k == 0),
                                       stop=(k == KD - 1))
                    mm = PE.done.inc(mm)
                    if g == 0:
                        m = A(act.copy, pre[:, 2 + h * BANK:2 + (h + 1) * BANK], ps[:],
                              after=[mm, *(pr.free.get("u_in", ()) if h == 0 else ())])
                    else:
                        m = A(act.activation, mix2[:, bass.ds(i + 4, 1), hs].rearrange("p a b -> p (a b)"), ps[:],
                              ACT.Gelu_apprx_tanh, after=[mm])
                    emptied(b, m)
                if g == 0:
                    V.wait(m)
                    m_uc = causal_conv(pre, 0, lambda j: par[:, j:j + 1], 4, par[:, 4:5], [uc])
                    pr.free["u_in"] = [m_uc]
            used(s, mm)
            m_y = m
            PE.wait(m_gwn, m_uc)
            for z in range(2):
                for ty, dst in ((0, ra), (1, ri)):
                    for h in range(HALVES):
                        hs = slice(h * BANK, (h + 1) * BANK)
                        b, ps = bank()
                        mm = PE(te.matmul, ps[:], gw_now[:, ty * 2 + z, :], uc[:, hs], start=True, stop=True)
                        m = A(act.activation, dst[:, hs], ps[:], ACT.Sigmoid,
                              bias=par[:, 5 + ty * 2 + z:6 + ty * 2 + z],
                              after=[mm, m_par, *pr.free.get(f"rg{ty}", ())])
                        emptied(b, m)
                m_i = m
                m_t = A(act.activation, th[:], ra[:], ACT.Tanh, scale=npar[:, z:z + 1], after=pr.free.get("th", ()))
                m_a = A(act.activation, a_[:], ra[:], ACT.Exp, scale=par[:, 9 + z:10 + z])
                V(dve.tensor_tensor, ri[:], ri[:], uc[:], ALU.mult, after=[m_i])
                V(dve.tensor_scalar, ra[:], th[:], 1.0, None, ALU.add, after=[m_a])
                V(dve.reciprocal, ra[:], ra[:])
                m = V(dve.scalar_tensor_tensor, th[:], th[:], 2.0, ra[:], ALU.mult, ALU.mult)
                pr.free["rg0"] = [m]
                m = A(act.activation, th[:], th[:], ACT.Sqrt, after=[m])
                V(dve.tensor_tensor, th[:], th[:], ri[:], ALU.mult, after=[m])
                pr.free["rg1"] = [V.last]
                if z == 0:
                    V(dve.tensor_tensor_scan, h_f[:], a_[:], th[:], 0.0, ALU.mult, ALU.add)
                else:
                    V(dve.tensor_tensor_scan, ri[:, ::-1], a_[:, ::-1], th[:, ::-1], 0.0, ALU.mult, ALU.add)
                pr.free["th"] = [V.last]
            V(dve.tensor_tensor, h_f[:], h_f[:], ri[:], ALU.add)
            V(dve.tensor_tensor, y, y, h_f[:], ALU.mult, after=[m_y])
            pr.free["rg1"] = [V.last]
            pr.free["gw_now"] = [mm]
    dump("rec", mix2[:, 4:8, :])

    at_space = ExitStack()
    k_feat = sb("k_feat", [P, 4, T], where=at_space)
    v_tok = sb("v_tok", [P, NT, 512], where=at_space)
    with ExitStack() as ph:
        inv_freq = sb("inv_freq", [P, 1], where=ph)
        pos_i = sb("pos_i", [P, T], I32, where=ph)
        ang, cos, sin, turns = (sb(n, [P, T], where=ph) for n in ("ang", "cos", "sin", "turns"))
        t_cos = [sb(f"t_cos{n}", [P, BANK], where=ph) for n in range(2)]
        t_sin = [sb(f"t_sin{n}", [P, BANK], where=ph) for n in range(2)]
        turns_i = pos_i
        SP.wait(Mark(V.done, V.done.count, None), Mark(A.done, A.done.count, None), Mark(PE.done, PE.done.count, None))
        sig = loads("positions")
        sig.inc(nc.sync.dma_start(inv_freq[:], dram["inv_freq"]))
        m = sig.inc(nc.sync.dma_start(pos_i[:], dram["positions_2"][0].partition_broadcast(P)))
        V(dve.tensor_copy, ang[:], pos_i[:], after=[m])
        V(dve.tensor_scalar, ang[:], ang[:], inv_freq[:], None, ALU.mult)
        C1 = 6.28125
        C2 = float.fromhex("0x1.fb4p-10")
        C3 = 2 * math.pi - C1 - C2
        for out, quarter in ((sin, 0.0), (cos, 0.25)):
            V(dve.tensor_scalar, turns[:], ang[:], 1.0 / (2 * math.pi), quarter, ALU.mult, ALU.add)
            V(dve.tensor_copy, turns_i[:], turns[:])
            V(dve.tensor_copy, turns[:], turns_i[:])
            V(dve.scalar_tensor_tensor, out[:], turns[:], -C1, ang[:], ALU.mult, ALU.add)
            V(dve.scalar_tensor_tensor, out[:], turns[:], -C2, out[:], ALU.mult, ALU.add)
            V(dve.scalar_tensor_tensor, out[:], turns[:], -C3, out[:], ALU.mult, ALU.add)
            V(dve.tensor_scalar, out[:], out[:], quarter * 2 * math.pi, math.pi, ALU.add, ALU.min)
            m = V(dve.tensor_scalar, out[:], out[:], -math.pi, None, ALU.max)
            A(act.activation, out[:], out[:], ACT.Sin, after=[m])
        for q in (0, 2):
            V(dve.tensor_scalar, sin[32 * q:32 * q + 32, :], sin[32 * q:32 * q + 32, :], -1.0, None, ALU.mult,
              after=[A.last])
        V.wait(A.last, V.last)

        def rope_into(dst):
            def done(c, h, ps, m):
                n = h % 2
                hs = slice(h * BANK, (h + 1) * BANK)
                V(dve.tensor_tensor, t_cos[n][:], ps, cos[:, hs], ALU.mult, after=[m, *pr.free.get(f"rope{n}", ())],
                  chain=False)
                for q in range(4):
                    o, i_ = 32 * q, 32 * (q ^ 1)
                    e = V(dve.tensor_tensor, t_sin[n][o:o + 32, :], ps[i_:i_ + 32, :], sin[o:o + 32, hs], ALU.mult,
                          chain=False)
                pr.free[f"rope{n}"] = [G(pool.tensor_tensor, dst[:, c, hs], t_cos[n][:], t_sin[n][:], ALU.add,
                                         after=[e])]
                return e
            return done
        project(w_in2, 0, 512, rope_into(mix2))
        project(w_in2, 512, 512, rope_into(k_feat))
        pr.barrier()
    halves = [load_panel(rows_of(w_in2, 4 * P * n, 4 * P, 1024, 512)) for n in range(2)]
    PE.wait(*[m for _, _, m in halves])
    for n in range(NT):
        b, ps = bank()
        for k in range(KD):
            m = te.matmul(ps[:], ft[:, k, n * P:(n + 1) * P], halves[k // 4][1][:, k % 4, :], start=(k == 0),
                          stop=(k == KD - 1))
        m = PE.done.inc(m)
        emptied(b, V(dve.tensor_copy, v_tok[:, n, :], ps[:], after=[m], chain=False))
    for s, _, _ in halves:
        used(s, m)
    dump("rq", mix2[:, 0:4, :])
    dump("rk", k_feat[:])
    pr.barrier()

    SPAN = 2 * T - P
    ln_count = sb("ln_count", [P, SPAN], where=at_space)
    with ExitStack() as ph:
        dist, rem, d2, in4 = (ft[:].rearrange("p a b -> p (a b)")[:, n * SPAN:(n + 1) * SPAN] for n in range(4))
        dist, rem = dist.bitcast(I32), rem.bitcast(I32)
        in16 = ln_count
        G(pool.iota, dist, pattern=[[1, SPAN]], base=-(T - P), channel_multiplier=-1)
        V(dve.tensor_copy, d2, dist, after=[G.last])
        V(dve.tensor_tensor, d2, d2, d2, ALU.mult)
        for mask, dil in ((in4, 4), (in16[:], 16)):
            V(dve.tensor_scalar, rem, dist, dil - 1, None, ALU.bitwise_and)
            V(dve.tensor_copy, mask, rem)
            V(dve.tensor_scalar, mask, mask, 0.0, None, ALU.is_equal)
            V(dve.scalar_tensor_tensor, mask, d2, float((RADIUS * dil) ** 2), mask, ALU.is_le, ALU.mult)
        V(dve.scalar_tensor_tensor, in4, d2, float(RADIUS ** 2), in4, ALU.is_le, ALU.add)
        V(dve.tensor_tensor, in4, in4, in16[:], ALU.add)
        m = V(dve.tensor_scalar, in16[:], in4, 1.0, None, ALU.max)
        A(act.activation, in16[:], in16[:], ACT.Ln, after=[m])
        V(dve.tensor_scalar, in4, in4, 1.0, -1.0, ALU.min, ALU.add)
        V(dve.scalar_tensor_tensor, ln_count[:], in4, 1e30, in16[:], ALU.mult, ALU.add, after=[A.last])
        pr.barrier()

    q_pad = sb("q_pad", [P, 2, T], where=at_space)
    v_pad = sb("v_pad", [P, NT, 2, P], where=at_space)
    scores = [sb(f"scores{n}", [P, T], where=at_space) for n in range(2)]
    row_stat = sb("row_stat", [P, 2, 4], where=at_space)
    p_t = ft[:].rearrange("p a (b c) -> p a b c", b=2)
    G(pool.memset, q_pad[:], 0.0)
    G(pool.memset, v_pad[:], 0.0)

    def softmax_rows(s, n_keys, st, after):
        V(dve.tensor_reduce, st[:, 0:1], s[:, 0:n_keys], AX, ALU.max, after=after)
        m = V(dve.tensor_scalar, st[:, 1:2], st[:, 0:1], -1.0, None, ALU.mult)
        m = A(act.activation, s[:, 0:n_keys], s[:, 0:n_keys], ACT.Exp, bias=st[:, 1:2], accum_out=st[:, 2:3],
              after=[m])
        V(dve.reciprocal, st[:, 3:4], st[:, 2:3], after=[m])
        return V(dve.tensor_scalar, s[:, 0:n_keys], s[:, 0:n_keys], st[:, 3:4], None, ALU.mult)

    with pr.repeat("dilated", HEADS // 2) as i:
        for hb in range(2):
            rows = slice(hb * HD, (hb + 1) * HD)
            G(pool.tensor_copy, q_pad[rows, hb, :], mix2[rows, bass.ds(i, 1), :].rearrange("p a b -> p (a b)"),
              after=pr.free.get("q_pad", ()))
            m_pad = G(pool.tensor_copy, v_pad[:, :, hb, hb * HD:(hb + 1) * HD],
                      v_tok[:, :, bass.ds(i * P + hb * HD, HD)], after=pr.free.get("v_pad", ()))
        ready, transposed = {}, {}

        def score(u):
            half, tile, hb = u // 8, u % 8 // 2, u % 2
            n = half * 4 + tile
            st, s = row_stat[:, u % 2, :], scores[u % 2]
            for h in range(2):
                b, ps = bank()
                m = PE(te.matmul, ps[:], q_pad[:, hb, n * P:(n + 1) * P],
                       k_feat[:, bass.ds(i, 1), h * BANK:(h + 1) * BANK].rearrange("p a b -> p (a b)"),
                       start=True, stop=True, after=[m_pad])
                x0 = T - P - n * P + h * BANK
                e = V(dve.scalar_tensor_tensor, s[:, h * BANK:(h + 1) * BANK], ps[:], HD ** -0.5,
                      ln_count[:, x0:x0 + BANK], ALU.mult, ALU.add,
                      after=[m, *pr.free.get(f"scores{u % 2}", ())], chain=False)
                emptied(b, e)
            pr.free["q_pad"] = [m]
            ready[u] = softmax_rows(s, T, st, [e])

        def turn_weights(u):
            half, tile, hb = u // 8, u % 8 // 2, u % 2
            s = scores[u % 2]
            PE.wait(ready[u])
            for h in range(2):
                b, ps = bank()
                for k in range(4):
                    m = te.transpose(ps[:, k * P:(k + 1) * P], s[:, (4 * h + k) * P:(4 * h + k + 1) * P], ident[:])
                m = PE.done.inc(m)
                o = p_t[:, 4 * h:4 * h + 4, hb, tile * P:(tile + 1) * P]
                src = ps[:].rearrange("p (a b) -> p a b", a=4)
                if h == 0:
                    e0 = A(act.copy, o, src, after=[m, *pr.free.get("p_t", ())], chain=False)
                    emptied(b, e0)
                else:
                    e1 = V(dve.tensor_copy, o, src, after=[m, *pr.free.get("p_t", ())], chain=False)
                    emptied(b, e1)
            pr.free[f"scores{u % 2}"] = [m]
            transposed[u] = [e0, e1]

        def weigh(half):
            b, ps = bank()
            PE.wait(*[m for u in range(half * 8, half * 8 + 8) for m in transposed[u]])
            for k in range(NT):
                for hb in range(2):
                    m = te.matmul(ps[:], v_pad[:, k, hb, :], p_t[:, k, hb, :], start=(k == 0 and hb == 0),
                                  stop=(k == NT - 1 and hb == 1))
            m = PE.done.inc(m)
            pr.free["p_t"] = pr.free["v_pad"] = [m]
            emptied(b, A(act.copy, mix2[:, bass.ds(i, 1), half * BANK:(half + 1) * BANK].rearrange("p a b -> p (a b)"),
                         ps[:], after=[m], chain=False))

        score(0)
        for u in range(16):
            if u < 15:
                score(u + 1)
            if u == 8:
                weigh(0)
            turn_weights(u)
        weigh(1)
    at_space.close()
    dump("attn", mix2[:, 0:4, :])

    def add_residual(h, n, ps, m):
        r = resid[:, n, h * BANK:(h + 1) * BANK]
        return V(dve.tensor_tensor, r, r, ps[:], ALU.add, after=[m], chain=False)

    project_tokens(lambda k, n: mix2[:, k, n * P:(n + 1) * P], 8, dram["w_out_2"][0], 0, add_residual)
    dump("x3", resid[:])

    def norm_features(name, gain):
        with norm_space():
            with pr.repeat(name, NT) as i:
                m = rms_norm_tile(resid[:, bass.ds(i, 1), :].rearrange("p a b -> p (a b)"), xhat[:])
                to_features(xhat, ft, i * P, P, lambda k: col(gain, k), None, [m])

    norm_features("norm_cross", "norm_cross_g")
    with ExitStack() as ph:
        k_mem = sb("k_mem", [P, CROSS, MEM], where=ph)
        v_mem = sb("v_mem", [P, MEM // P, 512], where=ph)
        mem_ft = sb("mem_ft", [P, KD, MEM], where=ph)
        with norm_space() as nph:
            mem_t = sb("mem_t", [P, MEM // P, D], where=nph)
            SP.wait(Mark(V.done, V.done.count, None), Mark(A.done, A.done.count, None),
                    Mark(PE.done, PE.done.count, None))
            m_mem = loads("mem").inc(nc.sync.dma_start(mem_t[:], dram["mem_2"][0].rearrange("(n p) d -> p n d", p=P)))
            for n in range(MEM // P):
                m = rms_norm_tile(mem_t[:, n, :], xhat[:], after=[m_mem])
                to_features(xhat, mem_ft, n * P, P, lambda k: col("norm_mem_g", k), None, [m])
        for base in range(2):
            s, wt, m = load_panel(rows_of(dram["w_ck_2"][0], 0, D, base * 256, 256))
            PE.wait(m)
            for c in range(2):
                b, ps = bank()
                for k in range(KD):
                    m = te.matmul(ps[:, 0:MEM], wt[:, k, c * P:(c + 1) * P], mem_ft[:, k, :], start=(k == 0),
                                  stop=(k == KD - 1))
                m = PE.done.inc(m)
                emptied(b, A(act.copy, k_mem[:, base * 2 + c, :], ps[:, 0:MEM], after=[m], chain=False))
            used(s, m)
        halves = [load_panel(rows_of(dram["w_cv_2"][0], 4 * P * n, 4 * P, 0, 512)) for n in range(2)]
        PE.wait(*[m for _, _, m in halves])
        for n in range(MEM // P):
            b, ps = bank()
            for k in range(KD):
                m = te.matmul(ps[:], mem_ft[:, k, n * P:(n + 1) * P], halves[k // 4][1][:, k % 4, :],
                              start=(k == 0), stop=(k == KD - 1))
            m = PE.done.inc(m)
            emptied(b, V(dve.tensor_copy, v_mem[:, n, :], ps[:], after=[m], chain=False))
        for s, _, _ in halves:
            used(s, m)

        def q_done(c, h, ps, m):
            return A(act.copy, mix2[:, c, h * BANK:(h + 1) * BANK], ps, after=[m], chain=False)
        project(dram["w_cq_2"][0], 0, 512, q_done)

        q_h = sb("q_h", [P, T], where=ph)
        k_h = sb("k_h", [P, MEM], where=ph)
        v_h = sb("v_h", [P, MEM // P, P], where=ph)
        scores = [sb(f"c_scores{n}", [P, MEM], where=ph) for n in range(2)]
        row_stat = sb("c_row_stat", [P, 2, 4], where=ph)
        p_tc = sb("p_tc", [P, MEM // P, BANK], where=ph)
        with pr.repeat("cross", CROSS) as i:
            m_q = A(act.copy, q_h[:], mix2[:, bass.ds(i, 1), :].rearrange("p a b -> p (a b)"),
                    after=pr.free.get("q_h", ()))
            G(pool.tensor_copy, k_h[:], k_mem[:, bass.ds(i, 1), :].rearrange("p a b -> p (a b)"),
              after=pr.free.get("q_h", ()))
            m_kv = G(pool.tensor_copy, v_h[:], v_mem[:, :, bass.ds(i * P, P)])
            ready, transposed = {}, {}

            def c_score(n):
                s = scores[n % 2]
                b, ps = bank()
                m = PE(te.matmul, ps[:, 0:MEM], q_h[:, n * P:(n + 1) * P], k_h[:], start=True, stop=True,
                       after=[m_q, m_kv])
                m = A(act.mul, s[:], ps[:, 0:MEM], float(P) ** -0.5,
                      after=[m, *pr.free.get(f"c_scores{n % 2}", ())])
                emptied(b, m)
                ready[n] = softmax_rows(s, MEM, row_stat[:, n % 2, :], [m])

            def c_turn(n):
                b, ps = bank()
                PE.wait(ready[n])
                for k in range(2):
                    m = te.transpose(ps[:, k * P:(k + 1) * P], scores[n % 2][:, k * P:(k + 1) * P], ident[:])
                m = PE.done.inc(m)
                pr.free[f"c_scores{n % 2}"] = [m]
                e = V(dve.tensor_copy, p_tc[:, :, (n % 4) * P:(n % 4 + 1) * P],
                      ps[:, 0:2 * P].rearrange("p (a b) -> p a b", a=2), after=[m, *pr.free.get("p_tc", ())],
                      chain=False)
                emptied(b, e)
                transposed[n] = e

            def c_weigh(half):
                b, ps = bank()
                PE.wait(*[transposed[half * 4 + n] for n in range(4)])
                for k in range(2):
                    m = te.matmul(ps[:], v_h[:, k, :], p_tc[:, k, :], start=(k == 0), stop=(k == 1))
                m = PE.done.inc(m)
                pr.free["p_tc"] = [m]
                emptied(b, V(dve.tensor_scalar,
                             mix2[:, bass.ds(i, 1), half * BANK:(half + 1) * BANK].rearrange("p a b -> p (a b)"),
                             ps[:], 1.0, None, ALU.mult, after=[m], chain=False))
                pr.free["q_h"] = [m]

            c_score(0)
            for n in range(NT):
                if n < NT - 1:
                    c_score(n + 1)
                c_turn(n)
                if n == 3:
                    c_weigh(0)
            c_weigh(1)
        project_tokens(lambda k, n: mix2[:, k, n * P:(n + 1) * P], 4, dram["w_co_2"][0], 0, add_residual)
        pr.barrier()
    dump("x4", resid[:])

    norm_features("norm_mlp", "norm_mlp_g")
    w_mi, w_mo = dram["w_mlp_in_2"][0], dram["w_mlp_out_2"][0]
    with ExitStack() as ph:
        hid = [sb(f"mlp_hid{n}", [P, T], where=ph) for n in range(4)]
        with pr.repeat("mlp", NFF2 // 4) as i:
            for u in range(2):
                s, wt, m = load_panel(rows_of(w_mi, 0, D, i * 4 * P + u * 2 * P, 2 * P))
                PE.wait(m)
                ms = []
                for c in range(2):
                    hb = hid[u * 2 + c]
                    for h in range(HALVES):
                        hs = slice(h * BANK, (h + 1) * BANK)
                        b, ps = bank()
                        for k in range(KD):
                            mm = te.matmul(ps[:], wt[:, k, c * P:(c + 1) * P], ft[:, k, hs], start=(k == 0),
                                           stop=(k == KD - 1))
                        mm = PE.done.inc(mm)
                        m = A(act.activation, hb[:, hs], ps[:], ACT.Relu,
                              after=[mm, *pr.free.get(f"mhid{u}", ())], chain=False)
                        emptied(b, m)
                        ms.append(G(pool.tensor_tensor, hb[:, hs], hb[:, hs], hb[:, hs], ALU.mult, after=[m],
                                    chain=False))
                used(s, mm)
                s2, wd, m2 = load_panel(rows_of(w_mo, i * 4 * P + u * 2 * P, 2 * P, 0, D))
                if u == 0:
                    first = (s2, wd, m2, ms)
            for u, (s2, wd, m2, ms) in enumerate((first, (s2, wd, m2, ms))):
                PE.wait(m2, *ms)
                for n in range(NT):
                    for h in range(2):
                        b, ps = bank()
                        for c in range(2):
                            m = te.matmul(ps[:], hid[u * 2 + c][:, n * P:(n + 1) * P],
                                          wd[:, c, h * BANK:(h + 1) * BANK], start=(c == 0), stop=(c == 1))
                        m = PE.done.inc(m)
                        emptied(b, add_residual(h, n, ps, m))
                used(s2, m)
                pr.free[f"mhid{u}"] = [m]

    with norm_space() as nph:
        out_t = [sb(f"out_t{n}", [P, D], where=nph) for n in range(2)]
        stored = [Counter(pr, f"out{n}_stored", 16) for n in range(2)]
        m_rows = load_norm_rows("norm_final_g_2")
        V.wait(m_rows)
        dst = dram["out"][0].rearrange("(n p) d -> n p d", p=P)
        with pr.repeat("final", NT // 2) as i:
            for n in range(2):
                rms_norm_tile(resid[:, bass.ds(i * 2 + n, 1), :].rearrange("p a b -> p (a b)"), xhat[:])
                m = V(dve.tensor_tensor, out_t[n][:], xhat[:], norm_rows[:, 0, :], ALU.mult,
                      after=pr.free.get(f"out_t{n}", ()))
                SP.wait(m)
                pr.free[f"out_t{n}"] = [stored[n].inc(nc.sync.dma_start(
                    dst[bass.ds(i * 2 + n, 1)].rearrange("a p d -> p (a d)"), out_t[n][:]))]
        for s in stored:
            SP.wait(Mark(s, s.count, None))


def rotary_frequencies(np):
    half = HD // 2
    freq = np.float32(10000.0) ** (-np.arange(half, dtype=np.float32) / np.float32(half))
    return np.tile(freq.astype(np.float32), P // half)[:, None]


def kernel(**inputs):
    import numpy as np
    import concourse.bacc as bacc
    from concourse.bass_utils import run_bass_kernel_spmd

    arrays = {f"in_{name}": np.ascontiguousarray(a) for name, a in inputs.items()}
    arrays["in_inv_freq"] = rotary_frequencies(np)

    def declare(nc):
        dram = {name[3:]: nc.dram_tensor(name, a.shape, mybir.dt.from_np(a.dtype), kind="ExternalInput").ap()
                for name, a in arrays.items()}
        dram["out"] = nc.dram_tensor("out", (1, T, D), F32, kind="ExternalOutput").ap()
        return dram

    def fresh():
        return bacc.Bacc("TRN2", target_bir_lowering=False, num_devices=1)

    counting = fresh()
    plan = build(counting, declare(counting), {})
    nc = fresh()
    assert build(nc, declare(nc), plan) == plan
    r = run_bass_kernel_spmd(nc, [arrays], core_ids=[0])
    return r.results[0]["out"]
```

```python
import math
from contextlib import ExitStack, contextmanager

import concourse.bass as bass
from concourse import mybir

F32 = mybir.dt.float32
F32R = mybir.dt.float32r
I32 = mybir.dt.int32
ALU = mybir.AluOpType
ACT = mybir.ActivationFunctionType
AX = mybir.AxisListType.X

P = 128
BANK = 512
D = 1024
KD = D // P
T = 1024
NT = T // P
HALVES = T // BANK
EPS = 1e-6
ALPHA = 2.0 ** 0.25
DN_HEADS, GLA_HEADS = 4, 4
DN_W, GLA_W, GLA_K = 512, 512, 64
O_Q, O_K, O_V, O_Z, O_A = 0, 512, 1024, 1536, 2048
O_GQ, O_GK, O_GV, O_GG, O_GR = 2056, 2312, 2568, 3080, 3592
RANK = 16
TAU = 16.0
GC = 64
NGC = T // GC
FF = 2816
NFF = FF // P
HEADS, HD = 8, 64
RADIUS = 64
MEM = 256
CROSS = 4
FF2 = 4096
NFF2 = FF2 // P
PANEL = 1024
SLOTS = 6
AHEAD = 2
DELTA_LAG = 2


class Mark:

    def __init__(self, counter, count, loop, back=0):
        self.counter, self.count, self.loop, self.back = counter, count, loop, back

    def value(self, program):
        if self.loop is None:
            return self.count * self.counter.step
        per = self.loop.per(self.counter)
        if program.loop is self.loop:
            assert self.count >= self.back * per, "a first iteration would wait for a count below zero"
            return program.loop.i * (per * self.counter.step) + (self.count - self.back * per) * self.counter.step
        return (self.count + (self.loop.n - 1) * per) * self.counter.step


class Counter:
    def __init__(self, program, name, step=1):
        self.sem = program.stack.enter_context(program.nc.semaphore(name))
        self.program, self.name, self.step, self.count = program, name, step, 0
        program.counters.append(self)

    def inc(self, ins):
        ins.then_inc(self.sem, self.step)
        self.count += 1
        return Mark(self, self.count, self.program.loop)


class Queue:

    def __init__(self, program, engine, name, chain):
        self.program, self.engine, self.name, self.chain, self.last = program, engine, name, chain, None
        self.done = Counter(program, f"{name}_done")
        self.passed = {}

    def wait(self, *marks):
        need = {}
        for m in marks:
            here = m.loop is not None and m.loop is self.program.loop
            order = (1, -m.back, m.count) if here else (0, 0, m.value(self.program))
            if m.counter.name not in need or need[m.counter.name][0] < order:
                need[m.counter.name] = (order, m)
        need = {name: m for name, (_, m) in need.items()}
        for m in need.values():
            v = m.value(self.program)
            if self.program.loop is None:
                if self.passed.get(m.counter.name, 0) >= v:
                    continue
                self.passed[m.counter.name] = v
            self.engine.wait_ge(m.counter.sem, v)

    def __call__(self, f, *args, after=(), chain=None, **kw):
        own = [self.last] if (self.chain if chain is None else chain) and self.last is not None else []
        self.wait(*after, *own)
        self.last = self.done.inc(f(*args, **kw))
        return self.last


class Loop:
    def __init__(self, program, name, n, i):
        self.program, self.name, self.n, self.i = program, name, n, i
        self.start = {s.name: s.count for s in program.counters}

    def per(self, signal):
        return self.program.plan.get(self.name, {}).get("per", {}).get(signal.name, 0)


class Program:

    def __init__(self, nc, plan, stack):
        self.nc, self.plan, self.stack = nc, plan, stack
        self.counters, self.loop, self.free, self.new_plan = [], None, {}, {}
        self.pe = Queue(self, nc.tensor, "pe", False)
        self.v = Queue(self, nc.vector, "dve", True)
        self.a = Queue(self, nc.scalar, "act", True)
        self.g = Queue(self, nc.gpsimd, "pool", True)
        self.sp = Queue(self, nc.sync, "sp", False)
        self.engines = [self.pe, self.v, self.a, self.g]

    def barrier(self):
        marks = [Mark(q.done, q.done.count, None) for q in self.engines if q.done.count]
        for q in self.engines:
            q.wait(*marks)
            q.last = None

    @contextmanager
    def repeat(self, name, n):
        self.barrier()
        carried = self.plan.get(name, {}).get("free", {})
        for key in carried:
            if key.startswith("slot"):
                self.sp.wait(*self.free.get(key, ()))
        before = dict(self.free)
        with self.nc.Fori(0, n) as i:
            loop = Loop(self, name, n, i)
            self.loop = loop
            by_name = {s.name: s for s in self.counters}
            for key, marks in carried.items():
                self.free[key] = [Mark(by_name[s], loop.start[s] + k, loop, 1) for s, k in marks]
            for q in self.engines:
                q.last = self.free.get(f"last_{q.name}", [None])[0]
            yield i
            for q in self.engines:
                if q.last is not None:
                    self.free[f"last_{q.name}"] = [q.last]
            per = {s.name: s.count - loop.start.get(s.name, 0) for s in self.counters}
            free = {key: [(m.counter.name, m.count - loop.start[m.counter.name]) for m in marks]
                    for key, marks in self.free.items()
                    if any(m.loop is loop and not m.back for m in marks) and marks is not before.get(key)}
            self.new_plan[name] = {"per": per, "free": free}
            self.loop = None
        for s in self.counters:
            if s.name in loop.start:
                s.count = loop.start[s.name] + n * per[s.name]
        for q in self.engines + [self.sp]:
            q.passed = {}
            q.last = None
        self.barrier()


def build(nc, dram, plan):
    with ExitStack() as stack:
        program = Program(nc, plan, stack)
        emit(nc, program, stack, dram)
        return program.new_plan


def softplus(x, out, one, A, V, act, dve, after):
    V(dve.tensor_scalar, out[:], x[:], 0.0, None, ALU.max)
    m = V(dve.scalar_tensor_tensor, x[:], out[:], -2.0, x[:], ALU.mult, ALU.add)
    A(act.activation, x[:], x[:], ACT.Exp, after=[m])
    m = A(act.activation, x[:], x[:], ACT.Ln, bias=one[:], scale=1.0)
    return V(dve.tensor_tensor, out[:], out[:], x[:], ALU.add, after=[m])


def emit(nc, pr, stack, dram):
    PE, V, A, G, SP = pr.pe, pr.v, pr.a, pr.g, pr.sp
    te, dve, act, pool = nc.tensor, nc.vector, nc.scalar, nc.gpsimd
    debug = dram.get("debug", {})

    times = {}

    def sb(name, shape, dt=F32, where=None):
        times[name] = times.get(name, 0) + 1
        name = name if times[name] == 1 else f"{name}_{times[name]}"
        return (where or stack).enter_context(nc.sbuf_tensor(name, shape, dt))

    def spread(ap, axis, n):
        a = ap.unsqueeze(axis)
        shape = list(a.shape)
        shape[axis] = n
        return a.broadcast_to(shape)

    def loads(name):
        return Counter(pr, f"{name}_loaded", 16)

    vectors_loaded = loads("vectors")

    banks = [stack.enter_context(nc.psum_tensor(f"bank{n}", [P, BANK], F32)) for n in range(8)]
    turn = [0]
    in_use = set()

    def bank(*after):
        while turn[0] % 8 in in_use:
            turn[0] += 1
        n = turn[0] % 8
        turn[0] += 1
        in_use.add(n)
        PE.wait(*pr.free.get(f"bank{n}", ()), *after)
        return n, banks[n]

    def emptied(n, *marks):
        in_use.discard(n)
        pr.free[f"bank{n}"] = list(marks)

    panels = [sb(f"panel{n}", [P, PANEL]) for n in range(SLOTS)]
    arrived = [Counter(pr, f"panel{n}_arrived", 16) for n in range(SLOTS)]
    slot_turn = [0]

    def load_panel(src):
        n = slot_turn[0] % SLOTS
        slot_turn[0] += 1
        SP.wait(*pr.free.get(f"slot{n}", ()))
        view = panels[n][:, 0:src.shape[1] * src.shape[2]].rearrange("p (a b) -> p a b", a=src.shape[1])
        return n, view, arrived[n].inc(nc.sync.dma_start(view, src))

    halved = []
    halved_turn = [0]

    @contextmanager
    def halved_panels(count):
        with ExitStack() as ph:
            halved.extend((sb("panel_hi", [P, PANEL], F32R, ph), sb("panel_lo", [P, PANEL], F32R, ph))
                          for _ in range(count))
            halved_turn[0] = 0
            yield
            pr.barrier()
            halved.clear()

    def f32(view):
        return view.bitcast(F32)

    class Weights:

        def __init__(self, src, scale_row=None):
            n, view, m = load_panel(src)
            if scale_row is not None:
                m = G(pool.tensor_tensor, view, view, scale_row, ALU.mult, after=[m], chain=False)
            if not halved:
                self.parts, self.ready, self.key = (view,), [m], f"slot{n}"
                return
            t = halved_turn[0] % len(halved)
            halved_turn[0] += 1
            words = view.shape[1] * view.shape[2]
            hi, lo = (x[:, 0:words].rearrange("p (a b) -> p a b", a=view.shape[1]) for x in halved[t])
            self.key = f"halved{t}"
            m = A(act.activation, hi, view, ACT.Copy, after=[m, *pr.free.get(self.key, ())], chain=False)
            m = G(pool.tensor_tensor, lo, view, f32(hi), ALU.subtract, after=[m], chain=False)
            pr.free[f"slot{n}"] = [m]
            self.parts, self.ready = (hi, lo), [m]

        def at(self, k, c=slice(None)):
            return tuple(x[:, k, c] for x in self.parts)

        def used(self, mark):
            pr.free[self.key] = [mark]

    def stream(sources, scale_row=None):
        ahead = None
        for n, src in enumerate(sources):
            new = Weights(src, scale_row[n] if scale_row else None)
            if ahead is not None:
                yield ahead
            ahead = new
        yield ahead

    def products(ps, steps, start=True, stop=True):
        for n, (lhs, rhs) in enumerate(steps):
            pairs = [(lhs[0], rhs[0])] + ([(lhs[0], rhs[1]), (lhs[1], rhs[0])] if len(lhs) > 1 else [])
            for j, (a, b) in enumerate(pairs):
                m = te.matmul(ps, a, b, start=(start and n == 0 and j == 0),
                              stop=(stop and n == len(steps) - 1 and j == len(pairs) - 1))
        return m

    def rows_of(w, r0, nr, c0, ncol):
        return w[bass.ds(r0, nr) if not isinstance(r0, int) else slice(r0, r0 + nr),
                 bass.ds(c0, ncol) if not isinstance(c0, int) else slice(c0, c0 + ncol)].rearrange(
                     "(k p) c -> p k c", p=P)

    def dump(name, ap):
        if name in debug:
            pr.barrier()
            SP.wait(*[Mark(q.done, q.done.count, None) for q in pr.engines if q.done.count])
            m = loads("dump_" + name).inc(nc.sync.dma_start(debug[name], ap))
            for q in pr.engines:
                q.wait(m)

    ident = sb("ident", [P, P])
    ones = sb("ones", [P, P])
    upper = sb("upper", [P, P])
    m_ones = G(pool.memset, ones[:], 1.0)
    G(pool.affine_select, out=ident[:], in_=ones[:], compare_op=ALU.is_equal, fill=0.0, base=0,
      pattern=[[-1, P]], channel_multiplier=1)
    G(pool.affine_select, out=upper[:], in_=ones[:], compare_op=ALU.is_ge, fill=0.0, base=0,
      pattern=[[1, P]], channel_multiplier=-1)

    vectors = [("c", dram["c"]), ("ln0_g", dram["ln0_g"]), ("ln0_b", dram["ln0_b"]), ("b_ada", dram["b_ada"]),
               ("dn_conv", dram["dn_conv"]), ("ln1_g", dram["ln1_g"]), ("ln1_b", dram["ln1_b"]),
               ("dn_norm_g", dram["dn_norm_g"]), ("gla_norm_g", dram["gla_norm_g"]),
               ("gla_b_gate", dram["gla_b_gate"]), ("ffn_conv", dram["ffn_conv"]),
               ("ffn_conv_b", dram["ffn_conv_b"]), ("norm_mix_g", dram["norm_mix_g_2"]),
               ("norm_cross_g", dram["norm_cross_g_2"]), ("norm_mem_g", dram["norm_mem_g_2"]),
               ("norm_mlp_g", dram["norm_mlp_g_2"]), ("conv_w", dram["conv_w_2"]),
               ("conv_b", dram["conv_b_2"]), ("rg_a_b", dram["rg_a_b_2"]), ("rg_x_b", dram["rg_x_b_2"]),
               ("rg_lambda", dram["rg_lambda_2"])]
    first_col, n_rows = {}, 0
    for name, ap in vectors:
        first_col[name] = n_rows
        n_rows += ap.size() // P
    n_vt = -(-n_rows // P)
    cols = sb("cols", [P, n_vt * P])
    vr = ExitStack()
    vec_rows = sb("vec_rows", [P, n_vt, P], where=vr)
    m_zero = V(dve.memset, vec_rows[:], 0.0)
    SP.wait(m_zero)
    for name, ap in vectors:
        flat = ap
        while len(flat.shape) > 1:
            names = " ".join("abcdef"[:len(flat.shape)])
            flat = flat.rearrange(f"{names} -> ({names})")
        flat = flat.rearrange("(r p) -> r p", p=P)
        at, n = first_col[name], ap.size() // P
        done = 0
        while done < n:
            tile, row = divmod(at + done, P)
            take = min(n - done, P - row)
            m_vec = vectors_loaded.inc(nc.sync.dma_start(vec_rows[row:row + take, tile, :], flat[done:done + take, :]))
            done += take

    def col(name, n=0, count=1):
        return cols[:, first_col[name] + n:first_col[name] + n + count]

    PE.wait(G.last)
    b, ps = bank()
    for n in range(4):
        m = PE(te.transpose, ps[:, 0:P], ident[:], ident[:])
        head = A(act.copy, cols[:, 0:1], ident[:, 0:1], after=[G.last])
    emptied(b, m)
    V.wait(head)
    PE.wait(m_vec)
    for n in range(n_vt):
        b, ps = bank()
        m = PE(te.transpose, ps[:, 0:P], vec_rows[:, n, :], ident[:])
        emptied(b, V(dve.tensor_copy, cols[:, n * P:(n + 1) * P], ps[:, 0:P], after=[m]))
    cols_ready = V.last
    pr.barrier()
    vr.close()

    resid = sb("resid", [P, NT, D])
    ft_space = ExitStack()
    ft = []

    def open_ft(parts):
        pr.barrier()
        ft_space.close()
        ft[:] = ([sb("ft", [P, KD, T], where=ft_space)] if parts == 1 else
                 [sb(f"ft_{n}", [P, KD, T], F32R, ft_space) for n in ("hi", "lo")])

    def ft_at(k, c):
        return tuple(x[:, k, c] for x in ft)


    eps_col = sb("eps_col", [P, 1])
    V(dve.memset, eps_col[:], EPS)
    eps_q = sb("eps_q", [P, 1])
    V(dve.memset, eps_q[:], EPS * P)
    stats = sb("stats", [P, 2, 2, 6])
    moments = sb("moments", [P, NT, 2])
    held = sb("held", [P, 1])
    rstd = sb("rstd", [P, NT])
    newton = sb("newton", [P, 2, NT])
    now = sb("now", [P, 2, 3])

    def to_features(src, dst, tok0, n_tok, scale, bias, after, name="xhat0"):
        n = int(name[-1])
        for q in range(KD // 4):
            b, ps = bank()
            PE.wait(*after)
            for k in range(4):
                m = te.transpose(ps[:, k * P:k * P + n_tok], src[0:n_tok, (4 * q + k) * P:(4 * q + k + 1) * P],
                                 ident[0:n_tok, 0:n_tok])
            m = PE.done.inc(m)
            split = len(dst) > 1
            free = pr.free.get(f"feat_tmp{n}", ()) if split else ()
            for k in range(4):
                kk = 4 * q + k
                src_k = ps[:, k * P:k * P + n_tok]
                o = feat_tmp[n][:, kk, 0:n_tok] if split else dst[0][:, kk, bass.ds(tok0, n_tok)]
                if q == 0:
                    e = V(dve.tensor_scalar, o, src_k, scale(kk), bias(kk) if bias else None, ALU.mult,
                          ALU.add if bias else ALU.bypass, after=[m, *free], chain=False)
                else:
                    e = A(act.activation, o, src_k, ACT.Identity if bias else ACT.Copy, scale=scale(kk),
                          bias=bias(kk) if bias else 0.0, after=[m, *free], chain=False)
            emptied(b, e)
            if split:
                ks = slice(4 * q, 4 * q + 4)
                hi, lo = (x[:, ks, bass.ds(tok0, n_tok)] for x in dst)
                tmp = feat_tmp[n][:, ks, 0:n_tok]
                e = A(act.activation, hi, tmp, ACT.Copy, after=[e], chain=False)
                e = V(dve.tensor_tensor, lo, tmp, f32(hi), ALU.subtract, after=[e], chain=False)
        if split:
            pr.free[f"feat_tmp{n}"] = [e]
        pr.free[name] = [m]

    def rms_heads(ps, m, tmp, out, gain):
        flat = tmp[:].rearrange("p a b -> p (a b)")
        m = A(act.activation, flat, ps[:], ACT.Square, after=[m, *pr.free.get("sq", ())])
        b, ps2 = bank(m)
        m = PE(te.matmul, ps2[:], ones[:], flat, start=True, stop=True)
        A(act.activation, flat, ps2[:], ACT.Ln, bias=eps_col[:], scale=1.0 / P, after=[m])
        emptied(b, A.last)
        m = A(act.activation, flat, flat, ACT.Exp, scale=-0.5)
        m = V(dve.scalar_tensor_tensor, out, ps[:].rearrange("p (h c) -> p h c", h=4), gain, tmp[:], ALU.mult,
              ALU.mult, after=[m])
        pr.free["sq"] = [m]
        return m

    def tile_of(t, n):
        return t[:, n, :] if isinstance(n, int) else t[:, bass.ds(n, 1), :].rearrange("p a b -> p (a b)")

    norm_rows, xhat, square, feat_tmp = None, None, None, None

    @contextmanager
    def norm_space(rows=(), row_scale=1.0):
        nonlocal norm_rows, xhat, square, feat_tmp
        pr.barrier()
        act.preload_act_table_set("natural_log_exp_and_others")
        with ExitStack() as ph:
            norm_rows = sb("norm_rows", [P, 2, D], where=ph) if rows else None
            xhat = [sb(f"xhat{n}", [P, D], where=ph) for n in range(2)]
            square = sb("square", [P, D], where=ph)
            feat_tmp = [sb(f"feat_tmp{n}", [P, KD, P], where=ph) for n in range(2)] if len(ft) > 1 else None
            if rows:
                SP.wait(*[Mark(q.done, q.done.count, None) for q in (V, A, G) if q.done.count])
                sig = loads(f"rows_{rows[0]}")
                for n, name in enumerate(rows):
                    v = dram[name]
                    m = sig.inc(nc.sync.dma_start(norm_rows[:, n, :],
                                                  (v[0] if len(v.shape) == 2 else v).partition_broadcast(P)))
                G.wait(m)
                V(dve.tensor_scalar, norm_rows[:, 0:len(rows), :], norm_rows[:, 0:len(rows), :], row_scale, None,
                  ALU.mult, after=[m]) if row_scale != 1.0 else V.wait(m)
                G.wait(*([V.last] if row_scale != 1.0 else []))
            yield ph
            pr.barrier()

    def deviation(of, scale, n):
        x, y = newton[:, 0, 0:n], rstd[:, 0:n]
        m = V(dve.tensor_scalar, x, of, scale, EPS, ALU.mult, ALU.add, after=[A.last] if A.last else [])
        A(act.activation, y, x, ACT.Ln, after=[m])
        m = A(act.activation, y, y, ACT.Exp, scale=-0.5)
        step = newton[:, 1, 0:n]
        V(dve.tensor_tensor, step, y, y, ALU.mult, after=[m])
        V(dve.tensor_tensor, step, step, x, ALU.mult)
        V(dve.tensor_scalar, step, step, -0.5, 1.5, ALU.mult, ALU.add)
        V(dve.tensor_tensor, y, y, step, ALU.mult)

    def moments_of(name, x):
        with pr.repeat(name, NT // 2) as i:
            for u in range(2):
                for n in range(2):
                    V(dve.bn_stats, stats[:, u, n, :], tile_of(x, i * 2 + u)[:, n * BANK:(n + 1) * BANK],
                      after=pr.free.get("stats", ()), chain=False)
            V(dve.memset, held[:], 0.0, after=pr.free.get("now2", ()))
            for u in range(2):
                m = V(dve.bn_aggr, now[:, u, 0:2], stats[:, u, :, :].rearrange("p a b -> p (a b)"), chain=False)
            pr.free["stats"] = [m]
            pr.free["now2"] = [V(dve.tensor_copy, moments[:, bass.ds(i * 2, 2), :], now[:, :, 0:2])]
        deviation(moments[:, :, 1], 1.0, NT)

    def squares_of(name, x, n_tiles=NT):
        if name is None:
            for n in range(n_tiles):
                m = A(act.activation, square[:], x[:, n, :], ACT.Square, accum_out=moments[:, n, 0:1])
        else:
            with pr.repeat(name, n_tiles) as i:
                A(act.activation, square[:], tile_of(x, i), ACT.Square,
                  accum_out=moments[:, bass.ds(i, 1), 0:1].rearrange("p a b -> p (a b)"))
        deviation(moments[:, 0:n_tiles, 0], 1.0 / D, n_tiles)

    def normed(x, n, u, centred):
        after = pr.free.get(f"xhat{u}", ())
        if isinstance(n, int):
            mean, dev = moments[:, n, 0:1], rstd[:, n:n + 1]
        else:
            V(dve.tensor_copy, now[:, u, 0:1], moments[:, bass.ds(n, 1), 0:1].rearrange("p a b -> p (a b)"),
              after=pr.free.get("now", ()), chain=False)
            V(dve.tensor_copy, now[:, u, 1:2], rstd[:, bass.ds(n, 1)], chain=False)
            mean, dev = now[:, u, 0:1], now[:, u, 1:2]
        if centred:
            m = V(dve.tensor_scalar, xhat[u][:], tile_of(x, n), mean, dev, ALU.subtract, ALU.mult, after=after)
        else:
            m = V(dve.tensor_scalar, xhat[u][:], tile_of(x, n), dev, None, ALU.mult, after=after)
        pr.free["now"] = [m]
        return m

    def affine(x, n, u, m):
        m = V(dve.tensor_tensor, tile_of(x, n), xhat[u][:], norm_rows[:, 0, :], ALU.mult)
        return m, G(pool.tensor_tensor, tile_of(x, n), tile_of(x, n), norm_rows[:, 1, :], ALU.add, after=[m],
                    chain=False)

    def layer_norm_features(name, rows, which):
        with norm_space(rows, ALPHA):
            moments_of(name + "_moments", resid)
            with pr.repeat(name, NT // 2) as i:
                for u in range(2):
                    m = normed(resid, i * 2 + u, u, True)
                    read, _ = affine(resid, i * 2 + u, u, m)
                    to_features(xhat[u], ft, (i * 2 + u) * P, P, lambda k: in_scale[:, which, k:k + 1],
                                lambda k: in_bias[:, which, k:k + 1], [m], f"xhat{u}")
                    pr.free[f"xhat{u}"].append(read)

    def rms_norm_features(name, gain):
        with norm_space():
            squares_of(name + "_squares", resid)
            with pr.repeat(name, NT // 2) as i:
                for u in range(2):
                    m = normed(resid, i * 2 + u, u, False)
                    to_features(xhat[u], ft, (i * 2 + u) * P, P, lambda k: col(gain, k), None, [m], f"xhat{u}")

    b1 = ExitStack()
    gate_row = sb("gate_row", [P, 2, D])
    in_scale = sb("in_scale", [P, 2, KD])
    in_bias = sb("in_bias", [P, 2, KD])
    mod_row = sb("mod_row", [P, 6, D], where=b1)
    with ExitStack() as ph:
        cond = sb("cond", [P, KD], where=ph)
        cond_b = sb("cond_b", [P, KD, P], where=ph)
        A(act.activation, cond[:], col("c", 0, KD), ACT.Silu, after=[cols_ready])
        m_cond = V(dve.tensor_copy, cond_b[:], spread(cond[:], 2, P), after=[A.last])
        w_ada = dram["w_ada"][0]
        m_b = loads("b_ada").inc(nc.sync.dma_start(mod_row[:].rearrange("p a b -> p (a b)"),
                                               dram["b_ada"][0].partition_broadcast(P)))
        PE.wait(m_cond)
        V.wait(m_b)
        with pr.repeat("ada", 6) as i:
            for n in range(2):
                b, ps = bank()
                for k2 in range(KD // 2):
                    w = Weights(rows_of(w_ada, 2 * k2 * P, 2 * P, i * D + n * BANK, BANK))
                    PE.wait(*w.ready)
                    for k in range(2):
                        mm = te.matmul(ps[:], cond_b[:, 2 * k2 + k, :], w.parts[0][:, k, :], start=(k2 == k == 0),
                                       stop=(k2 == KD // 2 - 1 and k == 1))
                    mm = PE.done.inc(mm)
                    w.used(mm)
                o = mod_row[:, bass.ds(i, 1), n * BANK:(n + 1) * BANK].rearrange("p a b -> p (a b)")
                emptied(b, V(dve.tensor_tensor, o, ps[:], o, ALU.add, after=[mm]))
    dump("mod", mod_row[0:1, :, :].rearrange("p a b -> p (a b)"))
    SH_A, SC_A, GT_A, SH_F, SC_F, GT_F = range(6)

    mod_col = sb("mod_col", [P, 4, KD], where=b1)
    square = sb("mod_diagonal", [P, D], where=b1)
    for n, part in enumerate((SH_A, SC_A, SH_F, SC_F)):
        for k in range(KD):
            V(dve.tensor_tensor, square[:, k * P:(k + 1) * P], mod_row[:, part, k * P:(k + 1) * P], ident[:],
              ALU.mult, chain=k == 0)
        V(dve.tensor_reduce, mod_col[:, n, :], square[:].rearrange("p (k c) -> p k c", k=KD), AX, ALU.add)
    for n, (g, b) in enumerate((("ln0_g", "ln0_b"), ("ln1_g", "ln1_b"))):
        V(dve.tensor_scalar, mod_col[:, 2 * n + 1, :], mod_col[:, 2 * n + 1, :], 1.0, None, ALU.add)
        V(dve.tensor_tensor, in_scale[:, n, :], mod_col[:, 2 * n + 1, :], col(g, 0, KD), ALU.mult)
        V(dve.tensor_tensor, in_bias[:, n, :], mod_col[:, 2 * n + 1, :], col(b, 0, KD), ALU.mult)
        V(dve.tensor_tensor, in_bias[:, n, :], in_bias[:, n, :], mod_col[:, 2 * n, :], ALU.add)
    for n, part in enumerate((GT_A, GT_F)):
        V(dve.tensor_scalar, gate_row[:, n, :], mod_row[:, part, :], 1.0, None, ALU.add)

    pr.barrier()
    b1.close()

    open_ft(1)
    m_x = loads("x").inc(nc.sync.dma_start(resid[:], dram["x"][0].rearrange("(n p) d -> p n d", p=P)))
    V.wait(m_x)
    layer_norm_features("norm0", ("ln0_g", "ln0_b"), 0)
    dump("x0", resid[:])
    dump("h0", ft[0][:])

    def project(w, c0, n_cols, done):
        for c, wt in enumerate(stream([rows_of(w, 0, D, c0 + base, P) for base in range(0, n_cols, P)])):
            PE.wait(*wt.ready)
            for h in range(HALVES):
                b, ps = bank()
                mm = PE.done.inc(products(ps[:], [(wt.at(k), ft_at(k, slice(h * BANK, (h + 1) * BANK)))
                                                  for k in range(KD)]))
                if h == HALVES - 1:
                    wt.used(mm)
                emptied(b, done(c, h, ps[:], mm))

    def project_tokens(src, n_k, w, r0, c0, halves, take, n_tiles=NT, scale_row=None):
        panels_of = [(h, k) for h in halves for k in range(0, n_k, 2)]
        views = [rows_of(w, r0 + k * P, 2 * P, c0 + h * BANK, BANK) for h, k in panels_of]
        rows = [spread(scale_row[:, h * BANK:(h + 1) * BANK], 1, 2) for h, _ in panels_of] if scale_row is not None \
            else None
        held_banks = []
        for (h, k0), wt in zip(panels_of, stream(views, rows)):
            PE.wait(*wt.ready)
            for n in range(n_tiles):
                if k0 == 0:
                    held_banks.append(bank())
                b, ps = held_banks[n]
                m = products(ps[:], [(src(k0 + j, n), wt.at(j)) for j in range(2)], k0 == 0, k0 == n_k - 2)
                if k0 == n_k - 2:
                    m = PE.done.inc(m)
                    emptied(b, take(h, n, ps, m))
            if k0 != n_k - 2:
                m = PE.done.inc(m)
            else:
                held_banks = []
            wt.used(m)

    def add_residual(h, n, ps, m):
        r = resid[:, n, h * BANK:(h + 1) * BANK]
        return V(dve.tensor_tensor, r, r, ps[:], ALU.add, after=[m], chain=False)

    w_in = dram["w_in"][0]
    mixed_space = ExitStack()
    mixed = sb("mixed", [P, 8, T], where=mixed_space)
    mx = ExitStack()

    v_feat = sb("v_feat", [P, 4, T], where=mx)
    cv = ExitStack()
    pre = [sb(f"conv_in{n}", [P, 3 + T], where=cv) for n in range(2)]
    conv = [sb(f"conv_out{n}", [P, T], where=cv) for n in range(2)]
    taps = sb("taps", [P, 12, 4], where=cv)
    tap_now = sb("tap_now", [P, 4, 4], where=cv)
    V(dve.tensor_copy, taps[:], col("dn_conv", 0, 48).rearrange("p (j c) -> p c j", j=4))
    for n in range(2):
        V(dve.memset, pre[n][:, 0:3], 0.0)

    def causal_conv(buf, n, w, n_taps, bias=None, conv=conv):
        lead = 3 - (n_taps - 1)
        V(dve.tensor_scalar, conv[n][:], buf[:, lead:lead + T], w(0), bias, ALU.mult,
          ALU.add if bias is not None else ALU.bypass, after=pr.free.get(f"conv{n}", ()))
        for j in range(1, n_taps):
            V(dve.scalar_tensor_tensor, conv[n][:], buf[:, lead + j:lead + j + T], w(j), conv[n][:], ALU.mult,
              ALU.add)
        return V.last

    def qkv_chunks(dst, i, c0):
        V(dve.tensor_copy, tap_now[:], taps[:, bass.ds(i * 4, 4), :])
        taps_ready = V.last

        def done(c, h, ps, m):
            n = c % 2
            m = A(act.copy, pre[n][:, 3 + h * BANK:3 + (h + 1) * BANK], ps,
                  after=[m, *(pr.free.get(f"pre{n}", ()) if h == 0 else ())], chain=False)
            if h == HALVES - 1:
                V.wait(m)
                r = causal_conv(pre[n], n, lambda j: tap_now[:, c, j:j + 1], 4)
                pr.free[f"pre{n}"] = [r]
                pr.free[f"conv{n}"] = [A(act.activation, dst(c), conv[n][:], ACT.Silu, after=[r], chain=False)]
            return m
        project(w_in, c0, 512, done)

    act.preload_act_table_set("silu_and_others")
    with pr.repeat("qk", 2) as i:
        qkv_chunks(lambda c: mixed[:, bass.ds(i * 4 + c, 1), :].rearrange("p a b -> p (a b)"), i, i * 512)
    qkv_chunks(lambda c: v_feat[:, c, :], 2, O_V)
    pr.barrier()
    cv.close()
    dump("q", mixed[:, 0:4, :])
    dump("kv", mixed[:, 4:8, :])

    log_a = sb("log_a", [P, NT, 4], where=mx)
    beta = sb("beta", [P, NT, 4], where=mx)
    with ExitStack() as ph:
        w_ab = sb("w_ab", [P, KD, 8], where=ph)
        heads = sb("heads", [P, 2, 4], where=ph)
        ab = sb("ab", [P, NT, 8], where=ph)
        tmp = sb("ab_tmp", [P, NT, 4], where=ph)
        one = sb("one_col", [P, 1], where=ph)
        SP.wait(Mark(V.done, V.done.count, None), Mark(A.done, A.done.count, None))
        sig = loads("ab")
        sig.inc(nc.sync.dma_start(w_ab[:], rows_of(w_in, 0, D, O_A, 8)))
        sig.inc(nc.sync.dma_start(heads[:, 0, :], dram["dn_a_log"][0].partition_broadcast(P)))
        m_ab = sig.inc(nc.sync.dma_start(heads[:, 1, :], dram["dn_dt_bias"][0].partition_broadcast(P)))
        V(dve.memset, one[:], 1.0)
        PE.wait(m_ab)
        b, ps = bank()
        for n in range(NT):
            for k in range(KD):
                m = te.matmul(ps[:, n * 8:n * 8 + 8], ft[0][:, k, n * P:(n + 1) * P], w_ab[:, k, :],
                              start=(k == 0), stop=(k == KD - 1))
        m = PE.done.inc(m)
        emptied(b, V(dve.tensor_copy, ab[:], ps[:, 0:NT * 8].rearrange("p (n c) -> p n c", c=8), after=[m, m_ab]))
        A(act.activation, heads[:, 0, :], heads[:, 0, :], ACT.Exp, after=[m_ab])
        m = V(dve.tensor_tensor, tmp[:], ab[:, :, 0:4], spread(heads[:, 1, :], 1, NT), ALU.add)
        softplus(tmp, log_a, one, A, V, act, dve, m)
        V(dve.tensor_tensor, log_a[:], log_a[:], spread(heads[:, 0, :], 1, NT), ALU.mult, after=[A.last])
        V(dve.tensor_scalar, log_a[:], log_a[:], -1.0, None, ALU.mult)
        A(act.activation, beta[:], ab[:, :, 4:8], ACT.Sigmoid, after=[V.last])
        pr.barrier()
    dump("log_a", log_a[:])
    dump("beta", beta[:])

    SCALE_Q = DN_W // DN_HEADS
    dn = ExitStack()
    H4 = DN_HEADS

    def four(name):
        return sb(name, [P, H4, P], where=dn)

    def words(t):
        return t[:].rearrange("p a b -> p (a b)")

    masks = sb("masks", [P, 7, P], where=dn)
    strict = sb("strict", [P, P], where=dn)
    for lv in range(7):
        s = 1 << lv
        G(pool.memset, masks[:, lv, :], 0.0)
        view = masks[:, lv, :].rearrange("p (n h c) -> p n h c", h=2, c=s)[:, :, 1, :]
        ones_v = ones[:].rearrange("p (n h c) -> p n h c", h=2, c=s)[:, :, 1, :]
        G(pool.affine_select, out=view, in_=ones_v, compare_op=ALU.is_ge, fill=0.0, base=0,
          pattern=[[-2 * s, P // (2 * s)], [0, s]], channel_multiplier=1)
        G(pool.affine_select, out=view, in_=view, compare_op=ALU.is_ge, fill=0.0, base=s - 1,
          pattern=[[2 * s, P // (2 * s)], [0, s]], channel_multiplier=-1)
    G(pool.affine_select, out=strict[:], in_=ones[:], compare_op=ALU.is_gt, fill=0.0, base=0,
      pattern=[[1, P]], channel_multiplier=-1)
    state = four("state")
    V(dve.memset, state[:], 0.0)

    class DeltaTile:

        def __init__(self, u):
            self.la, self.be = sb(f"la_t{u}", [P, H4], where=dn), sb(f"be_t{u}", [P, H4], where=dn)
            self.g_col = sb(f"g_col{u}", [P, 4, H4], where=dn)
            self.g_row = self.ktok = four(f"g_row_ktok{u}")
            self.b_row = self.inv_t = four(f"b_row_inv_t{u}")
            self.decay = self.prod = four(f"decay_prod{u}")
            self.q, self.k = four(f"qn{u}"), four(f"kn{u}")
            self.be_b = self.vt = self.rhs = four(f"vt_rhs{u}")
            self.la_b = self.lt = four(f"lt{u}")
            self.ltm = self.vnew = four(f"ltm_vnew{u}")
            self.at, self.vtok = four(f"at{u}"), four(f"vtok{u}")
            self.sq = self.inv = four(f"sq_inv{u}")

    def per_head(ps, lhs, rhs_of):
        for h in range(H4):
            m = te.matmul(ps[:, h * P:(h + 1) * P], lhs(h), rhs_of(h), start=True, stop=True)
        return PE.done.inc(m)

    ID4 = spread(ident[:], 1, H4)
    state_free = []

    def delta_tile(t, n):
        tok = bass.ds(n * P, P)
        V(dve.tensor_copy, t.la[:], log_a[:, bass.ds(n, 1), :].rearrange("p a b -> p (a b)"), chain=False)
        V(dve.tensor_copy, t.be[:], beta[:, bass.ds(n, 1), :].rearrange("p a b -> p (a b)"), chain=False)
        V(dve.tensor_copy, t.la_b[:], spread(t.la[:], 2, P))
        m_b = V(dve.tensor_copy, t.be_b[:], spread(t.be[:], 2, P))
        yield
        b0, ps = bank(m_b)
        m = per_head(ps, lambda h: t.la_b[:, h, :], lambda h: upper[:])
        m_g = A(act.copy, words(t.g_row), ps[:], after=[m])
        emptied(b0, m_g)
        b0, ps = bank()
        m = PE(te.matmul, ps[:, 0:H4], upper[:], t.la[:], start=True, stop=True)
        m = V(dve.tensor_copy, t.g_col[:, 0, :], ps[:, 0:H4], after=[m])
        emptied(b0, m)
        b0, ps = bank()
        m = per_head(ps, lambda h: t.be_b[:, h, :], lambda h: ident[:])
        m_br = V(dve.tensor_copy, words(t.b_row), ps[:], after=[m])
        emptied(b0, m_br)
        V(dve.tensor_tensor, t.decay[:], t.g_row[:], spread(t.g_col[:, 0, :], 2, P), ALU.subtract, after=[m_g])
        m = V(dve.tensor_scalar, t.decay[:], t.decay[:], 0.0, None, ALU.min)
        A(act.activation, t.decay[:], t.decay[:], ACT.Exp, after=[m])
        g_end = t.g_row[:, :, P - 1]
        m = V(dve.tensor_tensor, t.g_col[:, 2, :], g_end, t.g_col[:, 0, :], ALU.subtract)
        A(act.activation, t.g_col[:, 1, :], t.g_col[:, 0, :], ACT.Exp)
        A(act.activation, t.g_col[:, 2, :], t.g_col[:, 2, :], ACT.Exp, after=[m])
        m_e = A(act.activation, t.g_col[:, 3, :], g_end, ACT.Exp)
        m_er = A(act.activation, t.g_row[:], t.g_row[:], ACT.Exp)
        m_v = G(pool.tensor_copy, t.vt[:], v_feat[:, :, tok], after=[m_br])
        for src, dst, factor in ((mixed[:, 0:4, tok], t.q, float(SCALE_Q)), (mixed[:, 4:8, tok], t.k, 1.0)):
            m = G(pool.tensor_tensor, t.sq[:], src, src, ALU.mult, after=[V.last])
            yield
            b0, ps = bank(m)
            m = PE(te.matmul, ps[:], ones[:], words(t.sq), start=True, stop=True)
            A(act.activation, words(t.sq), ps[:], ACT.Ln, bias=eps_q[:] if factor != 1.0 else eps_col[:],
              scale=factor, after=[m])
            emptied(b0, A.last)
            m = A(act.activation, words(t.sq), words(t.sq), ACT.Exp, scale=-0.5)
            m_n = V(dve.tensor_tensor, dst[:], src, t.sq[:], ALU.mult, after=[m])
            if factor != 1.0:
                m_dec = V(dve.tensor_tensor, t.decay[:], t.decay[:], spread(upper[:], 1, H4), ALU.mult, after=[m_e])
        yield
        b0, ps = bank(m_n)
        m = per_head(ps, lambda h: t.k[:, h, :], lambda h: t.k[:, h, :])
        V(dve.tensor_tensor, words(t.lt), ps[:], words(t.decay), ALU.mult, after=[m])
        emptied(b0, V.last)
        b0, ps = bank()
        m = per_head(ps, lambda h: t.k[:, h, :], lambda h: t.q[:, h, :])
        m_at = V(dve.tensor_tensor, words(t.at), ps[:], words(t.decay), ALU.mult, after=[m])
        emptied(b0, m_at)
        V(dve.tensor_tensor, t.lt[:], t.lt[:], t.b_row[:], ALU.mult)
        m_lt = V(dve.tensor_tensor, t.lt[:], t.lt[:], spread(strict[:], 1, H4), ALU.mult)
        m_l = V(dve.tensor_tensor, t.ltm[:], t.lt[:], spread(masks[:, 0, :], 1, H4), ALU.mult)
        m_xt = V(dve.tensor_tensor, t.inv_t[:], ID4, t.ltm[:], ALU.subtract)
        m_qd = V(dve.tensor_tensor, t.q[:], t.q[:], t.g_row[:], ALU.mult, after=[m_er])
        for src, dst, w in ((t.vt, t.vtok, m_v), (t.k, t.ktok, m_qd)):
            b0, ps = bank(w)
            for h in range(H4):
                m = te.transpose(ps[:, h * P:(h + 1) * P], src[:, h, :], ident[:])
            m = PE.done.inc(m)
            m_tok = A(act.copy, words(dst), ps[:], after=[m, w])
            emptied(b0, m_tok)
        b0, ps = bank(m_l)
        for h in range(H4):
            mm = te.transpose(ps[:, h * P:(h + 1) * P], t.ltm[:, h, :], ident[:])
        mm = PE.done.inc(mm)
        m_x = V(dve.tensor_tensor, t.inv[:], ID4, ps[:].rearrange("p (h c) -> p h c", h=H4), ALU.subtract,
                after=[mm])
        emptied(b0, m_x)
        for lv in range(1, 7):
            m = G(pool.tensor_tensor, t.ltm[:], t.lt[:], spread(masks[:, lv, :], 1, H4), ALU.mult,
                  after=[m_lt, mm, m_xt])
            yield
            b0, ps = bank(m, m_x)
            mm = per_head(ps, lambda h: t.ltm[:, h, :], lambda h: t.inv[:, h, :])
            m = A(act.copy, words(t.prod), ps[:], after=[mm])
            emptied(b0, m)
            yield
            b1_, ps1 = bank(m, m_xt)
            m1 = per_head(ps1, lambda h: t.prod[:, h, :], lambda h: t.inv_t[:, h, :])
            m0 = m1
            if lv < 6:
                b2_, ps2 = bank()
                m0 = per_head(ps2, lambda h: t.inv_t[:, h, :], lambda h: t.prod[:, h, :])
                m_x = V(dve.tensor_tensor, words(t.inv), words(t.inv), ps2[:], ALU.subtract, after=[m0])
                emptied(b2_, m_x)
            m_xt = V(dve.tensor_tensor, words(t.inv_t), words(t.inv_t), ps1[:], ALU.subtract, after=[m0])
            emptied(b1_, m_xt)
            A.wait(m0)
        V(dve.tensor_tensor, t.ktok[:], t.ktok[:], spread(t.g_col[:, 2, :], 2, P), ALU.mult, after=[m_tok])
        yield
        b0, ps = bank(*state_free)
        m = per_head(ps, lambda h: t.k[:, h, :], lambda h: state[:, h, :])
        V(dve.tensor_tensor, t.rhs[:], ps[:].rearrange("p (h c) -> p h c", h=H4), spread(t.g_col[:, 1, :], 2, P),
          ALU.mult, after=[m])
        emptied(b0, V.last)
        V(dve.tensor_tensor, t.rhs[:], t.vtok[:], t.rhs[:], ALU.subtract)
        m = V(dve.tensor_tensor, t.rhs[:], t.rhs[:], spread(t.be[:], 2, P), ALU.mult)
        yield
        b0, ps = bank(m, m_xt)
        m = per_head(ps, lambda h: t.inv_t[:, h, :], lambda h: t.rhs[:, h, :])
        m_vn = A(act.copy, words(t.vnew), ps[:], after=[m])
        emptied(b0, m_vn)
        yield
        b0, ps = bank(m_qd, m_vn, m_at)
        for h in range(H4):
            te.matmul(ps[:, h * P:(h + 1) * P], state[:, h, :], t.q[:, h, :], start=True, stop=False)
            m = te.matmul(ps[:, h * P:(h + 1) * P], t.vnew[:, h, :], t.at[:, h, :], start=False, stop=True)
        m_o = PE.done.inc(m)
        V(dve.tensor_tensor, state[:], state[:], spread(t.g_col[:, 3, :], 2, P), ALU.mult, after=[m_o])
        b1_, ps1 = bank()
        m = per_head(ps1, lambda h: t.ktok[:, h, :], lambda h: t.vnew[:, h, :])
        m = V(dve.tensor_tensor, words(state), words(state), ps1[:], ALU.add, after=[m])
        emptied(b1_, m)
        state_free[:] = [m]
        pr.free["state"] = [m]
        yield
        emptied(b0, rms_heads(ps, m_o, t.sq, mixed[:, 0:4, tok], col("dn_norm_g")))

    def in_turn(steps, lag):
        at = [-lag * n for n in range(len(steps))]
        while steps:
            for n in range(len(at)):
                if at[n] >= 0 and steps[n] is not None and next(steps[n], "over") == "over":
                    steps[n] = None
                at[n] += 1
            if all(x is None for x in steps):
                break

    tiles = [DeltaTile(u) for u in range(2)]
    act.preload_act_table_set("natural_log_exp_and_others")
    with pr.repeat("delta", NT // 2) as i:
        V.wait(*[m for q in pr.engines for m in pr.free.get(f"last_{q.name}", ())])
        for n in range(8):
            emptied(n)
        state_free[:] = pr.free.get("state", ())
        in_turn([delta_tile(t, i * 2 + u) for u, t in enumerate(tiles)], DELTA_LAG)
    dn.close()
    dump("o_dn", mixed[:, 0:4, :])
    mx.close()

    gl = ExitStack()
    g_qk = sb("g_qk", [P, 4, T], where=gl)
    k_dec = sb("k_dec", [P, 2, T], where=gl)
    g_v = sb("g_v", [P, NT, GLA_W], where=gl)
    g_last = sb("g_last", [P, 2, NGC], where=gl)

    def gqk_done(c, h, ps, m):
        return A(act.mul, g_qk[:, c, h * BANK:(h + 1) * BANK], ps, GLA_K ** -0.5 if c < 2 else 1.0, after=[m],
                 chain=False)
    project(w_in, O_GQ, 512, gqk_done)
    project_tokens(lambda k, n: ft_at(k, slice(n * P, (n + 1) * P)), KD, w_in, 0, O_GV, (0,),
                   lambda h, n, ps, m: V(dve.tensor_copy, g_v[:, n, :], ps[:], after=[m], chain=False))

    with ExitStack() as ph:
        w_r = sb("w_r", [P, KD, RANK], where=ph)
        w_g2 = sb("w_g2", [RANK, 2 * P], where=ph)
        r_feat = sb("r_feat", [RANK, T], where=ph)
        cum = sb("cum", [P, 2, T], where=ph)
        tmp = sb("cum_tmp", [P, 2, T], where=ph)
        keep = sb("keep", [P, T], where=ph)
        one = sb("one_col2", [P, 1], where=ph)
        SP.wait(Mark(V.done, V.done.count, None), Mark(A.done, A.done.count, None))
        sig = loads("gate")
        sig.inc(nc.sync.dma_start(w_r[:], rows_of(w_in, 0, D, O_GR, RANK)))
        m_r = sig.inc(nc.sync.dma_start(w_g2[:], dram["gla_w_gate2"][0]))
        V(dve.memset, one[:], 1.0)
        V(dve.memset, keep[:], 1.0)
        m_keep = V(dve.memset, keep[:].rearrange("p (n c) -> p n c", c=GC)[:, :, 0:1], 0.0)
        PE.wait(m_r)
        for h in range(HALVES):
            b, ps = bank()
            for k in range(KD):
                m = te.matmul(ps[0:RANK, :], w_r[:, k, :], ft[0][:, k, h * BANK:(h + 1) * BANK], start=(k == 0),
                              stop=(k == KD - 1))
            m = PE.done.inc(m)
            emptied(b, A(act.copy, r_feat[:, h * BANK:(h + 1) * BANK], ps[0:RANK, :], after=[m]))
        for c in range(2):
            for h in range(HALVES):
                b, ps = bank()
                m = PE(te.matmul, ps[:], w_g2[:, c * P:(c + 1) * P], r_feat[:, h * BANK:(h + 1) * BANK],
                       start=True, stop=True, after=[A.last])
                emptied(b, V(dve.tensor_scalar, tmp[:, c, h * BANK:(h + 1) * BANK], ps[:],
                             col("gla_b_gate", c), -1.0, ALU.add, ALU.mult, after=[m]))
        softplus(tmp, cum, one, A, V, act, dve, V.last)
        for c in range(2):
            V(dve.tensor_tensor_scan, tmp[:, c, :], keep[:], cum[:, c, :], 0.0, ALU.mult, ALU.add)
        b_sum = tmp
        ends = b_sum[:].rearrange("p c (n t) -> p c n t", t=GC)[:, :, :, GC - 1]
        m = V(dve.tensor_tensor, k_dec[:].rearrange("p c (n t) -> p c n t", t=GC),
              b_sum[:].rearrange("p c (n t) -> p c n t", t=GC), spread(ends, 3, GC), ALU.subtract)
        A(act.activation, k_dec[:], k_dec[:], ACT.Exp, scale=1.0 / TAU, after=[m])
        A(act.activation, g_last[:], ends, ACT.Exp, scale=-1.0 / TAU)
        m = A(act.activation, cum[:], b_sum[:], ACT.Exp, scale=-1.0 / TAU)
        V(dve.tensor_tensor, g_qk[:, 0:2, :], g_qk[:, 0:2, :], cum[:], ALU.mult, after=[m])
        V(dve.tensor_tensor, k_dec[:], k_dec[:], g_qk[:, 2:4, :], ALU.mult)
        m = A(act.activation, cum[:], b_sum[:], ACT.Exp, scale=1.0 / TAU, after=[V.last])
        V(dve.tensor_tensor, g_qk[:, 2:4, :], g_qk[:, 2:4, :], cum[:], ALU.mult, after=[m])
        pr.barrier()

    def gls(name, shape):
        return sb(name, shape, where=gl)
    k_inv = gls("k_inv", [P, 4, P])
    kd_t = gls("kd_t", [P, 2, P])
    kd_tok = gls("kd_tok", [P, 2, 2, P])
    v_t = gls("v_t", [P, GLA_W])
    at_g = gls("at_g", [P, 4, P])
    sq_g = gls("sq_g", [P, 4, P])
    st_g = gls("st_g", [P, 4, P])
    gl_t = gls("gl_t", [P, 2, 2])
    chunk_mask = gls("chunk_mask", [P, P])
    G(pool.tensor_copy, chunk_mask[:], upper[:])
    G(pool.memset, chunk_mask[0:GC, GC:P], 0.0)
    for t in (k_inv, kd_tok, st_g):
        G(pool.memset, t[:], 0.0)
    pr.free.pop("sq", None)
    act.preload_act_table_set("natural_log_exp_and_others")
    with pr.repeat("gla", NT) as i:
        tok = bass.ds(i * P, P)
        m_k = None
        for hb in range(2):
            rows = slice(hb * GLA_K, (hb + 1) * GLA_K)
            m_k = G(pool.tensor_copy, k_inv[rows].rearrange("p (a b) t -> p a b t", b=2)[:, :, hb, :],
                    g_qk[rows, 2:4, tok], after=pr.free.get("k_inv", ()))
        m_kd = G(pool.tensor_copy, kd_t[:], k_dec[:, :, tok], after=pr.free.get("kd_t", ()))
        m_v = A(act.copy, v_t[:], g_v[:, bass.ds(i, 1), :].rearrange("p a b -> p (a b)"),
                after=pr.free.get("v_t", ()))
        m_gl = V(dve.tensor_copy, gl_t[:], g_last[:, :, bass.ds(i * 2, 2)])
        b0, ps = bank()
        PE.wait(m_k)
        for h in range(GLA_HEADS):
            m = te.matmul(ps[:, h * P:(h + 1) * P], k_inv[:, h, :], g_qk[:, h // 2, tok], start=True, stop=True)
        m = PE.done.inc(m)
        pr.free["k_inv"] = [m]
        m_at = V(dve.tensor_tensor, at_g[:], ps[:].rearrange("p (h c) -> p h c", h=4), spread(chunk_mask[:], 1, 4),
                 ALU.mult, after=[m, *pr.free.get("at_g", ())])
        emptied(b0, m_at)
        b0, ps = bank()
        PE.wait(m_kd)
        for p in range(2):
            m = te.transpose(ps[:, p * P:(p + 1) * P], kd_t[:, p, :], ident[:])
        m = PE.done.inc(m)
        pr.free["kd_t"] = [m]
        for c in range(2):
            rows = slice(c * GC, (c + 1) * GC)
            m_kt = A(act.copy, kd_tok[rows, c, :, :], ps[rows, 0:2 * P].rearrange("p (a b) -> p a b", a=2),
                     after=[m, *pr.free.get("kd_tok", ())])
        emptied(b0, m_kt)
        b0, ps = bank()
        PE.wait(m_at, m_v)
        for h in range(GLA_HEADS):
            te.matmul(ps[:, h * P:(h + 1) * P], v_t[:, h * P:(h + 1) * P], at_g[:, h, :], start=(h == 0), stop=False)
        for c in range(2):
            PE.wait(*pr.free.get("st_g", ()))
            for h in range(GLA_HEADS):
                m = te.matmul(ps[:, h * P + c * GC:h * P + (c + 1) * GC], st_g[:, h, :],
                              g_qk[:, h // 2, bass.ds(i * P + c * GC, GC)], start=False, stop=(h == 3 and c == 1))
            m_o = PE.done.inc(m)
            b1_, ps1 = bank()
            PE.wait(m_kt)
            for p in range(2):
                m = te.matmul(ps1[:, p * 2 * P:(p + 1) * 2 * P], kd_tok[:, c, p, :], v_t[:, p * 2 * P:(p + 1) * 2 * P],
                              start=True, stop=True)
            m = PE.done.inc(m)
            for h in range(GLA_HEADS):
                rows = slice((h % 2) * GLA_K, (h % 2 + 1) * GLA_K)
                V(dve.scalar_tensor_tensor, st_g[rows, h, :], st_g[rows, h, :], gl_t[rows, h // 2, c:c + 1],
                  ps1[rows, h * P:(h + 1) * P], ALU.mult, ALU.add, after=[m, m_o, m_gl], chain=True)
            emptied(b1_, V.last)
            pr.free["st_g"] = [V.last]
        pr.free["kd_tok"] = pr.free["v_t"] = [m]
        pr.free["at_g"] = [m_o]
        emptied(b0, rms_heads(ps, m_o, sq_g, mixed[:, 4:8, tok], col("gla_norm_g")))
    gl.close()
    dump("o_gla", mixed[:, 4:8, :])

    with ExitStack() as ph:
        gate = [sb(f"gate{n}", [P, BANK], where=ph) for n in range(2)]
        act.preload_act_table_set("silu_and_others")
        with pr.repeat("gates", 2) as i:
            def gate_done(c, h, ps, m):
                n = h % 2
                m = A(act.activation, gate[n][:], ps, ACT.Silu, after=[m, *pr.free.get(f"gate{n}", ())], chain=False)
                o = mixed[:, bass.ds(i * 4 + c, 1), h * BANK:(h + 1) * BANK].rearrange("p a b -> p (a b)")
                pr.free[f"gate{n}"] = [V(dve.tensor_tensor, o, o, gate[n][:], ALU.mult, after=[m], chain=False)]
                return m
            project(w_in, i * (O_GG - O_Z) + O_Z, 512, gate_done)
        dump("o_mix", mixed[:])

        project_tokens(lambda k, n: (mixed[:, k, n * P:(n + 1) * P],), 8, dram["w_o"][0], 0, 0, (0, 1), add_residual,
                       scale_row=gate_row[:, 0, :])
        pr.barrier()
    mixed_space.close()
    open_ft(2)

    layer_norm_features("norm1", ("ln1_g", "ln1_b"), 1)
    dump("x1", resid[:])

    with ExitStack() as ph:
        pre = [sb(f"ffn_in{n}", [P, 3 + T], where=ph) for n in range(2)]
        conv = [sb(f"ffn_conv{n}", [P, T], where=ph) for n in range(2)]
        hid = [[sb(f"ffn_hid{n}", [P, T], F32R, ph) for _ in range(2)] for n in range(2)]
        taps = sb("ffn_taps", [P, 2, NFF, 4], where=ph)
        tap_now = sb("ffn_tap_now", [P, 2, 2, 4], where=ph)
        V(dve.tensor_copy, taps[:, :, :, 0:3],
          col("ffn_conv", 0, 3 * 2 * NFF).rearrange("p (j g c) -> p g c j", j=3, g=2))
        V(dve.tensor_copy, taps[:, :, :, 3:4],
          col("ffn_conv_b", 0, 2 * NFF).rearrange("p (g c j) -> p g c j", g=2, j=1))
        for n in range(2):
            V(dve.memset, pre[n][:, 0:3], 0.0)
        w_up, w_down = dram["ffn_w_up"][0], dram["ffn_w_down"][0]

        gate_f = gate_row[:, 1, :]
        with halved_panels(3), pr.repeat("ffn", NFF // 2) as i:
            V(dve.tensor_copy, tap_now[:], taps[:, :, bass.ds(i * 2, 2), :])
            sources = [(u, g, rows_of(w_up, 0, D, (i * 2 + u) * P + g * FF, P)) for u in range(2) for g in range(2)]
            sources += [(h, 2, rows_of(w_down, i * 2 * P, 2 * P, h * BANK, BANK)) for h in range(2)]
            scale = [None] * 4 + [spread(gate_f[:, h * BANK:(h + 1) * BANK], 1, 2) for h in range(2)]
            hid_ready = {}
            for (u, g, _), wt in zip(sources, stream([x for _, _, x in sources], scale)):
                PE.wait(*wt.ready)
                if g < 2:
                    for h in range(HALVES):
                        hs = slice(h * BANK, (h + 1) * BANK)
                        b, ps = bank()
                        mm = PE.done.inc(products(ps[:], [(wt.at(k), ft_at(k, hs)) for k in range(KD)]))
                        m = A(act.activation, pre[g][:, 3 + h * BANK:3 + (h + 1) * BANK], ps[:], ACT.Copy,
                              after=[mm, *pr.free.get(f"pre{g}{h}", ())], chain=False)
                        emptied(b, m)
                        w = tap_now[:, g, u, :]
                        r = V(dve.tensor_scalar, conv[g][:, hs], pre[g][:, 1 + h * BANK:1 + (h + 1) * BANK], w[:, 0:1],
                              w[:, 3:4], ALU.mult, ALU.add, after=[m, *pr.free.get(f"fconv{g}{h}", ())])
                        for j in range(1, 3):
                            r = V(dve.scalar_tensor_tensor, conv[g][:, hs],
                                  pre[g][:, 1 + j + h * BANK:1 + j + (h + 1) * BANK], w[:, j:j + 1], conv[g][:, hs],
                                  ALU.mult, ALU.add)
                        pr.free[f"pre{g}{h}"] = [r]
                        if h:
                            pr.free[f"pre{g}0"] = [r]
                        if g == 0:
                            m_silu = A(act.activation, conv[0][:, hs], conv[0][:, hs], ACT.Silu, after=[r],
                                       chain=False)
                            pr.free[f"silu{h}"] = [m_silu]
                        else:
                            m = G(pool.tensor_tensor, conv[1][:, hs], conv[0][:, hs], conv[1][:, hs], ALU.mult,
                                  after=[r, *pr.free[f"silu{h}"]], chain=False)
                            pr.free[f"fconv0{h}"] = [m]
                            hi, lo = hid[u]
                            m = A(act.activation, hi[:, hs], conv[1][:, hs], ACT.Copy,
                                  after=[m, *pr.free.get("fhid", ())], chain=False)
                            m = G(pool.tensor_tensor, lo[:, hs], conv[1][:, hs], f32(hi[:, hs]), ALU.subtract,
                                  after=[m], chain=False)
                            pr.free[f"fconv1{h}"] = [m]
                            hid_ready[u, h] = m
                    wt.used(mm)
                else:
                    for n in range(NT):
                        b, ps = bank(*[hid_ready[j, n // (NT // 2)] for j in range(2)])
                        m = PE.done.inc(products(ps[:], [(tuple(x[:, n * P:(n + 1) * P] for x in hid[j]), wt.at(j))
                                                         for j in range(2)]))
                        emptied(b, add_residual(u, n, ps, m))
                    wt.used(m)
                    pr.free["fhid"] = [m]

    with norm_space(("ln2_g", "ln2_b")):
        moments_of("norm2_moments", resid)
        with pr.repeat("norm2", NT // 2) as i:
            for u in range(2):
                m = normed(resid, i * 2 + u, u, True)
                pr.free[f"xhat{u}"] = [affine(resid, i * 2 + u, u, m)[0]]
    open_ft(1)
    rms_norm_features("norm_mix", "norm_mix_g")
    dump("x2", resid[:])
    dump("xn", ft[0][:])


    w_in2 = dram["w_in_2"][0]
    O2_U = 3 * HEADS * HD
    mix2_space = ExitStack()
    mix2 = sb("mix2", [P, 8, T], where=mix2_space)

    with ExitStack() as ph:
        def rg(name, shape):
            return sb(name, shape, where=ph)
        gates_w = rg("gates_w", [P, 4, 4, P])
        gw_now = rg("gw_now", [P, 4, P])
        params = rg("params", [P, 4, 11])
        par = rg("par", [P, 11])
        npar = rg("npar", [P, 2])
        one = rg("one_col", [P, 1])
        lam = rg("lam", [P, 8])
        lam_sp = rg("lam_sp", [P, 8])
        pre = rg("u_in", [P, 3 + T])
        uc = rg("uc", [P, T])
        ra, ri, th, a_, h_f = (rg(n, [P, T]) for n in ("gate_a", "gate_x", "th", "a_coef", "h_fwd"))
        m = G(pool.memset, gates_w[:], 0.0)
        SP.wait(m)
        sig = loads("gates_w")
        for ty, w in enumerate((dram["rg_a_w_2"][0], dram["rg_x_w_2"][0])):
            for z in range(2):
                for g in range(2):
                    m_gw = sig.inc(nc.sync.dma_start(
                        gates_w[g * 64:(g + 1) * 64, :, ty * 2 + z, g * 64:(g + 1) * 64],
                        w[z].rearrange("(c g) i j -> g i c j", g=2)[g]))
        V(dve.memset, one[:], 1.0)
        V(dve.tensor_copy, params[:, :, 0:4], col("conv_w", 0, 16).rearrange("p (j c) -> p c j", c=4))
        V(dve.tensor_copy, params[:, :, 4:5], col("conv_b", 0, 4).rearrange("p (j c) -> p c j", c=4))
        V(dve.tensor_copy, params[:, :, 5:7], col("rg_a_b", 0, 8).rearrange("p (j c) -> p c j", c=4))
        V(dve.tensor_copy, params[:, :, 7:9], col("rg_x_b", 0, 8).rearrange("p (j c) -> p c j", c=4))
        V(dve.tensor_scalar, lam[:], col("rg_lambda", 0, 8), -1.0, None, ALU.mult)
        softplus(lam, lam_sp, one, A, V, act, dve, V.last)
        V(dve.tensor_scalar, params[:, :, 9:11], lam_sp[:].rearrange("p (j c) -> p c j", c=4), -8.0, None, ALU.mult)
        V(dve.memset, pre[:, 0:2], 0.0)
        V(dve.memset, pre[:, 2 + T:3 + T], 0.0)
        G.wait(m_gw)
        with pr.repeat("rglru", 4) as i:
            m_par = V(dve.tensor_copy, par[:], params[:, bass.ds(i, 1), :].rearrange("p a b -> p (a b)"))
            V(dve.tensor_scalar, npar[:], par[:, 9:11], -1.0, None, ALU.mult)
            m_par = V.last
            m_gwn = G(pool.tensor_copy, gw_now[:], gates_w[:, bass.ds(i, 1), :, :].rearrange("p a b c -> p (a b) c"),
                      after=pr.free.get("gw_now", ()))
            ug = stream([rows_of(w_in2, 0, D, i * P + (O2_U + g * 512), P) for g in range(2)])
            y = mix2[:, bass.ds(i + 4, 1), :].rearrange("p a b -> p (a b)")
            for g, wt in enumerate(ug):
                PE.wait(*wt.ready)
                for h in range(HALVES):
                    hs = slice(h * BANK, (h + 1) * BANK)
                    b, ps = bank()
                    mm = PE.done.inc(products(ps[:], [(wt.at(k), ft_at(k, hs)) for k in range(KD)]))
                    if h == HALVES - 1:
                        wt.used(mm)
                    if g == 0:
                        m = A(act.copy, pre[:, 2 + h * BANK:2 + (h + 1) * BANK], ps[:],
                              after=[mm, *(pr.free.get("u_in", ()) if h == 0 else ())])
                    else:
                        m = A(act.activation, mix2[:, bass.ds(i + 4, 1), hs].rearrange("p a b -> p (a b)"), ps[:],
                              ACT.Gelu_apprx_tanh, after=[mm])
                    emptied(b, m)
                if g == 0:
                    V.wait(m)
                    m_uc = causal_conv(pre, 0, lambda j: par[:, j:j + 1], 4, par[:, 4:5], [uc])
                    pr.free["u_in"] = [m_uc]
            m_y = m
            PE.wait(m_gwn, m_uc)
            for z in range(2):
                for ty, dst in ((0, ra), (1, ri)):
                    for h in range(HALVES):
                        hs = slice(h * BANK, (h + 1) * BANK)
                        b, ps = bank()
                        mm = PE(te.matmul, ps[:], gw_now[:, ty * 2 + z, :], uc[:, hs], start=True, stop=True)
                        m = A(act.activation, dst[:, hs], ps[:], ACT.Sigmoid,
                              bias=par[:, 5 + ty * 2 + z:6 + ty * 2 + z],
                              after=[mm, m_par, *pr.free.get(f"rg{ty}", ())])
                        emptied(b, m)
                m_i = m
                m_t = A(act.activation, th[:], ra[:], ACT.Tanh, scale=npar[:, z:z + 1], after=pr.free.get("th", ()))
                m_a = A(act.activation, a_[:], ra[:], ACT.Exp, scale=par[:, 9 + z:10 + z])
                V(dve.tensor_tensor, ri[:], ri[:], uc[:], ALU.mult, after=[m_i])
                V(dve.tensor_scalar, ra[:], th[:], 1.0, None, ALU.add, after=[m_a])
                V(dve.reciprocal, ra[:], ra[:])
                m = V(dve.scalar_tensor_tensor, th[:], th[:], 2.0, ra[:], ALU.mult, ALU.mult)
                pr.free["rg0"] = [m]
                m = A(act.activation, th[:], th[:], ACT.Sqrt, after=[m])
                V(dve.tensor_tensor, th[:], th[:], ri[:], ALU.mult, after=[m])
                pr.free["rg1"] = [V.last]
                if z == 0:
                    V(dve.tensor_tensor_scan, h_f[:], a_[:], th[:], 0.0, ALU.mult, ALU.add)
                else:
                    V(dve.tensor_tensor_scan, ri[:, ::-1], a_[:, ::-1], th[:, ::-1], 0.0, ALU.mult, ALU.add)
                pr.free["th"] = [V.last]
            V(dve.tensor_tensor, h_f[:], h_f[:], ri[:], ALU.add)
            V(dve.tensor_tensor, y, y, h_f[:], ALU.mult, after=[m_y])
            pr.free["rg1"] = [V.last]
            pr.free["gw_now"] = [mm]
    dump("rec", mix2[:, 4:8, :])

    at_space = ExitStack()
    k_feat = sb("k_feat", [P, 4, T], where=at_space)
    v_tok = sb("v_tok", [P, NT, 512], where=at_space)
    with ExitStack() as ph:
        inv_freq = sb("inv_freq", [P, 1], where=ph)
        pos_i = sb("pos_i", [P, T], I32, where=ph)
        ang, cos, sin, turns = (sb(n, [P, T], where=ph) for n in ("ang", "cos", "sin", "turns"))
        t_cos = [sb(f"t_cos{n}", [P, BANK], where=ph) for n in range(2)]
        t_sin = [sb(f"t_sin{n}", [P, BANK], where=ph) for n in range(2)]
        turns_i = pos_i
        SP.wait(Mark(V.done, V.done.count, None), Mark(A.done, A.done.count, None), Mark(PE.done, PE.done.count, None))
        sig = loads("positions")
        sig.inc(nc.sync.dma_start(inv_freq[:], dram["inv_freq"]))
        m = sig.inc(nc.sync.dma_start(pos_i[:], dram["positions_2"][0].partition_broadcast(P)))
        V(dve.tensor_copy, ang[:], pos_i[:], after=[m])
        V(dve.tensor_scalar, ang[:], ang[:], inv_freq[:], None, ALU.mult)
        act.preload_act_table_set("silu_and_others")
        C1 = 6.28125
        C2 = float.fromhex("0x1.fb4p-10")
        C3 = 2 * math.pi - C1 - C2
        for out, quarter in ((sin, 0.0), (cos, 0.25)):
            V(dve.tensor_scalar, turns[:], ang[:], 1.0 / (2 * math.pi), quarter, ALU.mult, ALU.add)
            V(dve.tensor_copy, turns_i[:], turns[:])
            V(dve.tensor_copy, turns[:], turns_i[:])
            V(dve.scalar_tensor_tensor, out[:], turns[:], -C1, ang[:], ALU.mult, ALU.add)
            V(dve.scalar_tensor_tensor, out[:], turns[:], -C2, out[:], ALU.mult, ALU.add)
            V(dve.scalar_tensor_tensor, out[:], turns[:], -C3, out[:], ALU.mult, ALU.add)
            V(dve.tensor_scalar, out[:], out[:], quarter * 2 * math.pi, math.pi, ALU.add, ALU.min)
            m = V(dve.tensor_scalar, out[:], out[:], -math.pi, None, ALU.max)
            A(act.activation, out[:], out[:], ACT.Sin, after=[m])
        for q in (0, 2):
            V(dve.tensor_scalar, sin[32 * q:32 * q + 32, :], sin[32 * q:32 * q + 32, :], -1.0, None, ALU.mult,
              after=[A.last])
        V.wait(A.last, V.last)

        def rope_into(dst):
            def done(c, h, ps, m):
                n = h % 2
                hs = slice(h * BANK, (h + 1) * BANK)
                V(dve.tensor_tensor, t_cos[n][:], ps, cos[:, hs], ALU.mult, after=[m, *pr.free.get(f"rope{n}", ())],
                  chain=False)
                for q in range(4):
                    o, i_ = 32 * q, 32 * (q ^ 1)
                    e = V(dve.tensor_tensor, t_sin[n][o:o + 32, :], ps[i_:i_ + 32, :], sin[o:o + 32, hs], ALU.mult,
                          chain=False)
                pr.free[f"rope{n}"] = [G(pool.tensor_tensor, dst[:, c, hs], t_cos[n][:], t_sin[n][:], ALU.add,
                                         after=[e])]
                return e
            return done
        project(w_in2, 0, 512, rope_into(mix2))
        project(w_in2, 512, 512, rope_into(k_feat))
        pr.barrier()
    project_tokens(lambda k, n: ft_at(k, slice(n * P, (n + 1) * P)), KD, w_in2, 0, 2 * 512, (0,),
                   lambda h, n, ps, m: V(dve.tensor_copy, v_tok[:, n, :], ps[:], after=[m], chain=False))
    dump("rq", mix2[:, 0:4, :])
    dump("rk", k_feat[:])
    pr.barrier()

    SPAN = 2 * T - P
    ln_count = sb("ln_count", [P, SPAN], where=at_space)
    with ExitStack() as ph:
        dist, rem, d2, in4 = (ft[0][:].rearrange("p a b -> p (a b)")[:, n * SPAN:(n + 1) * SPAN] for n in range(4))
        dist, rem = dist.bitcast(I32), rem.bitcast(I32)
        in16 = ln_count
        G(pool.iota, dist, pattern=[[1, SPAN]], base=-(T - P), channel_multiplier=-1)
        V(dve.tensor_copy, d2, dist, after=[G.last])
        V(dve.tensor_tensor, d2, d2, d2, ALU.mult)
        for mask, dil in ((in4, 4), (in16[:], 16)):
            V(dve.tensor_scalar, rem, dist, dil - 1, None, ALU.bitwise_and)
            V(dve.tensor_copy, mask, rem)
            V(dve.tensor_scalar, mask, mask, 0.0, None, ALU.is_equal)
            V(dve.scalar_tensor_tensor, mask, d2, float((RADIUS * dil) ** 2), mask, ALU.is_le, ALU.mult)
        V(dve.scalar_tensor_tensor, in4, d2, float(RADIUS ** 2), in4, ALU.is_le, ALU.add)
        V(dve.tensor_tensor, in4, in4, in16[:], ALU.add)
        m = V(dve.tensor_scalar, in16[:], in4, 1.0, None, ALU.max)
        A(act.activation, in16[:], in16[:], ACT.Ln, after=[m])
        V(dve.tensor_scalar, in4, in4, 1.0, -1.0, ALU.min, ALU.add)
        V(dve.scalar_tensor_tensor, ln_count[:], in4, 1e30, in16[:], ALU.mult, ALU.add, after=[A.last])
        pr.barrier()

    q_now = [sb(f"q_now{n}", [P, T], where=at_space) for n in range(2)]
    k_now = [sb(f"k_now{n}", [P, T], where=at_space) for n in range(2)]
    v_now = [sb(f"v_now{n}", [P, NT, P], where=at_space) for n in range(2)]
    scores = [sb(f"scores{n}", [P, T], where=at_space) for n in range(AHEAD + 1)]
    row_stat = sb("row_stat", [P, AHEAD + 1, 4], where=at_space)
    p_t = ft[0][:].rearrange("p a (b c) -> p a b c", b=2)

    def exp_rows(s, n_keys, st, after):
        V(dve.tensor_reduce, st[:, 0:1], s[:, 0:n_keys], AX, ALU.max, after=after)
        m = V(dve.tensor_scalar, st[:, 1:2], st[:, 0:1], -1.0, None, ALU.mult)
        return A(act.activation, s[:, 0:n_keys], s[:, 0:n_keys], ACT.Exp, bias=st[:, 1:2], accum_out=st[:, 2:3],
                 after=[m], chain=False)

    def norm_rows_of(s, n_keys, st, after):
        m = V(dve.reciprocal, st[:, 3:4], st[:, 2:3], after=after)
        return A(act.activation, s[:, 0:n_keys], s[:, 0:n_keys], ACT.Copy, scale=st[:, 3:4], after=[m], chain=False)

    act.preload_act_table_set("natural_log_exp_and_others")
    with pr.repeat("dilated", HEADS // 4) as i:
        ready, transposed, now_ready = {}, {}, {}
        for pair in range(2):
            G(pool.tensor_copy, q_now[pair][:], mix2[:, bass.ds(i * 2 + pair, 1), :].rearrange("p a b -> p (a b)"),
              after=pr.free.get(f"q_now{pair}", ()))
            G(pool.tensor_copy, k_now[pair][:], k_feat[:, bass.ds(i * 2 + pair, 1), :].rearrange("p a b -> p (a b)"))
            now_ready[pair] = G(pool.tensor_copy, v_now[pair][:], v_tok[:, :, bass.ds((i * 2 + pair) * P, P)],
                                after=pr.free.get(f"v_now{pair}", ()))

        def place(u):
            pair, half, tile, hb = u // 16, u // 8 % 2, u % 8 // 2, u % 2
            return pair, half, tile, hb, slice(hb * HD, (hb + 1) * HD), u % (AHEAD + 1)

        def score(u):
            pair, half, tile, hb, rows, slot = place(u)
            n = half * 4 + tile
            st, s = row_stat[:, slot, :], scores[slot]
            for h in range(2):
                b, ps = bank(now_ready[pair])
                m = PE(te.matmul, ps[:], q_now[pair][rows, n * P:(n + 1) * P],
                       k_now[pair][rows, h * BANK:(h + 1) * BANK], start=True, stop=True)
                x0 = T - P - n * P + h * BANK
                e = V(dve.scalar_tensor_tensor, s[:, h * BANK:(h + 1) * BANK], ps[:], HD ** -0.5,
                      ln_count[:, x0:x0 + BANK], ALU.mult, ALU.add,
                      after=[m, *pr.free.get(f"scores{slot}", ())], chain=False)
                emptied(b, e)
            pr.free[f"q_now{pair}"] = [m]
            ready[u] = exp_rows(s, T, st, [e])

        def finish(u):
            slot = place(u)[-1]
            ready[u] = norm_rows_of(scores[slot], T, row_stat[:, slot, :], [ready[u]])

        def turn_weights(u):
            pair, half, tile, hb, rows, slot = place(u)
            s = scores[slot]
            for h in range(2):
                b, ps = bank(ready[u])
                for k in range(4):
                    m = te.transpose(ps[:, k * P:(k + 1) * P], s[:, (4 * h + k) * P:(4 * h + k + 1) * P], ident[:])
                m = PE.done.inc(m)
                o = p_t[:, 4 * h:4 * h + 4, hb, tile * P:(tile + 1) * P]
                src = ps[:].rearrange("p (a b) -> p a b", a=4)
                if h == 0:
                    e0 = A(act.copy, o, src, after=[m, *pr.free.get("p_t", ())], chain=False)
                    emptied(b, e0)
                else:
                    e1 = V(dve.tensor_copy, o, src, after=[m, *pr.free.get("p_t", ())], chain=False)
                    emptied(b, e1)
            pr.free[f"scores{slot}"] = [m]
            transposed[u] = [e0, e1]

        def weigh(first):
            pair, half = place(first)[:2]
            b, ps = bank(*[m for u in range(first, first + 8) for m in transposed[u]])
            for hb in range(2):
                for k in range(NT):
                    m = te.matmul(ps[hb * HD:(hb + 1) * HD, :], v_now[pair][:, k, hb * HD:(hb + 1) * HD],
                                  p_t[:, k, hb, :], start=(k == 0), stop=(k == NT - 1))
            m = PE.done.inc(m)
            pr.free["p_t"] = pr.free[f"v_now{pair}"] = [m]
            emptied(b, A(act.copy, mix2[:, bass.ds(i * 2 + pair, 1), half * BANK:(half + 1) * BANK].rearrange(
                "p a b -> p (a b)"), ps[:], after=[m], chain=False))

        UNITS = 32
        for u in range(AHEAD):
            score(u)
        finish(0)
        for u in range(UNITS):
            if u < UNITS - AHEAD:
                score(u + AHEAD)
            if u < UNITS - 1:
                finish(u + 1)
            if u and u % 8 == 0:
                weigh(u - 8)
            turn_weights(u)
        weigh(UNITS - 8)
    at_space.close()
    dump("attn", mix2[:, 0:4, :])

    project_tokens(lambda k, n: (mix2[:, k, n * P:(n + 1) * P],), 8, dram["w_out_2"][0], 0, 0, (0, 1), add_residual)
    dump("x3", resid[:])

    rms_norm_features("norm_cross", "norm_cross_g")
    with ExitStack() as ph:
        k_mem = sb("k_mem", [P, CROSS, MEM], where=ph)
        v_mem = sb("v_mem", [P, MEM // P, 512], where=ph)
        mem_ft = sb("mem_ft", [P, KD, MEM], where=ph)
        with norm_space() as nph:
            mem_t = sb("mem_t", [P, MEM // P, D], where=nph)
            SP.wait(Mark(V.done, V.done.count, None), Mark(A.done, A.done.count, None),
                    Mark(PE.done, PE.done.count, None))
            m_mem = loads("mem").inc(nc.sync.dma_start(mem_t[:], dram["mem_2"][0].rearrange("(n p) d -> p n d", p=P)))
            A.wait(m_mem)
            squares_of(None, mem_t, MEM // P)
            for n in range(MEM // P):
                V.wait(A.last)
                m = normed(mem_t, n, n, False)
                to_features(xhat[n], [mem_ft], n * P, P, lambda k: col("norm_mem_g", k), None, [m], f"xhat{n}")
        for c, wt in enumerate(stream([rows_of(dram["w_ck_2"][0], 0, D, c * P, P) for c in range(CROSS)])):
            PE.wait(*wt.ready)
            b, ps = bank()
            m = PE.done.inc(products(ps[:, 0:MEM], [(wt.at(k), (mem_ft[:, k, :],)) for k in range(KD)]))
            wt.used(m)
            emptied(b, A(act.copy, k_mem[:, c, :], ps[:, 0:MEM], after=[m], chain=False))
        project_tokens(lambda k, n: (mem_ft[:, k, n * P:(n + 1) * P],), KD, dram["w_cv_2"][0], 0, 0, (0,),
                       lambda h, n, ps, m: V(dve.tensor_copy, v_mem[:, n, :], ps[:], after=[m], chain=False),
                       n_tiles=MEM // P)

        def q_done(c, h, ps, m):
            return A(act.copy, mix2[:, c, h * BANK:(h + 1) * BANK], ps, after=[m], chain=False)
        project(dram["w_cq_2"][0], 0, 512, q_done)

        q_h = sb("q_h", [P, T], where=ph)
        k_h = sb("k_h", [P, MEM], where=ph)
        v_h = sb("v_h", [P, MEM // P, P], where=ph)
        scores = [sb(f"c_scores{n}", [P, MEM], where=ph) for n in range(3)]
        row_stat = sb("c_row_stat", [P, 3, 4], where=ph)
        p_tc = sb("p_tc", [P, MEM // P, BANK], where=ph)
        with pr.repeat("cross", CROSS) as i:
            m_q = A(act.copy, q_h[:], mix2[:, bass.ds(i, 1), :].rearrange("p a b -> p (a b)"),
                    after=pr.free.get("q_h", ()))
            G(pool.tensor_copy, k_h[:], k_mem[:, bass.ds(i, 1), :].rearrange("p a b -> p (a b)"),
              after=pr.free.get("q_h", ()))
            m_kv = G(pool.tensor_copy, v_h[:], v_mem[:, :, bass.ds(i * P, P)])
            ready, transposed = {}, {}

            def c_score(n):
                s = scores[n % 3]
                b, ps = bank()
                m = PE(te.matmul, ps[:, 0:MEM], q_h[:, n * P:(n + 1) * P], k_h[:], start=True, stop=True,
                       after=[m_q, m_kv])
                m = A(act.mul, s[:], ps[:, 0:MEM], float(P) ** -0.5,
                      after=[m, *pr.free.get(f"c_scores{n % 3}", ())])
                emptied(b, m)
                ready[n] = exp_rows(s, MEM, row_stat[:, n % 3, :], [m])

            def c_finish(n):
                ready[n] = norm_rows_of(scores[n % 3], MEM, row_stat[:, n % 3, :], [ready[n]])

            def c_turn(n):
                b, ps = bank()
                PE.wait(ready[n])
                for k in range(2):
                    m = te.transpose(ps[:, k * P:(k + 1) * P], scores[n % 3][:, k * P:(k + 1) * P], ident[:])
                m = PE.done.inc(m)
                pr.free[f"c_scores{n % 3}"] = [m]
                e = V(dve.tensor_copy, p_tc[:, :, (n % 4) * P:(n % 4 + 1) * P],
                      ps[:, 0:2 * P].rearrange("p (a b) -> p a b", a=2), after=[m, *pr.free.get("p_tc", ())],
                      chain=False)
                emptied(b, e)
                transposed[n] = e

            def c_weigh(half):
                b, ps = bank()
                PE.wait(*[transposed[half * 4 + n] for n in range(4)])
                for k in range(2):
                    m = te.matmul(ps[:], v_h[:, k, :], p_tc[:, k, :], start=(k == 0), stop=(k == 1))
                m = PE.done.inc(m)
                pr.free["p_tc"] = [m]
                emptied(b, V(dve.tensor_scalar,
                             mix2[:, bass.ds(i, 1), half * BANK:(half + 1) * BANK].rearrange("p a b -> p (a b)"),
                             ps[:], 1.0, None, ALU.mult, after=[m], chain=False))
                pr.free["q_h"] = [m]

            c_score(0)
            c_score(1)
            c_finish(0)
            for n in range(NT):
                if n < NT - 2:
                    c_score(n + 2)
                if n < NT - 1:
                    c_finish(n + 1)
                c_turn(n)
                if n == 3:
                    c_weigh(0)
            c_weigh(1)
        project_tokens(lambda k, n: (mix2[:, k, n * P:(n + 1) * P],), 4, dram["w_co_2"][0], 0, 0, (0, 1), add_residual)
        pr.barrier()
    dump("x4", resid[:])

    mix2_space.close()
    open_ft(2)
    rms_norm_features("norm_mlp", "norm_mlp_g")
    w_mi, w_mo = dram["w_mlp_in_2"][0], dram["w_mlp_out_2"][0]
    with ExitStack() as ph:
        hid = [[sb(f"mlp_hid{n}", [P, T], F32R, ph) for _ in range(2)] for n in range(4)]
        act_tmp = [sb(f"mlp_act{n}", [P, BANK], where=ph) for n in range(2)]
        sq_tmp = [sb(f"mlp_square{n}", [P, BANK], where=ph) for n in range(2)]
        with halved_panels(3), pr.repeat("mlp", NFF2 // 4) as i:
            sources = [(c, rows_of(w_mi, 0, D, i * 4 * P + c * P, P)) for c in range(4)]
            sources += [(4 + u * 2 + h, rows_of(w_mo, i * 4 * P + u * 2 * P, 2 * P, h * BANK, BANK))
                        for u in range(2) for h in range(2)]
            hid_ready = {}
            for (c, _), wt in zip(sources, stream([x for _, x in sources])):
                PE.wait(*wt.ready)
                if c < 4:
                    hi, lo = hid[c]
                    for h in range(HALVES):
                        hs = slice(h * BANK, (h + 1) * BANK)
                        b, ps = bank()
                        mm = PE.done.inc(products(ps[:], [(wt.at(k), ft_at(k, hs)) for k in range(KD)]))
                        m = A(act.activation, act_tmp[h][:], ps[:], ACT.Relu,
                              after=[mm, *pr.free.get(f"act_tmp{h}", ())], chain=False)
                        emptied(b, m)
                        m = V(dve.tensor_tensor, sq_tmp[h][:], act_tmp[h][:], act_tmp[h][:], ALU.mult,
                              after=[m, *pr.free.get(f"sq_tmp{h}", ())], chain=False)
                        pr.free[f"act_tmp{h}"] = [m]
                        m = A(act.activation, hi[:, hs], sq_tmp[h][:], ACT.Copy,
                              after=[m, *pr.free.get(f"mhid{c // 2}", ())], chain=False)
                        m = V(dve.tensor_tensor, lo[:, hs], sq_tmp[h][:], f32(hi[:, hs]), ALU.subtract, after=[m],
                              chain=False)
                        pr.free[f"sq_tmp{h}"] = [m]
                    wt.used(mm)
                    hid_ready[c] = m
                else:
                    u, h = divmod(c - 4, 2)
                    PE.wait(hid_ready[2 * u], hid_ready[2 * u + 1])
                    for n in range(NT):
                        b, ps = bank()
                        m = PE.done.inc(products(ps[:], [(tuple(x[:, n * P:(n + 1) * P] for x in hid[2 * u + j]),
                                                          wt.at(j)) for j in range(2)]))
                        emptied(b, add_residual(h, n, ps, m))
                    wt.used(m)
                    pr.free[f"mhid{u}"] = [m]

    pr.barrier()
    ft_space.close()

    with norm_space(("norm_final_g_2",)) as nph:
        out_t = [sb(f"out_t{n}", [P, D], where=nph) for n in range(2)]
        stored = [Counter(pr, f"out{n}_stored", 16) for n in range(2)]
        squares_of("final_squares", resid)
        dst = dram["out"][0].rearrange("(n p) d -> n p d", p=P)
        with pr.repeat("final", NT // 2) as i:
            for n in range(2):
                normed(resid, i * 2 + n, n, False)
                m = V(dve.tensor_tensor, out_t[n][:], xhat[n][:], norm_rows[:, 0, :], ALU.mult,
                      after=pr.free.get(f"out_t{n}", ()))
                pr.free[f"xhat{n}"] = [m]
                SP.wait(m)
                pr.free[f"out_t{n}"] = [stored[n].inc(nc.sync.dma_start(
                    dst[bass.ds(i * 2 + n, 1)].rearrange("a p d -> p (a d)"), out_t[n][:]))]
        for s in stored:
            SP.wait(Mark(s, s.count, None))


def rotary_frequencies(np):
    half = HD // 2
    freq = np.float32(10000.0) ** (-np.arange(half, dtype=np.float32) / np.float32(half))
    return np.tile(freq.astype(np.float32), P // half)[:, None]


def kernel(**inputs):
    import numpy as np
    import concourse.bacc as bacc
    from concourse.bass_utils import run_bass_kernel_spmd

    arrays = {f"in_{name}": np.ascontiguousarray(a) for name, a in inputs.items()}
    arrays["in_inv_freq"] = rotary_frequencies(np)

    def declare(nc):
        dram = {name[3:]: nc.dram_tensor(name, a.shape, mybir.dt.from_np(a.dtype), kind="ExternalInput").ap()
                for name, a in arrays.items()}
        dram["out"] = nc.dram_tensor("out", (1, T, D), F32, kind="ExternalOutput").ap()
        return dram

    def fresh():
        return bacc.Bacc("TRN2", target_bir_lowering=False, num_devices=1)

    counting = fresh()
    plan = build(counting, declare(counting), {})
    nc = fresh()
    assert build(nc, declare(nc), plan) == plan
    r = run_bass_kernel_spmd(nc, [arrays], core_ids=[0])
    return r.results[0]["out"]
```

```python
import math
from contextlib import ExitStack, contextmanager

import concourse.bass as bass
from concourse import mybir

F32 = mybir.dt.float32
F32R = mybir.dt.float32r
I32 = mybir.dt.int32
ALU = mybir.AluOpType
ACT = mybir.ActivationFunctionType
AX = mybir.AxisListType.X

P = 128
BANK = 512
D = 1024
KD = D // P
T = 1024
NT = T // P
HALVES = T // BANK
EPS = 1e-6
ALPHA = 2.0 ** 0.25
DN_HEADS, GLA_HEADS = 4, 4
DN_W, GLA_W, GLA_K = 512, 512, 64
O_Q, O_K, O_V, O_Z, O_A = 0, 512, 1024, 1536, 2048
O_GQ, O_GK, O_GV, O_GG, O_GR = 2056, 2312, 2568, 3080, 3592
RANK = 16
TAU = 16.0
GC = 64
NGC = T // GC
FF = 2816
NFF = FF // P
HEADS, HD = 8, 64
RADIUS = 64
MEM = 256
CROSS = 4
FF2 = 4096
NFF2 = FF2 // P
PANEL = 1024
SLOTS = 6
AHEAD = 2
DELTA_LAG = 2


class Mark:

    def __init__(self, counter, count, loop, back=0):
        self.counter, self.count, self.loop, self.back = counter, count, loop, back

    def value(self, program):
        if self.loop is None:
            return self.count * self.counter.step
        per = self.loop.per(self.counter)
        if program.loop is self.loop:
            assert self.count >= self.back * per, "a first iteration would wait for a count below zero"
            return program.loop.i * (per * self.counter.step) + (self.count - self.back * per) * self.counter.step
        return (self.count + (self.loop.n - 1) * per) * self.counter.step


class Counter:
    def __init__(self, program, name, step=1):
        self.sem = program.stack.enter_context(program.nc.semaphore(name))
        self.program, self.name, self.step, self.count = program, name, step, 0
        program.counters.append(self)

    def inc(self, ins):
        ins.then_inc(self.sem, self.step)
        self.count += 1
        return Mark(self, self.count, self.program.loop)


class Queue:

    def __init__(self, program, engine, name, chain):
        self.program, self.engine, self.name, self.chain, self.last = program, engine, name, chain, None
        self.done = Counter(program, f"{name}_done")
        self.passed = {}

    def wait(self, *marks):
        need = {}
        for m in marks:
            here = m.loop is not None and m.loop is self.program.loop
            order = (1, -m.back, m.count) if here else (0, 0, m.value(self.program))
            if m.counter.name not in need or need[m.counter.name][0] < order:
                need[m.counter.name] = (order, m)
        need = {name: m for name, (_, m) in need.items()}
        for m in need.values():
            v = m.value(self.program)
            if self.program.loop is None:
                if self.passed.get(m.counter.name, 0) >= v:
                    continue
                self.passed[m.counter.name] = v
            self.engine.wait_ge(m.counter.sem, v)

    def __call__(self, f, *args, after=(), chain=None, **kw):
        own = [self.last] if (self.chain if chain is None else chain) and self.last is not None else []
        self.wait(*after, *own)
        self.last = self.done.inc(f(*args, **kw))
        return self.last


class Loop:
    def __init__(self, program, name, n, i):
        self.program, self.name, self.n, self.i = program, name, n, i
        self.start = {s.name: s.count for s in program.counters}

    def per(self, signal):
        return self.program.plan.get(self.name, {}).get("per", {}).get(signal.name, 0)


class Program:

    def __init__(self, nc, plan, stack):
        self.nc, self.plan, self.stack = nc, plan, stack
        self.counters, self.loop, self.free, self.new_plan = [], None, {}, {}
        self.pe = Queue(self, nc.tensor, "pe", False)
        self.v = Queue(self, nc.vector, "dve", True)
        self.a = Queue(self, nc.scalar, "act", True)
        self.g = Queue(self, nc.gpsimd, "pool", True)
        self.sp = Queue(self, nc.sync, "sp", False)
        self.engines = [self.pe, self.v, self.a, self.g]

    def barrier(self):
        marks = [Mark(q.done, q.done.count, None) for q in self.engines if q.done.count]
        for q in self.engines:
            q.wait(*marks)
            q.last = None

    @contextmanager
    def repeat(self, name, n):
        self.barrier()
        carried = self.plan.get(name, {}).get("free", {})
        for key in carried:
            if key.startswith("slot"):
                self.sp.wait(*self.free.get(key, ()))
        before = dict(self.free)
        with self.nc.Fori(0, n) as i:
            loop = Loop(self, name, n, i)
            self.loop = loop
            by_name = {s.name: s for s in self.counters}
            for key, marks in carried.items():
                self.free[key] = [Mark(by_name[s], loop.start[s] + k, loop, 1) for s, k in marks]
            for q in self.engines:
                q.last = self.free.get(f"last_{q.name}", [None])[0]
            yield i
            for q in self.engines:
                if q.last is not None:
                    self.free[f"last_{q.name}"] = [q.last]
            per = {s.name: s.count - loop.start.get(s.name, 0) for s in self.counters}
            free = {key: [(m.counter.name, m.count - loop.start[m.counter.name]) for m in marks]
                    for key, marks in self.free.items()
                    if any(m.loop is loop and not m.back for m in marks) and marks is not before.get(key)}
            self.new_plan[name] = {"per": per, "free": free}
            self.loop = None
        for s in self.counters:
            if s.name in loop.start:
                s.count = loop.start[s.name] + n * per[s.name]
        for q in self.engines + [self.sp]:
            q.passed = {}
            q.last = None
        self.barrier()


def build(nc, dram, plan):
    with ExitStack() as stack:
        program = Program(nc, plan, stack)
        emit(nc, program, stack, dram)
        return program.new_plan


def softplus(x, out, one, A, V, act, dve, after):
    V(dve.tensor_scalar, out[:], x[:], 0.0, None, ALU.max)
    m = V(dve.scalar_tensor_tensor, x[:], out[:], -2.0, x[:], ALU.mult, ALU.add)
    A(act.activation, x[:], x[:], ACT.Exp, after=[m])
    m = A(act.activation, x[:], x[:], ACT.Ln, bias=one[:], scale=1.0)
    return V(dve.tensor_tensor, out[:], out[:], x[:], ALU.add, after=[m])


def emit(nc, pr, stack, dram):
    PE, V, A, G, SP = pr.pe, pr.v, pr.a, pr.g, pr.sp
    te, dve, act, pool = nc.tensor, nc.vector, nc.scalar, nc.gpsimd

    times = {}

    def sb(name, shape, dt=F32, where=None):
        times[name] = times.get(name, 0) + 1
        name = name if times[name] == 1 else f"{name}_{times[name]}"
        return (where or stack).enter_context(nc.sbuf_tensor(name, shape, dt))

    def spread(ap, axis, n):
        a = ap.unsqueeze(axis)
        shape = list(a.shape)
        shape[axis] = n
        return a.broadcast_to(shape)

    def loads(name):
        return Counter(pr, f"{name}_loaded", 16)

    vectors_loaded = loads("vectors")

    banks = [stack.enter_context(nc.psum_tensor(f"bank{n}", [P, BANK], F32)) for n in range(8)]
    turn = [0]
    in_use = set()

    def bank(*after):
        while turn[0] % 8 in in_use:
            turn[0] += 1
        n = turn[0] % 8
        turn[0] += 1
        in_use.add(n)
        PE.wait(*pr.free.get(f"bank{n}", ()), *after)
        return n, banks[n]

    def emptied(n, *marks):
        in_use.discard(n)
        pr.free[f"bank{n}"] = list(marks)

    panels = [sb(f"panel{n}", [P, PANEL]) for n in range(SLOTS)]
    arrived = [Counter(pr, f"panel{n}_arrived", 16) for n in range(SLOTS)]
    slot_turn = [0]

    def load_panel(src):
        n = slot_turn[0] % SLOTS
        slot_turn[0] += 1
        SP.wait(*pr.free.get(f"slot{n}", ()))
        view = panels[n][:, 0:src.shape[1] * src.shape[2]].rearrange("p (a b) -> p a b", a=src.shape[1])
        return n, view, arrived[n].inc(nc.sync.dma_start(view, src))

    halved = []
    halved_turn = [0]

    @contextmanager
    def halved_panels(count):
        with ExitStack() as ph:
            halved.extend((sb("panel_hi", [P, PANEL], F32R, ph), sb("panel_lo", [P, PANEL], F32R, ph))
                          for _ in range(count))
            halved_turn[0] = 0
            yield
            pr.barrier()
            halved.clear()

    def f32(view):
        return view.bitcast(F32)

    class Weights:

        def __init__(self, src, scale_row=None):
            n, view, m = load_panel(src)
            if scale_row is not None:
                m = G(pool.tensor_tensor, view, view, scale_row, ALU.mult, after=[m], chain=False)
            if not halved:
                self.parts, self.ready, self.key = (view,), [m], f"slot{n}"
                return
            t = halved_turn[0] % len(halved)
            halved_turn[0] += 1
            words = view.shape[1] * view.shape[2]
            hi, lo = (x[:, 0:words].rearrange("p (a b) -> p a b", a=view.shape[1]) for x in halved[t])
            self.key = f"halved{t}"
            m = A(act.activation, hi, view, ACT.Copy, after=[m, *pr.free.get(self.key, ())], chain=False)
            m = G(pool.tensor_tensor, lo, view, f32(hi), ALU.subtract, after=[m], chain=False)
            pr.free[f"slot{n}"] = [m]
            self.parts, self.ready = (hi, lo), [m]

        def at(self, k, c=slice(None)):
            return tuple(x[:, k, c] for x in self.parts)

        def used(self, mark):
            pr.free[self.key] = [mark]

    def stream(sources, scale_row=None):
        ahead = None
        for n, src in enumerate(sources):
            new = Weights(src, scale_row[n] if scale_row else None)
            if ahead is not None:
                yield ahead
            ahead = new
        yield ahead

    def products(ps, steps, start=True, stop=True):
        for n, (lhs, rhs) in enumerate(steps):
            pairs = [(lhs[0], rhs[0])] + ([(lhs[0], rhs[1]), (lhs[1], rhs[0])] if len(lhs) > 1 else [])
            for j, (a, b) in enumerate(pairs):
                m = te.matmul(ps, a, b, start=(start and n == 0 and j == 0),
                              stop=(stop and n == len(steps) - 1 and j == len(pairs) - 1))
        return m

    def rows_of(w, r0, nr, c0, ncol):
        return w[bass.ds(r0, nr) if not isinstance(r0, int) else slice(r0, r0 + nr),
                 bass.ds(c0, ncol) if not isinstance(c0, int) else slice(c0, c0 + ncol)].rearrange(
                     "(k p) c -> p k c", p=P)

    ident = sb("ident", [P, P])
    ones = sb("ones", [P, P])
    upper = sb("upper", [P, P])
    m_ones = G(pool.memset, ones[:], 1.0)
    G(pool.affine_select, out=ident[:], in_=ones[:], compare_op=ALU.is_equal, fill=0.0, base=0,
      pattern=[[-1, P]], channel_multiplier=1)
    G(pool.affine_select, out=upper[:], in_=ones[:], compare_op=ALU.is_ge, fill=0.0, base=0,
      pattern=[[1, P]], channel_multiplier=-1)

    vectors = [("c", dram["c"]), ("ln0_g", dram["ln0_g"]), ("ln0_b", dram["ln0_b"]), ("b_ada", dram["b_ada"]),
               ("dn_conv", dram["dn_conv"]), ("ln1_g", dram["ln1_g"]), ("ln1_b", dram["ln1_b"]),
               ("dn_norm_g", dram["dn_norm_g"]), ("gla_norm_g", dram["gla_norm_g"]),
               ("gla_b_gate", dram["gla_b_gate"]), ("ffn_conv", dram["ffn_conv"]),
               ("ffn_conv_b", dram["ffn_conv_b"]), ("norm_mix_g", dram["norm_mix_g_2"]),
               ("norm_cross_g", dram["norm_cross_g_2"]), ("norm_mem_g", dram["norm_mem_g_2"]),
               ("norm_mlp_g", dram["norm_mlp_g_2"]), ("conv_w", dram["conv_w_2"]),
               ("conv_b", dram["conv_b_2"]), ("rg_a_b", dram["rg_a_b_2"]), ("rg_x_b", dram["rg_x_b_2"]),
               ("rg_lambda", dram["rg_lambda_2"])]
    first_col, n_rows = {}, 0
    for name, ap in vectors:
        first_col[name] = n_rows
        n_rows += ap.size() // P
    n_vt = -(-n_rows // P)
    cols = sb("cols", [P, n_vt * P])
    vr = ExitStack()
    vec_rows = sb("vec_rows", [P, n_vt, P], where=vr)
    m_zero = V(dve.memset, vec_rows[:], 0.0)
    SP.wait(m_zero)
    for name, ap in vectors:
        flat = ap
        while len(flat.shape) > 1:
            names = " ".join("abcdef"[:len(flat.shape)])
            flat = flat.rearrange(f"{names} -> ({names})")
        flat = flat.rearrange("(r p) -> r p", p=P)
        at, n = first_col[name], ap.size() // P
        done = 0
        while done < n:
            tile, row = divmod(at + done, P)
            take = min(n - done, P - row)
            m_vec = vectors_loaded.inc(nc.sync.dma_start(vec_rows[row:row + take, tile, :], flat[done:done + take, :]))
            done += take

    def col(name, n=0, count=1):
        return cols[:, first_col[name] + n:first_col[name] + n + count]

    PE.wait(G.last)
    b, ps = bank()
    for n in range(4):
        m = PE(te.transpose, ps[:, 0:P], ident[:], ident[:])
        head = A(act.copy, cols[:, 0:1], ident[:, 0:1], after=[G.last])
    emptied(b, m)
    V.wait(head)
    PE.wait(m_vec)
    for n in range(n_vt):
        b, ps = bank()
        m = PE(te.transpose, ps[:, 0:P], vec_rows[:, n, :], ident[:])
        emptied(b, V(dve.tensor_copy, cols[:, n * P:(n + 1) * P], ps[:, 0:P], after=[m]))
    cols_ready = V.last
    pr.barrier()
    vr.close()

    resid = sb("resid", [P, NT, D])
    ft_space = ExitStack()
    ft = []

    def open_ft(parts):
        pr.barrier()
        ft_space.close()
        ft[:] = ([sb("ft", [P, KD, T], where=ft_space)] if parts == 1 else
                 [sb(f"ft_{n}", [P, KD, T], F32R, ft_space) for n in ("hi", "lo")])

    def ft_at(k, c):
        return tuple(x[:, k, c] for x in ft)


    eps_col = sb("eps_col", [P, 1])
    V(dve.memset, eps_col[:], EPS)
    eps_q = sb("eps_q", [P, 1])
    V(dve.memset, eps_q[:], EPS * P)
    stats = sb("stats", [P, 2, 2, 6])
    moments = sb("moments", [P, NT, 2])
    held = sb("held", [P, 1])
    rstd = sb("rstd", [P, NT])
    newton = sb("newton", [P, 2, NT])
    now = sb("now", [P, 2, 3])

    def to_features(src, dst, tok0, n_tok, scale, bias, after, name="xhat0"):
        n = int(name[-1])
        scaled = []
        for q in range(KD // 4):
            b, ps = bank()
            PE.wait(*after)
            for k in range(4):
                m = te.transpose(ps[:, k * P:k * P + n_tok], src[0:n_tok, (4 * q + k) * P:(4 * q + k + 1) * P],
                                 ident[0:n_tok, 0:n_tok])
            m = PE.done.inc(m)
            split = len(dst) > 1
            free = pr.free.get(f"feat_tmp{n}", ()) if split else ()
            for k in range(4):
                kk = 4 * q + k
                src_k = ps[:, k * P:k * P + n_tok]
                o = feat_tmp[n][:, kk, 0:n_tok] if split else dst[0][:, kk, bass.ds(tok0, n_tok)]
                if q == 0:
                    e = V(dve.tensor_scalar, o, src_k, scale(kk), bias(kk) if bias else None, ALU.mult,
                          ALU.add if bias else ALU.bypass, after=[m, *free], chain=False)
                else:
                    e = A(act.activation, o, src_k, ACT.Identity if bias else ACT.Copy, scale=scale(kk),
                          bias=bias(kk) if bias else 0.0, after=[m, *free], chain=False)
            emptied(b, e)
            scaled.append(e)
        for q, e in enumerate(scaled if split else ()):
            ks = slice(4 * q, 4 * q + 4)
            hi, lo = (x[:, ks, bass.ds(tok0, n_tok)] for x in dst)
            tmp = feat_tmp[n][:, ks, 0:n_tok]
            e = A(act.activation, hi, tmp, ACT.Copy, after=[e], chain=False)
            e = G(pool.tensor_tensor, lo, tmp, f32(hi), ALU.subtract, after=[e], chain=False)
        if split:
            pr.free[f"feat_tmp{n}"] = [e]
        pr.free[name] = [m]

    def rms_heads(ps, m, tmp, out, gain):
        flat = tmp[:].rearrange("p a b -> p (a b)")
        m = A(act.activation, flat, ps[:], ACT.Square, after=[m, *pr.free.get("sq", ())])
        b, ps2 = bank(m)
        m = PE(te.matmul, ps2[:], ones[:], flat, start=True, stop=True)
        A(act.activation, flat, ps2[:], ACT.Ln, bias=eps_col[:], scale=1.0 / P, after=[m])
        emptied(b, A.last)
        m = A(act.activation, flat, flat, ACT.Exp, scale=-0.5)
        m = V(dve.scalar_tensor_tensor, out, ps[:].rearrange("p (h c) -> p h c", h=4), gain, tmp[:], ALU.mult,
              ALU.mult, after=[m])
        pr.free["sq"] = [m]
        return m

    def tile_of(t, n):
        return t[:, n, :] if isinstance(n, int) else t[:, bass.ds(n, 1), :].rearrange("p a b -> p (a b)")

    norm_rows, xhat, square, feat_tmp = None, None, None, None

    @contextmanager
    def norm_space(rows=(), row_scale=1.0):
        nonlocal norm_rows, xhat, square, feat_tmp
        pr.barrier()
        act.preload_act_table_set("natural_log_exp_and_others")
        with ExitStack() as ph:
            norm_rows = sb("norm_rows", [P, 2, D], where=ph) if rows else None
            xhat = [sb(f"xhat{n}", [P, D], where=ph) for n in range(2)]
            square = sb("square", [P, D], where=ph)
            feat_tmp = [sb(f"feat_tmp{n}", [P, KD, P], where=ph) for n in range(2)] if len(ft) > 1 else None
            if rows:
                SP.wait(*[Mark(q.done, q.done.count, None) for q in (V, A, G) if q.done.count])
                sig = loads(f"rows_{rows[0]}")
                for n, name in enumerate(rows):
                    v = dram[name]
                    m = sig.inc(nc.sync.dma_start(norm_rows[:, n, :],
                                                  (v[0] if len(v.shape) == 2 else v).partition_broadcast(P)))
                G.wait(m)
                V(dve.tensor_scalar, norm_rows[:, 0:len(rows), :], norm_rows[:, 0:len(rows), :], row_scale, None,
                  ALU.mult, after=[m]) if row_scale != 1.0 else V.wait(m)
                G.wait(*([V.last] if row_scale != 1.0 else []))
            yield ph
            pr.barrier()

    def deviation(of, scale, n):
        x, y = newton[:, 0, 0:n], rstd[:, 0:n]
        m = V(dve.tensor_scalar, x, of, scale, EPS, ALU.mult, ALU.add, after=[A.last] if A.last else [])
        A(act.activation, y, x, ACT.Ln, after=[m])
        m = A(act.activation, y, y, ACT.Exp, scale=-0.5)
        step = newton[:, 1, 0:n]
        V(dve.tensor_tensor, step, y, y, ALU.mult, after=[m])
        V(dve.tensor_tensor, step, step, x, ALU.mult)
        V(dve.tensor_scalar, step, step, -0.5, 1.5, ALU.mult, ALU.add)
        V(dve.tensor_tensor, y, y, step, ALU.mult)

    def moments_of(name, x):
        with pr.repeat(name, NT // 2) as i:
            for u in range(2):
                for n in range(2):
                    V(dve.bn_stats, stats[:, u, n, :], tile_of(x, i * 2 + u)[:, n * BANK:(n + 1) * BANK],
                      after=pr.free.get("stats", ()), chain=False)
            V(dve.memset, held[:], 0.0, after=pr.free.get("now2", ()))
            for u in range(2):
                m = V(dve.bn_aggr, now[:, u, 0:2], stats[:, u, :, :].rearrange("p a b -> p (a b)"), chain=False)
            pr.free["stats"] = [m]
            pr.free["now2"] = [V(dve.tensor_copy, moments[:, bass.ds(i * 2, 2), :], now[:, :, 0:2])]
        deviation(moments[:, :, 1], 1.0, NT)

    def squares_of(name, x, n_tiles=NT):
        if name is None:
            for n in range(n_tiles):
                m = A(act.activation, square[:], x[:, n, :], ACT.Square, accum_out=moments[:, n, 0:1])
        else:
            with pr.repeat(name, n_tiles) as i:
                A(act.activation, square[:], tile_of(x, i), ACT.Square,
                  accum_out=moments[:, bass.ds(i, 1), 0:1].rearrange("p a b -> p (a b)"))
        deviation(moments[:, 0:n_tiles, 0], 1.0 / D, n_tiles)

    def normed(x, n, u, centred):
        after = pr.free.get(f"xhat{u}", ())
        if isinstance(n, int):
            mean, dev = moments[:, n, 0:1], rstd[:, n:n + 1]
        else:
            V(dve.tensor_copy, now[:, u, 0:1], moments[:, bass.ds(n, 1), 0:1].rearrange("p a b -> p (a b)"),
              after=pr.free.get("now", ()), chain=False)
            V(dve.tensor_copy, now[:, u, 1:2], rstd[:, bass.ds(n, 1)], chain=False)
            mean, dev = now[:, u, 0:1], now[:, u, 1:2]
        if centred:
            m = V(dve.tensor_scalar, xhat[u][:], tile_of(x, n), mean, dev, ALU.subtract, ALU.mult, after=after)
        else:
            m = V(dve.tensor_scalar, xhat[u][:], tile_of(x, n), dev, None, ALU.mult, after=after)
        pr.free["now"] = [m]
        return m

    def affine(x, n, u, m):
        m = V(dve.tensor_tensor, tile_of(x, n), xhat[u][:], norm_rows[:, 0, :], ALU.mult)
        return m, G(pool.tensor_tensor, tile_of(x, n), tile_of(x, n), norm_rows[:, 1, :], ALU.add, after=[m],
                    chain=False)

    def layer_norm_features(name, rows, which):
        with norm_space(rows, ALPHA):
            moments_of(name + "_moments", resid)
            with pr.repeat(name, NT // 2) as i:
                marks = [normed(resid, i * 2 + u, u, True) for u in range(2)]
                for u, m in enumerate(marks):
                    read, _ = affine(resid, i * 2 + u, u, m)
                    to_features(xhat[u], ft, (i * 2 + u) * P, P, lambda k: in_scale[:, which, k:k + 1],
                                lambda k: in_bias[:, which, k:k + 1], [m], f"xhat{u}")
                    pr.free[f"xhat{u}"].append(read)

    def rms_norm_features(name, gain):
        with norm_space():
            squares_of(name + "_squares", resid)
            with pr.repeat(name, NT // 2) as i:
                marks = [normed(resid, i * 2 + u, u, False) for u in range(2)]
                for u, m in enumerate(marks):
                    to_features(xhat[u], ft, (i * 2 + u) * P, P, lambda k: col(gain, k), None, [m], f"xhat{u}")

    b1 = ExitStack()
    gate_row = sb("gate_row", [P, 2, D])
    in_scale = sb("in_scale", [P, 2, KD])
    in_bias = sb("in_bias", [P, 2, KD])
    mod_row = sb("mod_row", [P, 6, D], where=b1)
    with ExitStack() as ph:
        cond = sb("cond", [P, KD], where=ph)
        cond_b = sb("cond_b", [P, KD, P], where=ph)
        A(act.activation, cond[:], col("c", 0, KD), ACT.Silu, after=[cols_ready])
        m_cond = V(dve.tensor_copy, cond_b[:], spread(cond[:], 2, P), after=[A.last])
        w_ada = dram["w_ada"][0]
        m_b = loads("b_ada").inc(nc.sync.dma_start(mod_row[:].rearrange("p a b -> p (a b)"),
                                               dram["b_ada"][0].partition_broadcast(P)))
        PE.wait(m_cond)
        V.wait(m_b)
        with pr.repeat("ada", 6) as i:
            for n in range(2):
                b, ps = bank()
                for k2 in range(KD // 2):
                    w = Weights(rows_of(w_ada, 2 * k2 * P, 2 * P, i * D + n * BANK, BANK))
                    PE.wait(*w.ready)
                    for k in range(2):
                        mm = te.matmul(ps[:], cond_b[:, 2 * k2 + k, :], w.parts[0][:, k, :], start=(k2 == k == 0),
                                       stop=(k2 == KD // 2 - 1 and k == 1))
                    mm = PE.done.inc(mm)
                    w.used(mm)
                o = mod_row[:, bass.ds(i, 1), n * BANK:(n + 1) * BANK].rearrange("p a b -> p (a b)")
                emptied(b, V(dve.tensor_tensor, o, ps[:], o, ALU.add, after=[mm]))
    SH_A, SC_A, GT_A, SH_F, SC_F, GT_F = range(6)

    mod_col = sb("mod_col", [P, 4, KD], where=b1)
    square = sb("mod_diagonal", [P, D], where=b1)
    for n, part in enumerate((SH_A, SC_A, SH_F, SC_F)):
        for k in range(KD):
            V(dve.tensor_tensor, square[:, k * P:(k + 1) * P], mod_row[:, part, k * P:(k + 1) * P], ident[:],
              ALU.mult, chain=k == 0)
        V(dve.tensor_reduce, mod_col[:, n, :], square[:].rearrange("p (k c) -> p k c", k=KD), AX, ALU.add)
    for n, (g, b) in enumerate((("ln0_g", "ln0_b"), ("ln1_g", "ln1_b"))):
        V(dve.tensor_scalar, mod_col[:, 2 * n + 1, :], mod_col[:, 2 * n + 1, :], 1.0, None, ALU.add)
        V(dve.tensor_tensor, in_scale[:, n, :], mod_col[:, 2 * n + 1, :], col(g, 0, KD), ALU.mult)
        V(dve.tensor_tensor, in_bias[:, n, :], mod_col[:, 2 * n + 1, :], col(b, 0, KD), ALU.mult)
        V(dve.tensor_tensor, in_bias[:, n, :], in_bias[:, n, :], mod_col[:, 2 * n, :], ALU.add)
    for n, part in enumerate((GT_A, GT_F)):
        V(dve.tensor_scalar, gate_row[:, n, :], mod_row[:, part, :], 1.0, None, ALU.add)

    pr.barrier()
    b1.close()

    open_ft(1)
    m_x = loads("x").inc(nc.sync.dma_start(resid[:], dram["x"][0].rearrange("(n p) d -> p n d", p=P)))
    V.wait(m_x)
    layer_norm_features("norm0", ("ln0_g", "ln0_b"), 0)

    def project(w, c0, n_cols, done):
        for c, wt in enumerate(stream([rows_of(w, 0, D, c0 + base, P) for base in range(0, n_cols, P)])):
            PE.wait(*wt.ready)
            for h in range(HALVES):
                b, ps = bank()
                mm = PE.done.inc(products(ps[:], [(wt.at(k), ft_at(k, slice(h * BANK, (h + 1) * BANK)))
                                                  for k in range(KD)]))
                if h == HALVES - 1:
                    wt.used(mm)
                emptied(b, done(c, h, ps[:], mm))

    def project_tokens(src, n_k, w, r0, c0, halves, take, n_tiles=NT, scale_row=None):
        panels_of = [(h, k) for h in halves for k in range(0, n_k, 2)]
        views = [rows_of(w, r0 + k * P, 2 * P, c0 + h * BANK, BANK) for h, k in panels_of]
        rows = [spread(scale_row[:, h * BANK:(h + 1) * BANK], 1, 2) for h, _ in panels_of] if scale_row is not None \
            else None
        held_banks = []
        for (h, k0), wt in zip(panels_of, stream(views, rows)):
            PE.wait(*wt.ready)
            for n in range(n_tiles):
                if k0 == 0:
                    held_banks.append(bank())
                b, ps = held_banks[n]
                m = products(ps[:], [(src(k0 + j, n), wt.at(j)) for j in range(2)], k0 == 0, k0 == n_k - 2)
                if k0 == n_k - 2:
                    m = PE.done.inc(m)
                    emptied(b, take(h, n, ps, m))
            if k0 != n_k - 2:
                m = PE.done.inc(m)
            else:
                held_banks = []
            wt.used(m)

    def add_residual(h, n, ps, m):
        r = resid[:, n, h * BANK:(h + 1) * BANK]
        return V(dve.tensor_tensor, r, r, ps[:], ALU.add, after=[m], chain=False)

    w_in = dram["w_in"][0]
    mixed_space = ExitStack()
    mixed = sb("mixed", [P, 8, T], where=mixed_space)
    mx = ExitStack()

    v_feat = sb("v_feat", [P, 4, T], where=mx)
    cv = ExitStack()
    pre = [sb(f"conv_in{n}", [P, 3 + T], where=cv) for n in range(2)]
    conv = [sb(f"conv_out{n}", [P, T], where=cv) for n in range(2)]
    taps = sb("taps", [P, 12, 4], where=cv)
    tap_now = sb("tap_now", [P, 4, 4], where=cv)
    V(dve.tensor_copy, taps[:], col("dn_conv", 0, 48).rearrange("p (j c) -> p c j", j=4))
    for n in range(2):
        V(dve.memset, pre[n][:, 0:3], 0.0)

    def causal_conv(buf, n, w, n_taps, bias=None, conv=conv):
        lead = 3 - (n_taps - 1)
        V(dve.tensor_scalar, conv[n][:], buf[:, lead:lead + T], w(0), bias, ALU.mult,
          ALU.add if bias is not None else ALU.bypass, after=pr.free.get(f"conv{n}", ()))
        for j in range(1, n_taps):
            V(dve.scalar_tensor_tensor, conv[n][:], buf[:, lead + j:lead + j + T], w(j), conv[n][:], ALU.mult,
              ALU.add)
        return V.last

    def qkv_chunks(dst, i, c0):
        V(dve.tensor_copy, tap_now[:], taps[:, bass.ds(i * 4, 4), :])
        taps_ready = V.last

        def done(c, h, ps, m):
            n = c % 2
            m = A(act.copy, pre[n][:, 3 + h * BANK:3 + (h + 1) * BANK], ps,
                  after=[m, *(pr.free.get(f"pre{n}", ()) if h == 0 else ())], chain=False)
            if h == HALVES - 1:
                V.wait(m)
                r = causal_conv(pre[n], n, lambda j: tap_now[:, c, j:j + 1], 4)
                pr.free[f"pre{n}"] = [r]
                pr.free[f"conv{n}"] = [A(act.activation, dst(c), conv[n][:], ACT.Silu, after=[r], chain=False)]
            return m
        project(w_in, c0, 512, done)

    act.preload_act_table_set("silu_and_others")
    with pr.repeat("qk", 2) as i:
        qkv_chunks(lambda c: mixed[:, bass.ds(i * 4 + c, 1), :].rearrange("p a b -> p (a b)"), i, i * 512)
    qkv_chunks(lambda c: v_feat[:, c, :], 2, O_V)
    pr.barrier()
    cv.close()

    log_a = sb("log_a", [P, NT, 4], where=mx)
    beta = sb("beta", [P, NT, 4], where=mx)
    with ExitStack() as ph:
        w_ab = sb("w_ab", [P, KD, 8], where=ph)
        heads = sb("heads", [P, 2, 4], where=ph)
        ab = sb("ab", [P, NT, 8], where=ph)
        tmp = sb("ab_tmp", [P, NT, 4], where=ph)
        one = sb("one_col", [P, 1], where=ph)
        SP.wait(Mark(V.done, V.done.count, None), Mark(A.done, A.done.count, None))
        sig = loads("ab")
        sig.inc(nc.sync.dma_start(w_ab[:], rows_of(w_in, 0, D, O_A, 8)))
        sig.inc(nc.sync.dma_start(heads[:, 0, :], dram["dn_a_log"][0].partition_broadcast(P)))
        m_ab = sig.inc(nc.sync.dma_start(heads[:, 1, :], dram["dn_dt_bias"][0].partition_broadcast(P)))
        V(dve.memset, one[:], 1.0)
        PE.wait(m_ab)
        b, ps = bank()
        for n in range(NT):
            for k in range(KD):
                m = te.matmul(ps[:, n * 8:n * 8 + 8], ft[0][:, k, n * P:(n + 1) * P], w_ab[:, k, :],
                              start=(k == 0), stop=(k == KD - 1))
        m = PE.done.inc(m)
        emptied(b, V(dve.tensor_copy, ab[:], ps[:, 0:NT * 8].rearrange("p (n c) -> p n c", c=8), after=[m, m_ab]))
        A(act.activation, heads[:, 0, :], heads[:, 0, :], ACT.Exp, after=[m_ab])
        m = V(dve.tensor_tensor, tmp[:], ab[:, :, 0:4], spread(heads[:, 1, :], 1, NT), ALU.add)
        softplus(tmp, log_a, one, A, V, act, dve, m)
        V(dve.tensor_tensor, log_a[:], log_a[:], spread(heads[:, 0, :], 1, NT), ALU.mult, after=[A.last])
        V(dve.tensor_scalar, log_a[:], log_a[:], -1.0, None, ALU.mult)
        A(act.activation, beta[:], ab[:, :, 4:8], ACT.Sigmoid, after=[V.last])
        pr.barrier()

    SCALE_Q = DN_W // DN_HEADS
    dn = ExitStack()
    H4 = DN_HEADS

    def four(name):
        return sb(name, [P, H4, P], where=dn)

    def words(t):
        return t[:].rearrange("p a b -> p (a b)")

    masks = sb("masks", [P, 7, P], where=dn)
    for lv in range(7):
        s = 1 << lv
        G(pool.memset, masks[:, lv, :], 0.0)
        view = masks[:, lv, :].rearrange("p (n h c) -> p n h c", h=2, c=s)[:, :, 1, :]
        ones_v = ones[:].rearrange("p (n h c) -> p n h c", h=2, c=s)[:, :, 1, :]
        G(pool.affine_select, out=view, in_=ones_v, compare_op=ALU.is_ge, fill=0.0, base=0,
          pattern=[[-2 * s, P // (2 * s)], [0, s]], channel_multiplier=1)
        G(pool.affine_select, out=view, in_=view, compare_op=ALU.is_ge, fill=0.0, base=s - 1,
          pattern=[[2 * s, P // (2 * s)], [0, s]], channel_multiplier=-1)
    state = four("state")
    V(dve.memset, state[:], 0.0)

    class DeltaTile:

        def __init__(self, u):
            self.la, self.be = sb(f"la_t{u}", [P, H4], where=dn), sb(f"be_t{u}", [P, H4], where=dn)
            self.g_col = sb(f"g_col{u}", [P, 4, H4], where=dn)
            self.g_row = self.ktok = four(f"g_row_ktok{u}")
            self.b_row = self.inv_t = four(f"b_row_inv_t{u}")
            self.decay = self.prod = four(f"decay_prod{u}")
            self.q, self.k = four(f"qn{u}"), four(f"kn{u}")
            self.be_b = self.vt = self.rhs = four(f"vt_rhs{u}")
            self.la_b = self.lt = four(f"lt{u}")
            self.ltm = self.vnew = four(f"ltm_vnew{u}")
            self.at, self.vtok = four(f"at{u}"), four(f"vtok{u}")
            self.sq = self.inv = four(f"sq_inv{u}")

    def per_head(ps, lhs, rhs_of):
        for h in range(H4):
            m = te.matmul(ps[:, h * P:(h + 1) * P], lhs(h), rhs_of(h), start=True, stop=True)
        return PE.done.inc(m)

    ID4 = spread(ident[:], 1, H4)
    state_free = []

    def delta_tile(t, n):
        tok = bass.ds(n * P, P)
        V(dve.tensor_copy, t.la[:], log_a[:, bass.ds(n, 1), :].rearrange("p a b -> p (a b)"), chain=False)
        V(dve.tensor_copy, t.be[:], beta[:, bass.ds(n, 1), :].rearrange("p a b -> p (a b)"), chain=False)
        V(dve.tensor_copy, t.la_b[:], spread(t.la[:], 2, P))
        m_b = V(dve.tensor_copy, t.be_b[:], spread(t.be[:], 2, P))
        unit = ((mixed[:, 0:4, tok], t.q, float(SCALE_Q), t.at), (mixed[:, 4:8, tok], t.k, 1.0, t.sq))
        m_sq = [G(pool.tensor_tensor, sq[:], src, src, ALU.mult, after=[m_b]) for src, _, _, sq in unit]
        yield
        b0, ps = bank(m_b)
        m = per_head(ps, lambda h: t.la_b[:, h, :], lambda h: upper[:])
        m_g = A(act.copy, words(t.g_row), ps[:], after=[m])
        emptied(b0, m_g)
        b0, ps = bank()
        m = PE(te.matmul, ps[:, 0:H4], upper[:], t.la[:], start=True, stop=True)
        m = V(dve.tensor_copy, t.g_col[:, 0, :], ps[:, 0:H4], after=[m])
        emptied(b0, m)
        b0, ps = bank()
        m = per_head(ps, lambda h: t.be_b[:, h, :], lambda h: ident[:])
        m_br = V(dve.tensor_copy, words(t.b_row), ps[:], after=[m])
        emptied(b0, m_br)
        for (src, dst, factor, sq), m in zip(unit, m_sq):
            b0, ps = bank(m)
            m = PE(te.matmul, ps[:], ones[:], words(sq), start=True, stop=True)
            A(act.activation, words(sq), ps[:], ACT.Ln, bias=eps_q[:] if factor != 1.0 else eps_col[:],
              scale=factor, after=[m])
            emptied(b0, A.last)
            m = A(act.activation, words(sq), words(sq), ACT.Exp, scale=-0.5)
            m_n = V(dve.tensor_tensor, dst[:], src, sq[:], ALU.mult, after=[m])
        V(dve.tensor_tensor, t.decay[:], t.g_row[:], spread(t.g_col[:, 0, :], 2, P), ALU.subtract, after=[m_g])
        m = V(dve.tensor_scalar, t.decay[:], t.decay[:], 0.0, None, ALU.min)
        A(act.activation, t.decay[:], t.decay[:], ACT.Exp, after=[m])
        g_end = t.g_row[:, :, P - 1]
        m = V(dve.tensor_tensor, t.g_col[:, 2, :], g_end, t.g_col[:, 0, :], ALU.subtract)
        A(act.activation, t.g_col[:, 1, :], t.g_col[:, 0, :], ACT.Exp)
        A(act.activation, t.g_col[:, 2, :], t.g_col[:, 2, :], ACT.Exp, after=[m])
        m_e = A(act.activation, t.g_col[:, 3, :], g_end, ACT.Exp)
        m_er = A(act.activation, t.g_row[:], t.g_row[:], ACT.Exp)
        m_v = G(pool.tensor_copy, t.vt[:], v_feat[:, :, tok], after=[m_br])
        V(dve.tensor_tensor, t.decay[:], t.decay[:], spread(upper[:], 1, H4), ALU.mult, after=[m_e])
        yield
        b0, ps = bank(m_n)
        m = per_head(ps, lambda h: t.k[:, h, :], lambda h: t.k[:, h, :])
        V(dve.tensor_tensor, words(t.lt), ps[:], words(t.decay), ALU.mult, after=[m])
        emptied(b0, V.last)
        b0, ps = bank()
        m = per_head(ps, lambda h: t.k[:, h, :], lambda h: t.q[:, h, :])
        m_at = V(dve.tensor_tensor, words(t.at), ps[:], words(t.decay), ALU.mult, after=[m])
        emptied(b0, m_at)
        m_lt = V(dve.tensor_tensor, t.lt[:], t.lt[:], t.b_row[:], ALU.mult)
        m_l = V(dve.tensor_tensor, t.ltm[:], t.lt[:], spread(masks[:, 0, :], 1, H4), ALU.mult)
        m_xt = V(dve.tensor_tensor, t.inv_t[:], ID4, t.ltm[:], ALU.subtract)
        m_qd = V(dve.tensor_tensor, t.q[:], t.q[:], t.g_row[:], ALU.mult, after=[m_er])
        for src, dst, w in ((t.vt, t.vtok, m_v), (t.k, t.ktok, m_qd)):
            b0, ps = bank(m_v, m_n)
            for h in range(H4):
                m = te.transpose(ps[:, h * P:(h + 1) * P], src[:, h, :], ident[:])
            m = PE.done.inc(m)
            m_tok = A(act.copy, words(dst), ps[:], after=[m, w])
            emptied(b0, m_tok)
        b0, ps = bank(m_l)
        for h in range(H4):
            mm = te.transpose(ps[:, h * P:(h + 1) * P], t.ltm[:, h, :], ident[:])
        mm = PE.done.inc(mm)
        m_x = V(dve.tensor_tensor, t.inv[:], ID4, ps[:].rearrange("p (h c) -> p h c", h=H4), ALU.subtract,
                after=[mm])
        emptied(b0, m_x)
        for lv in range(1, 7):
            m = G(pool.tensor_tensor, t.ltm[:], t.lt[:], spread(masks[:, lv, :], 1, H4), ALU.mult,
                  after=[m_lt, mm, m_xt])
            yield
            b0, ps = bank(m, m_x)
            mm = per_head(ps, lambda h: t.ltm[:, h, :], lambda h: t.inv[:, h, :])
            m = A(act.copy, words(t.prod), ps[:], after=[mm])
            emptied(b0, m)
            yield
            b1_, ps1 = bank(m, m_xt)
            m1 = per_head(ps1, lambda h: t.prod[:, h, :], lambda h: t.inv_t[:, h, :])
            m0 = m1
            if lv < 6:
                b2_, ps2 = bank()
                m0 = per_head(ps2, lambda h: t.inv_t[:, h, :], lambda h: t.prod[:, h, :])
                m_x = V(dve.tensor_tensor, words(t.inv), words(t.inv), ps2[:], ALU.subtract, after=[m0])
                emptied(b2_, m_x)
            m_xt = V(dve.tensor_tensor, words(t.inv_t), words(t.inv_t), ps1[:], ALU.subtract, after=[m0])
            emptied(b1_, m_xt)
            A.wait(m0)
        V(dve.tensor_tensor, t.ktok[:], t.ktok[:], spread(t.g_col[:, 2, :], 2, P), ALU.mult, after=[m_tok])
        yield
        b0, ps = bank(*state_free)
        m = per_head(ps, lambda h: t.k[:, h, :], lambda h: state[:, h, :])
        V(dve.tensor_tensor, t.rhs[:], ps[:].rearrange("p (h c) -> p h c", h=H4), spread(t.g_col[:, 1, :], 2, P),
          ALU.mult, after=[m])
        emptied(b0, V.last)
        V(dve.tensor_tensor, t.rhs[:], t.vtok[:], t.rhs[:], ALU.subtract)
        m = V(dve.tensor_tensor, t.rhs[:], t.rhs[:], spread(t.be[:], 2, P), ALU.mult)
        yield
        b0, ps = bank(m, m_xt)
        m = per_head(ps, lambda h: t.inv_t[:, h, :], lambda h: t.rhs[:, h, :])
        m_vn = A(act.copy, words(t.vnew), ps[:], after=[m])
        emptied(b0, m_vn)
        yield
        b0, ps = bank(m_qd, m_vn, m_at)
        for h in range(H4):
            te.matmul(ps[:, h * P:(h + 1) * P], state[:, h, :], t.q[:, h, :], start=True, stop=False)
            m = te.matmul(ps[:, h * P:(h + 1) * P], t.vnew[:, h, :], t.at[:, h, :], start=False, stop=True)
        m_o = PE.done.inc(m)
        V(dve.tensor_tensor, state[:], state[:], spread(t.g_col[:, 3, :], 2, P), ALU.mult, after=[m_o])
        b1_, ps1 = bank()
        m = per_head(ps1, lambda h: t.ktok[:, h, :], lambda h: t.vnew[:, h, :])
        m = V(dve.tensor_tensor, words(state), words(state), ps1[:], ALU.add, after=[m])
        emptied(b1_, m)
        state_free[:] = [m]
        pr.free["state"] = [m]
        yield
        emptied(b0, rms_heads(ps, m_o, t.sq, mixed[:, 0:4, tok], col("dn_norm_g")))

    def in_turn(steps, lag):
        at = [-lag * n for n in range(len(steps))]
        while steps:
            for n in range(len(at)):
                if at[n] >= 0 and steps[n] is not None and next(steps[n], "over") == "over":
                    steps[n] = None
                at[n] += 1
            if all(x is None for x in steps):
                break

    tiles = [DeltaTile(u) for u in range(2)]
    act.preload_act_table_set("natural_log_exp_and_others")
    with pr.repeat("delta", NT // 2) as i:
        V.wait(*[m for q in pr.engines for m in pr.free.get(f"last_{q.name}", ())])
        for n in range(8):
            emptied(n)
        state_free[:] = pr.free.get("state", ())
        in_turn([delta_tile(t, i * 2 + u) for u, t in enumerate(tiles)], DELTA_LAG)
    dn.close()
    mx.close()

    gl = ExitStack()
    g_qk = sb("g_qk", [P, 4, T], where=gl)
    k_dec = sb("k_dec", [P, 2, T], where=gl)
    g_v = sb("g_v", [P, NT, GLA_W], where=gl)
    g_last = sb("g_last", [P, 2, NGC], where=gl)

    def gqk_done(c, h, ps, m):
        return A(act.mul, g_qk[:, c, h * BANK:(h + 1) * BANK], ps, GLA_K ** -0.5 if c < 2 else 1.0, after=[m],
                 chain=False)
    project(w_in, O_GQ, 512, gqk_done)
    project_tokens(lambda k, n: ft_at(k, slice(n * P, (n + 1) * P)), KD, w_in, 0, O_GV, (0,),
                   lambda h, n, ps, m: V(dve.tensor_copy, g_v[:, n, :], ps[:], after=[m], chain=False))

    with ExitStack() as ph:
        w_r = sb("w_r", [P, KD, RANK], where=ph)
        w_g2 = sb("w_g2", [RANK, 2 * P], where=ph)
        r_feat = sb("r_feat", [RANK, T], where=ph)
        cum = sb("cum", [P, 2, T], where=ph)
        tmp = sb("cum_tmp", [P, 2, T], where=ph)
        keep = sb("keep", [P, T], where=ph)
        one = sb("one_col2", [P, 1], where=ph)
        SP.wait(Mark(V.done, V.done.count, None), Mark(A.done, A.done.count, None))
        sig = loads("gate")
        sig.inc(nc.sync.dma_start(w_r[:], rows_of(w_in, 0, D, O_GR, RANK)))
        m_r = sig.inc(nc.sync.dma_start(w_g2[:], dram["gla_w_gate2"][0]))
        V(dve.memset, one[:], 1.0)
        V(dve.memset, keep[:], 1.0)
        m_keep = V(dve.memset, keep[:].rearrange("p (n c) -> p n c", c=GC)[:, :, 0:1], 0.0)
        PE.wait(m_r)
        for h in range(HALVES):
            b, ps = bank()
            for k in range(KD):
                m = te.matmul(ps[0:RANK, :], w_r[:, k, :], ft[0][:, k, h * BANK:(h + 1) * BANK], start=(k == 0),
                              stop=(k == KD - 1))
            m = PE.done.inc(m)
            emptied(b, A(act.copy, r_feat[:, h * BANK:(h + 1) * BANK], ps[0:RANK, :], after=[m]))
        for c in range(2):
            for h in range(HALVES):
                b, ps = bank()
                m = PE(te.matmul, ps[:], w_g2[:, c * P:(c + 1) * P], r_feat[:, h * BANK:(h + 1) * BANK],
                       start=True, stop=True, after=[A.last])
                emptied(b, V(dve.tensor_scalar, tmp[:, c, h * BANK:(h + 1) * BANK], ps[:],
                             col("gla_b_gate", c), -1.0, ALU.add, ALU.mult, after=[m]))
        softplus(tmp, cum, one, A, V, act, dve, V.last)
        for c in range(2):
            V(dve.tensor_tensor_scan, tmp[:, c, :], keep[:], cum[:, c, :], 0.0, ALU.mult, ALU.add)
        b_sum = tmp
        ends = b_sum[:].rearrange("p c (n t) -> p c n t", t=GC)[:, :, :, GC - 1]
        m = V(dve.tensor_tensor, k_dec[:].rearrange("p c (n t) -> p c n t", t=GC),
              b_sum[:].rearrange("p c (n t) -> p c n t", t=GC), spread(ends, 3, GC), ALU.subtract)
        A(act.activation, k_dec[:], k_dec[:], ACT.Exp, scale=1.0 / TAU, after=[m])
        A(act.activation, g_last[:], ends, ACT.Exp, scale=-1.0 / TAU)
        m = A(act.activation, cum[:], b_sum[:], ACT.Exp, scale=-1.0 / TAU)
        V(dve.tensor_tensor, g_qk[:, 0:2, :], g_qk[:, 0:2, :], cum[:], ALU.mult, after=[m])
        V(dve.tensor_tensor, k_dec[:], k_dec[:], g_qk[:, 2:4, :], ALU.mult)
        m = A(act.activation, cum[:], b_sum[:], ACT.Exp, scale=1.0 / TAU, after=[V.last])
        V(dve.tensor_tensor, g_qk[:, 2:4, :], g_qk[:, 2:4, :], cum[:], ALU.mult, after=[m])
        pr.barrier()

    def gls(name, shape):
        return sb(name, shape, where=gl)
    st_g = gls("st_g", [P, 4, P])
    chunk_mask = gls("chunk_mask", [P, P])

    class GlaTile:

        def __init__(self, u):
            self.u = u
            self.k_inv = gls(f"k_inv{u}", [P, 4, P])
            self.kd = gls(f"kd{u}", [P, 2, P])
            self.kd_tok = gls(f"kd_tok{u}", [P, 2, 2, P])
            self.v = gls(f"v_t{u}", [P, GLA_W])
            self.at, self.sq = gls(f"at_g{u}", [P, 4, P]), gls(f"sq_g{u}", [P, 4, P])
            self.g_last = gls(f"gl_t{u}", [P, 2, 2])

    G(pool.tensor_copy, chunk_mask[:], upper[:])
    G(pool.memset, chunk_mask[0:GC, GC:P], 0.0)
    tiles = [GlaTile(u) for u in range(2)]
    for t in [st_g] + [x for t in tiles for x in (t.k_inv, t.kd_tok)]:
        G(pool.memset, t[:], 0.0)

    def gla_tile(t, n):
        tok = bass.ds(n * P, P)

        def free(key):
            return pr.free.get(f"gla_{key}{t.u}", ())

        for hb in range(2):
            rows = slice(hb * GLA_K, (hb + 1) * GLA_K)
            m_k = G(pool.tensor_copy, t.k_inv[rows].rearrange("p (a b) t -> p a b t", b=2)[:, :, hb, :],
                    g_qk[rows, 2:4, tok], after=free("k_inv"))
        m_kd = G(pool.tensor_copy, t.kd[:], k_dec[:, :, tok], after=free("kd"))
        m_v = A(act.copy, t.v[:], g_v[:, bass.ds(n, 1), :].rearrange("p a b -> p (a b)"), after=free("v"))
        m_gl = V(dve.tensor_copy, t.g_last[:], g_last[:, :, bass.ds(n * 2, 2)])
        b0, ps = bank(m_k)
        for h in range(GLA_HEADS):
            m = te.matmul(ps[:, h * P:(h + 1) * P], t.k_inv[:, h, :], g_qk[:, h // 2, tok], start=True, stop=True)
        m = PE.done.inc(m)
        pr.free[f"gla_k_inv{t.u}"] = [m]
        m_at = V(dve.tensor_tensor, t.at[:], ps[:].rearrange("p (h c) -> p h c", h=4), spread(chunk_mask[:], 1, 4),
                 ALU.mult, after=[m, *free("at")])
        emptied(b0, m_at)
        b0, ps = bank(m_kd)
        for p in range(2):
            m = te.transpose(ps[:, p * P:(p + 1) * P], t.kd[:, p, :], ident[:])
        m = PE.done.inc(m)
        pr.free[f"gla_kd{t.u}"] = [m]
        for c in range(2):
            rows = slice(c * GC, (c + 1) * GC)
            m_kt = A(act.copy, t.kd_tok[rows, c, :, :], ps[rows, 0:2 * P].rearrange("p (a b) -> p a b", a=2),
                     after=[m, *free("kd_tok")])
        emptied(b0, m_kt)
        yield
        b0, ps = bank(m_at, m_v)
        for h in range(GLA_HEADS):
            m = te.matmul(ps[:, h * P:(h + 1) * P], t.v[:, h * P:(h + 1) * P], t.at[:, h, :], start=(h == 0),
                          stop=False)
        m = PE.done.inc(m)
        adds = []
        for c in range(2):
            b1_, ps1 = bank(m_kt)
            for p in range(2):
                m = te.matmul(ps1[:, p * 2 * P:(p + 1) * 2 * P], t.kd_tok[:, c, p, :],
                              t.v[:, p * 2 * P:(p + 1) * 2 * P], start=True, stop=True)
            adds.append((b1_, ps1, PE.done.inc(m)))
        pr.free[f"gla_kd_tok{t.u}"] = pr.free[f"gla_v{t.u}"] = [m_add for _, _, m_add in adds[1:]]
        yield
        for c in range(2):
            PE.wait(*state_free)
            for h in range(GLA_HEADS):
                m = te.matmul(ps[:, h * P + c * GC:h * P + (c + 1) * GC], st_g[:, h, :],
                              g_qk[:, h // 2, bass.ds(n * P + c * GC, GC)], start=False, stop=(h == 3 and c == 1))
            m_o = PE.done.inc(m)
            b1_, ps1, m_add = adds[c]
            for h in range(GLA_HEADS):
                rows = slice((h % 2) * GLA_K, (h % 2 + 1) * GLA_K)
                m = V(dve.scalar_tensor_tensor, st_g[rows, h, :], st_g[rows, h, :], t.g_last[rows, h // 2, c:c + 1],
                      ps1[rows, h * P:(h + 1) * P], ALU.mult, ALU.add, after=[m_add, m_o, m_gl], chain=h == 0)
            emptied(b1_, m)
            state_free[:] = [m]
            pr.free["gla_state"] = [m]
            yield
        pr.free[f"gla_at{t.u}"] = [m_o]
        emptied(b0, rms_heads(ps, m_o, t.sq, mixed[:, 4:8, tok], col("gla_norm_g")))

    pr.free.pop("sq", None)
    act.preload_act_table_set("natural_log_exp_and_others")
    with pr.repeat("gla", NT // 2) as i:
        state_free[:] = pr.free.get("gla_state", ())
        in_turn([gla_tile(t, i * 2 + u) for u, t in enumerate(tiles)], 2)
    gl.close()

    with ExitStack() as ph:
        gate = [sb(f"gate{n}", [P, BANK], where=ph) for n in range(2)]
        act.preload_act_table_set("silu_and_others")
        with pr.repeat("gates", 2) as i:
            def gate_done(c, h, ps, m):
                n = h % 2
                m = A(act.activation, gate[n][:], ps, ACT.Silu, after=[m, *pr.free.get(f"gate{n}", ())], chain=False)
                o = mixed[:, bass.ds(i * 4 + c, 1), h * BANK:(h + 1) * BANK].rearrange("p a b -> p (a b)")
                pr.free[f"gate{n}"] = [V(dve.tensor_tensor, o, o, gate[n][:], ALU.mult, after=[m], chain=False)]
                return m
            project(w_in, i * (O_GG - O_Z) + O_Z, 512, gate_done)

        project_tokens(lambda k, n: (mixed[:, k, n * P:(n + 1) * P],), 8, dram["w_o"][0], 0, 0, (0, 1), add_residual,
                       scale_row=gate_row[:, 0, :])
        pr.barrier()
    mixed_space.close()
    open_ft(2)

    layer_norm_features("norm1", ("ln1_g", "ln1_b"), 1)

    with ExitStack() as ph:
        pre = [sb(f"ffn_in{n}", [P, 3 + T], where=ph) for n in range(2)]
        conv = [sb(f"ffn_conv{n}", [P, T], where=ph) for n in range(2)]
        hid = [[sb(f"ffn_hid{n}", [P, T], F32R, ph) for _ in range(2)] for n in range(2)]
        taps = sb("ffn_taps", [P, 2, NFF, 4], where=ph)
        tap_now = sb("ffn_tap_now", [P, 2, 2, 4], where=ph)
        V(dve.tensor_copy, taps[:, :, :, 0:3],
          col("ffn_conv", 0, 3 * 2 * NFF).rearrange("p (j g c) -> p g c j", j=3, g=2))
        V(dve.tensor_copy, taps[:, :, :, 3:4],
          col("ffn_conv_b", 0, 2 * NFF).rearrange("p (g c j) -> p g c j", g=2, j=1))
        for n in range(2):
            V(dve.memset, pre[n][:, 0:3], 0.0)
        w_up, w_down = dram["ffn_w_up"][0], dram["ffn_w_down"][0]

        gate_f = gate_row[:, 1, :]
        with halved_panels(3), pr.repeat("ffn", NFF // 2) as i:
            V(dve.tensor_copy, tap_now[:], taps[:, :, bass.ds(i * 2, 2), :])
            sources = [(u, g, rows_of(w_up, 0, D, (i * 2 + u) * P + g * FF, P)) for u in range(2) for g in range(2)]
            sources += [(h, 2, rows_of(w_down, i * 2 * P, 2 * P, h * BANK, BANK)) for h in range(2)]
            scale = [None] * 4 + [spread(gate_f[:, h * BANK:(h + 1) * BANK], 1, 2) for h in range(2)]
            hid_ready = {}
            for (u, g, _), wt in zip(sources, stream([x for _, _, x in sources], scale)):
                PE.wait(*wt.ready)
                if g < 2:
                    for h in range(HALVES):
                        hs = slice(h * BANK, (h + 1) * BANK)
                        b, ps = bank()
                        mm = PE.done.inc(products(ps[:], [(wt.at(k), ft_at(k, hs)) for k in range(KD)]))
                        m = A(act.activation, pre[g][:, 3 + h * BANK:3 + (h + 1) * BANK], ps[:], ACT.Copy,
                              after=[mm, *pr.free.get(f"pre{g}{h}", ())], chain=False)
                        emptied(b, m)
                        w = tap_now[:, g, u, :]
                        r = V(dve.tensor_scalar, conv[g][:, hs], pre[g][:, 1 + h * BANK:1 + (h + 1) * BANK], w[:, 0:1],
                              w[:, 3:4], ALU.mult, ALU.add, after=[m, *pr.free.get(f"fconv{g}{h}", ())])
                        for j in range(1, 3):
                            r = V(dve.scalar_tensor_tensor, conv[g][:, hs],
                                  pre[g][:, 1 + j + h * BANK:1 + j + (h + 1) * BANK], w[:, j:j + 1], conv[g][:, hs],
                                  ALU.mult, ALU.add)
                        pr.free[f"pre{g}{h}"] = [r]
                        if h:
                            pr.free[f"pre{g}0"] = [r]
                        if g == 0:
                            m_silu = A(act.activation, conv[0][:, hs], conv[0][:, hs], ACT.Silu, after=[r],
                                       chain=False)
                            pr.free[f"silu{h}"] = [m_silu]
                        else:
                            m = G(pool.tensor_tensor, conv[1][:, hs], conv[0][:, hs], conv[1][:, hs], ALU.mult,
                                  after=[r, *pr.free[f"silu{h}"]], chain=False)
                            pr.free[f"fconv0{h}"] = [m]
                            hi, lo = hid[u]
                            m = A(act.activation, hi[:, hs], conv[1][:, hs], ACT.Copy,
                                  after=[m, *pr.free.get("fhid", ())], chain=False)
                            m = G(pool.tensor_tensor, lo[:, hs], conv[1][:, hs], f32(hi[:, hs]), ALU.subtract,
                                  after=[m], chain=False)
                            pr.free[f"fconv1{h}"] = [m]
                            hid_ready[u, h] = m
                    wt.used(mm)
                else:
                    for n in range(NT):
                        b, ps = bank(*[hid_ready[j, n // (NT // 2)] for j in range(2)])
                        m = PE.done.inc(products(ps[:], [(tuple(x[:, n * P:(n + 1) * P] for x in hid[j]), wt.at(j))
                                                         for j in range(2)]))
                        emptied(b, add_residual(u, n, ps, m))
                    wt.used(m)
                    pr.free["fhid"] = [m]

    with norm_space(("ln2_g", "ln2_b")):
        moments_of("norm2_moments", resid)
        with pr.repeat("norm2", NT // 2) as i:
            for u in range(2):
                m = normed(resid, i * 2 + u, u, True)
                pr.free[f"xhat{u}"] = [affine(resid, i * 2 + u, u, m)[0]]
    open_ft(1)
    rms_norm_features("norm_mix", "norm_mix_g")


    w_in2 = dram["w_in_2"][0]
    O2_U = 3 * HEADS * HD
    mix2_space = ExitStack()
    mix2 = sb("mix2", [P, 8, T], where=mix2_space)

    with ExitStack() as ph:
        def rg(name, shape):
            return sb(name, shape, where=ph)
        gates_w = rg("gates_w", [P, 4, 4, P])
        gw_now = rg("gw_now", [P, 4, P])
        params = rg("params", [P, 4, 11])
        par = rg("par", [P, 11])
        npar = rg("npar", [P, 2])
        one = rg("one_col", [P, 1])
        lam = rg("lam", [P, 8])
        lam_sp = rg("lam_sp", [P, 8])
        pre = rg("u_in", [P, 3 + T])
        uc = rg("uc", [P, T])
        h_f = rg("h_fwd", [P, T])
        ra, ri, th, a_ = ([rg(f"{n}{z}", [P, T]) for z in range(2)] for n in ("gate_a", "gate_x", "th", "a_coef"))
        m = G(pool.memset, gates_w[:], 0.0)
        SP.wait(m)
        sig = loads("gates_w")
        for ty, w in enumerate((dram["rg_a_w_2"][0], dram["rg_x_w_2"][0])):
            for z in range(2):
                for g in range(2):
                    m_gw = sig.inc(nc.sync.dma_start(
                        gates_w[g * 64:(g + 1) * 64, :, ty * 2 + z, g * 64:(g + 1) * 64],
                        w[z].rearrange("(c g) i j -> g i c j", g=2)[g]))
        V(dve.memset, one[:], 1.0)
        V(dve.tensor_copy, params[:, :, 0:4], col("conv_w", 0, 16).rearrange("p (j c) -> p c j", c=4))
        V(dve.tensor_copy, params[:, :, 4:5], col("conv_b", 0, 4).rearrange("p (j c) -> p c j", c=4))
        V(dve.tensor_copy, params[:, :, 5:7], col("rg_a_b", 0, 8).rearrange("p (j c) -> p c j", c=4))
        V(dve.tensor_copy, params[:, :, 7:9], col("rg_x_b", 0, 8).rearrange("p (j c) -> p c j", c=4))
        V(dve.tensor_scalar, lam[:], col("rg_lambda", 0, 8), -1.0, None, ALU.mult)
        softplus(lam, lam_sp, one, A, V, act, dve, V.last)
        V(dve.tensor_scalar, params[:, :, 9:11], lam_sp[:].rearrange("p (j c) -> p c j", c=4), -8.0, None, ALU.mult)
        V(dve.memset, pre[:, 0:2], 0.0)
        V(dve.memset, pre[:, 2 + T:3 + T], 0.0)
        G.wait(m_gw)
        with pr.repeat("rglru", 4) as i:
            m_par = V(dve.tensor_copy, par[:], params[:, bass.ds(i, 1), :].rearrange("p a b -> p (a b)"))
            V(dve.tensor_scalar, npar[:], par[:, 9:11], -1.0, None, ALU.mult)
            m_par = V.last
            m_gwn = G(pool.tensor_copy, gw_now[:], gates_w[:, bass.ds(i, 1), :, :].rearrange("p a b c -> p (a b) c"),
                      after=pr.free.get("gw_now", ()))
            ug = stream([rows_of(w_in2, 0, D, i * P + (O2_U + g * 512), P) for g in range(2)])
            y = mix2[:, bass.ds(i + 4, 1), :].rearrange("p a b -> p (a b)")
            for g, wt in enumerate(ug):
                PE.wait(*wt.ready)
                for h in range(HALVES):
                    hs = slice(h * BANK, (h + 1) * BANK)
                    b, ps = bank()
                    mm = PE.done.inc(products(ps[:], [(wt.at(k), ft_at(k, hs)) for k in range(KD)]))
                    if h == HALVES - 1:
                        wt.used(mm)
                    if g == 0:
                        m = A(act.copy, pre[:, 2 + h * BANK:2 + (h + 1) * BANK], ps[:],
                              after=[mm, *(pr.free.get("u_in", ()) if h == 0 else ())])
                    else:
                        m = A(act.activation, mix2[:, bass.ds(i + 4, 1), hs].rearrange("p a b -> p (a b)"), ps[:],
                              ACT.Gelu_apprx_tanh, after=[mm])
                    emptied(b, m)
                if g == 0:
                    V.wait(m)
                    m_uc = causal_conv(pre, 0, lambda j: par[:, j:j + 1], 4, par[:, 4:5], [uc])
                    pr.free["u_in"] = [m_uc]
            m_y = m
            PE.wait(m_gwn, m_uc)
            for z in range(2):
                for ty, dst in ((0, ra[z]), (1, ri[z])):
                    for h in range(HALVES):
                        hs = slice(h * BANK, (h + 1) * BANK)
                        b, ps = bank()
                        mm = PE(te.matmul, ps[:], gw_now[:, ty * 2 + z, :], uc[:, hs], start=True, stop=True)
                        m_gate = A(act.activation, dst[:, hs], ps[:], ACT.Sigmoid,
                                   bias=par[:, 5 + ty * 2 + z:6 + ty * 2 + z], after=[mm, m_par])
                        emptied(b, m_gate)
            for z in range(2):
                m_t = A(act.activation, th[z][:], ra[z][:], ACT.Tanh, scale=npar[:, z:z + 1])
                m_a = A(act.activation, a_[z][:], ra[z][:], ACT.Exp, scale=par[:, 9 + z:10 + z], chain=False)
                V(dve.tensor_scalar, ra[z][:], th[z][:], 1.0, None, ALU.add, after=[m_a])
                V(dve.reciprocal, ra[z][:], ra[z][:])
                m_sq = V(dve.scalar_tensor_tensor, th[z][:], th[z][:], 2.0, ra[z][:], ALU.mult, ALU.mult)
                G(pool.tensor_tensor, ri[z][:], ri[z][:], uc[:], ALU.mult, after=[m_gate])
            for z in range(2):
                m = A(act.activation, th[z][:], th[z][:], ACT.Sqrt, after=[m_sq])
                V(dve.tensor_tensor, th[z][:], th[z][:], ri[z][:], ALU.mult, after=[m, G.last])
                if z == 0:
                    V(dve.tensor_tensor_scan, h_f[:], a_[z][:], th[z][:], 0.0, ALU.mult, ALU.add)
                else:
                    V(dve.tensor_tensor_scan, ri[z][:, ::-1], a_[z][:, ::-1], th[z][:, ::-1], 0.0, ALU.mult, ALU.add)
            V(dve.tensor_tensor, h_f[:], h_f[:], ri[1][:], ALU.add)
            V(dve.tensor_tensor, y, y, h_f[:], ALU.mult, after=[m_y])
            pr.free["gates"] = [V.last]
            pr.free["gw_now"] = [mm]

    at_space = ExitStack()
    k_feat = sb("k_feat", [P, 4, T], where=at_space)
    v_tok = sb("v_tok", [P, NT, 512], where=at_space)
    with ExitStack() as ph:
        inv_freq = sb("inv_freq", [P, 1], where=ph)
        pos_i = sb("pos_i", [P, T], I32, where=ph)
        ang, cos, sin, turns = (sb(n, [P, T], where=ph) for n in ("ang", "cos", "sin", "turns"))
        t_cos = [sb(f"t_cos{n}", [P, BANK], where=ph) for n in range(2)]
        t_sin = [sb(f"t_sin{n}", [P, BANK], where=ph) for n in range(2)]
        turns_i = pos_i
        SP.wait(Mark(V.done, V.done.count, None), Mark(A.done, A.done.count, None), Mark(PE.done, PE.done.count, None))
        sig = loads("positions")
        sig.inc(nc.sync.dma_start(inv_freq[:], dram["inv_freq"]))
        m = sig.inc(nc.sync.dma_start(pos_i[:], dram["positions_2"][0].partition_broadcast(P)))
        V(dve.tensor_copy, ang[:], pos_i[:], after=[m])
        V(dve.tensor_scalar, ang[:], ang[:], inv_freq[:], None, ALU.mult)
        act.preload_act_table_set("silu_and_others")
        C1 = 6.28125
        C2 = float.fromhex("0x1.fb4p-10")
        C3 = 2 * math.pi - C1 - C2
        for out, quarter in ((sin, 0.0), (cos, 0.25)):
            V(dve.tensor_scalar, turns[:], ang[:], 1.0 / (2 * math.pi), quarter, ALU.mult, ALU.add)
            V(dve.tensor_copy, turns_i[:], turns[:])
            V(dve.tensor_copy, turns[:], turns_i[:])
            V(dve.scalar_tensor_tensor, out[:], turns[:], -C1, ang[:], ALU.mult, ALU.add)
            V(dve.scalar_tensor_tensor, out[:], turns[:], -C2, out[:], ALU.mult, ALU.add)
            V(dve.scalar_tensor_tensor, out[:], turns[:], -C3, out[:], ALU.mult, ALU.add)
            V(dve.tensor_scalar, out[:], out[:], quarter * 2 * math.pi, math.pi, ALU.add, ALU.min)
            m = V(dve.tensor_scalar, out[:], out[:], -math.pi, None, ALU.max)
            A(act.activation, out[:], out[:], ACT.Sin, after=[m])
        for q in (0, 2):
            V(dve.tensor_scalar, sin[32 * q:32 * q + 32, :], sin[32 * q:32 * q + 32, :], -1.0, None, ALU.mult,
              after=[A.last])
        V.wait(A.last, V.last)

        project_tokens(lambda k, n: ft_at(k, slice(n * P, (n + 1) * P)), KD, w_in2, 0, 2 * 512, (0,),
                       lambda h, n, ps, m: V(dve.tensor_copy, v_tok[:, n, :], ps[:], after=[m], chain=False))

        def rope_into(dst):
            def done(c, h, ps, m):
                n = h % 2
                hs = slice(h * BANK, (h + 1) * BANK)
                V(dve.tensor_tensor, t_cos[n][:], ps, cos[:, hs], ALU.mult, after=[m, *pr.free.get(f"rope{n}", ())],
                  chain=False)
                for q in range(4):
                    o, i_ = 32 * q, 32 * (q ^ 1)
                    e = V(dve.tensor_tensor, t_sin[n][o:o + 32, :], ps[i_:i_ + 32, :], sin[o:o + 32, hs], ALU.mult,
                          chain=False)
                pr.free[f"rope{n}"] = [G(pool.tensor_tensor, dst[:, c, hs], t_cos[n][:], t_sin[n][:], ALU.add,
                                         after=[e])]
                return e
            return done
        project(w_in2, 0, 512, rope_into(mix2))
        project(w_in2, 512, 512, rope_into(k_feat))
        pr.barrier()
    pr.barrier()

    SPAN = 2 * T - P
    ln_count = sb("ln_count", [P, SPAN], where=at_space)
    with ExitStack() as ph:
        dist, rem, d2, in4 = (ft[0][:].rearrange("p a b -> p (a b)")[:, n * SPAN:(n + 1) * SPAN] for n in range(4))
        dist, rem = dist.bitcast(I32), rem.bitcast(I32)
        in16 = ln_count
        G(pool.iota, dist, pattern=[[1, SPAN]], base=-(T - P), channel_multiplier=-1)
        V(dve.tensor_copy, d2, dist, after=[G.last])
        V(dve.tensor_tensor, d2, d2, d2, ALU.mult)
        for mask, dil in ((in4, 4), (in16[:], 16)):
            V(dve.tensor_scalar, rem, dist, dil - 1, None, ALU.bitwise_and)
            V(dve.tensor_copy, mask, rem)
            V(dve.tensor_scalar, mask, mask, 0.0, None, ALU.is_equal)
            V(dve.scalar_tensor_tensor, mask, d2, float((RADIUS * dil) ** 2), mask, ALU.is_le, ALU.mult)
        V(dve.scalar_tensor_tensor, in4, d2, float(RADIUS ** 2), in4, ALU.is_le, ALU.add)
        V(dve.tensor_tensor, in4, in4, in16[:], ALU.add)
        m = V(dve.tensor_scalar, in16[:], in4, 1.0, None, ALU.max)
        A(act.activation, in16[:], in16[:], ACT.Ln, after=[m])
        V(dve.tensor_scalar, in4, in4, 1.0, -1.0, ALU.min, ALU.add)
        V(dve.scalar_tensor_tensor, ln_count[:], in4, 1e30, in16[:], ALU.mult, ALU.add, after=[A.last])
        pr.barrier()

    q_now = [sb(f"q_now{n}", [P, T], where=at_space) for n in range(2)]
    k_now = [sb(f"k_now{n}", [P, T], where=at_space) for n in range(2)]
    v_now = [sb(f"v_now{n}", [P, NT, P], where=at_space) for n in range(2)]
    scores = [sb(f"scores{n}", [P, T], where=at_space) for n in range(AHEAD + 1)]
    row_stat = sb("row_stat", [P, AHEAD + 1, 4], where=at_space)
    p_t = ft[0][:].rearrange("p a (b c) -> p a b c", b=2)

    def exp_rows(s, n_keys, st, after):
        V(dve.tensor_reduce, st[:, 0:1], s[:, 0:n_keys], AX, ALU.max, after=after)
        m = V(dve.tensor_scalar, st[:, 1:2], st[:, 0:1], -1.0, None, ALU.mult)
        return A(act.activation, s[:, 0:n_keys], s[:, 0:n_keys], ACT.Exp, bias=st[:, 1:2], accum_out=st[:, 2:3],
                 after=[m], chain=False)

    def norm_rows_of(s, n_keys, st, after):
        m = V(dve.reciprocal, st[:, 3:4], st[:, 2:3], after=after)
        return A(act.activation, s[:, 0:n_keys], s[:, 0:n_keys], ACT.Copy, scale=st[:, 3:4], after=[m], chain=False)

    act.preload_act_table_set("natural_log_exp_and_others")
    with pr.repeat("dilated", HEADS // 4) as i:
        ready, transposed, now_ready = {}, {}, {}
        for pair in range(2):
            G(pool.tensor_copy, q_now[pair][:], mix2[:, bass.ds(i * 2 + pair, 1), :].rearrange("p a b -> p (a b)"),
              after=pr.free.get(f"q_now{pair}", ()))
            G(pool.tensor_copy, k_now[pair][:], k_feat[:, bass.ds(i * 2 + pair, 1), :].rearrange("p a b -> p (a b)"))
            now_ready[pair] = G(pool.tensor_copy, v_now[pair][:], v_tok[:, :, bass.ds((i * 2 + pair) * P, P)],
                                after=pr.free.get(f"v_now{pair}", ()))

        def place(u):
            pair, half, tile, hb = u // 16, u // 8 % 2, u % 8 // 2, u % 2
            return pair, half, tile, hb, slice(hb * HD, (hb + 1) * HD), u % (AHEAD + 1)

        def score(u):
            pair, half, tile, hb, rows, slot = place(u)
            n = half * 4 + tile
            st, s = row_stat[:, slot, :], scores[slot]
            for h in range(2):
                b, ps = bank(now_ready[pair])
                m = PE(te.matmul, ps[:], q_now[pair][rows, n * P:(n + 1) * P],
                       k_now[pair][rows, h * BANK:(h + 1) * BANK], start=True, stop=True)
                x0 = T - P - n * P + h * BANK
                e = V(dve.scalar_tensor_tensor, s[:, h * BANK:(h + 1) * BANK], ps[:], HD ** -0.5,
                      ln_count[:, x0:x0 + BANK], ALU.mult, ALU.add,
                      after=[m, *pr.free.get(f"scores{slot}", ())], chain=False)
                emptied(b, e)
            pr.free[f"q_now{pair}"] = [m]
            ready[u] = exp_rows(s, T, st, [e])

        def finish(u):
            slot = place(u)[-1]
            ready[u] = norm_rows_of(scores[slot], T, row_stat[:, slot, :], [ready[u]])

        def turn_weights(u):
            pair, half, tile, hb, rows, slot = place(u)
            s = scores[slot]
            for h in range(2):
                b, ps = bank(ready[u])
                for k in range(4):
                    m = te.transpose(ps[:, k * P:(k + 1) * P], s[:, (4 * h + k) * P:(4 * h + k + 1) * P], ident[:])
                m = PE.done.inc(m)
                o = p_t[:, 4 * h:4 * h + 4, hb, tile * P:(tile + 1) * P]
                src = ps[:].rearrange("p (a b) -> p a b", a=4)
                if h == 0:
                    e0 = A(act.copy, o, src, after=[m, *pr.free.get("p_t", ())], chain=False)
                    emptied(b, e0)
                else:
                    e1 = V(dve.tensor_copy, o, src, after=[m, *pr.free.get("p_t", ())], chain=False)
                    emptied(b, e1)
            pr.free[f"scores{slot}"] = [m]
            transposed[u] = [e0, e1]

        def weigh(first):
            pair, half = place(first)[:2]
            b, ps = bank(*[m for u in range(first, first + 8) for m in transposed[u]])
            for hb in range(2):
                for k in range(NT):
                    m = te.matmul(ps[hb * HD:(hb + 1) * HD, :], v_now[pair][:, k, hb * HD:(hb + 1) * HD],
                                  p_t[:, k, hb, :], start=(k == 0), stop=(k == NT - 1))
            m = PE.done.inc(m)
            pr.free["p_t"] = pr.free[f"v_now{pair}"] = [m]
            emptied(b, A(act.copy, mix2[:, bass.ds(i * 2 + pair, 1), half * BANK:(half + 1) * BANK].rearrange(
                "p a b -> p (a b)"), ps[:], after=[m], chain=False))

        UNITS = 32
        for u in range(AHEAD):
            score(u)
        finish(0)
        for u in range(UNITS):
            if u < UNITS - AHEAD:
                score(u + AHEAD)
            if u < UNITS - 1:
                finish(u + 1)
            if u and u % 8 == 0:
                weigh(u - 8)
            turn_weights(u)
        weigh(UNITS - 8)
    at_space.close()

    project_tokens(lambda k, n: (mix2[:, k, n * P:(n + 1) * P],), 8, dram["w_out_2"][0], 0, 0, (0, 1), add_residual)

    rms_norm_features("norm_cross", "norm_cross_g")
    with ExitStack() as ph:
        k_mem = sb("k_mem", [P, CROSS, MEM], where=ph)
        v_mem = sb("v_mem", [P, MEM // P, 512], where=ph)
        mem_ft = sb("mem_ft", [P, KD, MEM], where=ph)
        with norm_space() as nph:
            mem_t = sb("mem_t", [P, MEM // P, D], where=nph)
            SP.wait(Mark(V.done, V.done.count, None), Mark(A.done, A.done.count, None),
                    Mark(PE.done, PE.done.count, None))
            m_mem = loads("mem").inc(nc.sync.dma_start(mem_t[:], dram["mem_2"][0].rearrange("(n p) d -> p n d", p=P)))
            A.wait(m_mem)
            squares_of(None, mem_t, MEM // P)
            for n in range(MEM // P):
                V.wait(A.last)
                m = normed(mem_t, n, n, False)
                to_features(xhat[n], [mem_ft], n * P, P, lambda k: col("norm_mem_g", k), None, [m], f"xhat{n}")
        for c, wt in enumerate(stream([rows_of(dram["w_ck_2"][0], 0, D, c * P, P) for c in range(CROSS)])):
            PE.wait(*wt.ready)
            b, ps = bank()
            m = PE.done.inc(products(ps[:, 0:MEM], [(wt.at(k), (mem_ft[:, k, :],)) for k in range(KD)]))
            wt.used(m)
            emptied(b, A(act.copy, k_mem[:, c, :], ps[:, 0:MEM], after=[m], chain=False))
        project_tokens(lambda k, n: (mem_ft[:, k, n * P:(n + 1) * P],), KD, dram["w_cv_2"][0], 0, 0, (0,),
                       lambda h, n, ps, m: V(dve.tensor_copy, v_mem[:, n, :], ps[:], after=[m], chain=False),
                       n_tiles=MEM // P)

        def q_done(c, h, ps, m):
            return A(act.copy, mix2[:, c, h * BANK:(h + 1) * BANK], ps, after=[m], chain=False)
        project(dram["w_cq_2"][0], 0, 512, q_done)

        q_h, k_h, v_h = ([sb(f"{name}{n}", shape, where=ph) for n in range(2)] for name, shape in
                         (("q_h", [P, T]), ("k_h", [P, MEM]), ("v_h", [P, MEM // P, P])))
        scores = [sb(f"c_scores{n}", [P, MEM], where=ph) for n in range(4)]
        row_stat = sb("c_row_stat", [P, 4, 4], where=ph)
        p_tc = [sb(f"p_tc{n}", [P, MEM // P, BANK], where=ph) for n in range(2)]
        with pr.repeat("cross", CROSS // 2) as i:
            now_ready, ready, transposed = {}, {}, {}
            for e in range(2):
                m_q = A(act.copy, q_h[e][:], mix2[:, bass.ds(i * 2 + e, 1), :].rearrange("p a b -> p (a b)"),
                        after=pr.free.get(f"q_h{e}", ()))
                G(pool.tensor_copy, k_h[e][:], k_mem[:, bass.ds(i * 2 + e, 1), :].rearrange("p a b -> p (a b)"),
                  after=pr.free.get(f"q_h{e}", ()))
                now_ready[e] = [m_q, G(pool.tensor_copy, v_h[e][:], v_mem[:, :, bass.ds((i * 2 + e) * P, P)])]

            def c_score(u):
                e, n = divmod(u, NT)
                s = scores[u % 4]
                b, ps = bank(*now_ready[e])
                m = PE(te.matmul, ps[:, 0:MEM], q_h[e][:, n * P:(n + 1) * P], k_h[e][:], start=True, stop=True)
                m = A(act.mul, s[:], ps[:, 0:MEM], float(P) ** -0.5,
                      after=[m, *pr.free.get(f"c_scores{u % 4}", ())], chain=False)
                emptied(b, m)
                ready[u] = exp_rows(s, MEM, row_stat[:, u % 4, :], [m])

            def c_finish(u):
                ready[u] = norm_rows_of(scores[u % 4], MEM, row_stat[:, u % 4, :], [ready[u]])

            def c_turn(u):
                b, ps = bank(ready[u])
                for k in range(2):
                    m = te.transpose(ps[:, k * P:(k + 1) * P], scores[u % 4][:, k * P:(k + 1) * P], ident[:])
                m = PE.done.inc(m)
                pr.free[f"c_scores{u % 4}"] = [m]
                half = u // 4 % 2
                e = V(dve.tensor_copy, p_tc[half][:, :, (u % 4) * P:(u % 4 + 1) * P],
                      ps[:, 0:2 * P].rearrange("p (a b) -> p a b", a=2), after=[m, *pr.free.get(f"p_tc{half}", ())],
                      chain=False)
                emptied(b, e)
                transposed[u] = e

            def c_weigh(first):
                e, half = first // NT, first // 4 % 2
                b, ps = bank(*[transposed[u] for u in range(first, first + 4)])
                for k in range(2):
                    m = te.matmul(ps[:], v_h[e][:, k, :], p_tc[half][:, k, :], start=(k == 0), stop=(k == 1))
                m = PE.done.inc(m)
                pr.free[f"p_tc{half}"] = [m]
                emptied(b, V(dve.tensor_scalar,
                             mix2[:, bass.ds(i * 2 + e, 1), half * BANK:(half + 1) * BANK].rearrange(
                                 "p a b -> p (a b)"), ps[:], 1.0, None, ALU.mult, after=[m], chain=False))
                pr.free[f"q_h{e}"] = [m]

            units = 2 * NT
            for u in range(3):
                c_score(u)
            c_finish(0)
            for u in range(units):
                if u < units - 3:
                    c_score(u + 3)
                if u < units - 1:
                    c_finish(u + 1)
                c_turn(u)
                if u % 4 == 1 and u > 4:
                    c_weigh(u - 5)
            c_weigh(units - 4)
        project_tokens(lambda k, n: (mix2[:, k, n * P:(n + 1) * P],), 4, dram["w_co_2"][0], 0, 0, (0, 1), add_residual)
        pr.barrier()

    mix2_space.close()
    open_ft(2)
    rms_norm_features("norm_mlp", "norm_mlp_g")
    w_mi, w_mo = dram["w_mlp_in_2"][0], dram["w_mlp_out_2"][0]
    with ExitStack() as ph:
        hid = [[sb(f"mlp_hid{n}", [P, T], F32R, ph) for _ in range(2)] for n in range(4)]
        act_tmp = [sb(f"mlp_act{n}", [P, BANK], where=ph) for n in range(2)]
        sq_tmp = [sb(f"mlp_square{n}", [P, BANK], where=ph) for n in range(2)]
        with halved_panels(3), pr.repeat("mlp", NFF2 // 4) as i:
            sources = [(c, rows_of(w_mi, 0, D, i * 4 * P + c * P, P)) for c in range(4)]
            sources += [(4 + u * 2 + h, rows_of(w_mo, i * 4 * P + u * 2 * P, 2 * P, h * BANK, BANK))
                        for u in range(2) for h in range(2)]
            hid_ready = {}
            for (c, _), wt in zip(sources, stream([x for _, x in sources])):
                PE.wait(*wt.ready)
                if c < 4:
                    hi, lo = hid[c]
                    for h in range(HALVES):
                        hs = slice(h * BANK, (h + 1) * BANK)
                        b, ps = bank()
                        mm = PE.done.inc(products(ps[:], [(wt.at(k), ft_at(k, hs)) for k in range(KD)]))
                        m = A(act.activation, act_tmp[h][:], ps[:], ACT.Relu,
                              after=[mm, *pr.free.get(f"act_tmp{h}", ())], chain=False)
                        emptied(b, m)
                        m = V(dve.tensor_tensor, sq_tmp[h][:], act_tmp[h][:], act_tmp[h][:], ALU.mult,
                              after=[m, *pr.free.get(f"sq_tmp{h}", ())], chain=False)
                        pr.free[f"act_tmp{h}"] = [m]
                        m = A(act.activation, hi[:, hs], sq_tmp[h][:], ACT.Copy,
                              after=[m, *pr.free.get(f"mhid{c // 2}", ())], chain=False)
                        m = V(dve.tensor_tensor, lo[:, hs], sq_tmp[h][:], f32(hi[:, hs]), ALU.subtract, after=[m],
                              chain=False)
                        pr.free[f"sq_tmp{h}"] = [m]
                    wt.used(mm)
                    hid_ready[c] = m
                else:
                    u, h = divmod(c - 4, 2)
                    PE.wait(hid_ready[2 * u], hid_ready[2 * u + 1])
                    for n in range(NT):
                        b, ps = bank()
                        m = PE.done.inc(products(ps[:], [(tuple(x[:, n * P:(n + 1) * P] for x in hid[2 * u + j]),
                                                          wt.at(j)) for j in range(2)]))
                        emptied(b, add_residual(h, n, ps, m))
                    wt.used(m)
                    pr.free[f"mhid{u}"] = [m]

    pr.barrier()
    ft_space.close()

    with norm_space(("norm_final_g_2",)) as nph:
        out_t = [sb(f"out_t{n}", [P, D], where=nph) for n in range(2)]
        stored = [Counter(pr, f"out{n}_stored", 16) for n in range(2)]
        squares_of("final_squares", resid)
        dst = dram["out"][0].rearrange("(n p) d -> n p d", p=P)
        with pr.repeat("final", NT // 2) as i:
            for n in range(2):
                normed(resid, i * 2 + n, n, False)
                m = V(dve.tensor_tensor, out_t[n][:], xhat[n][:], norm_rows[:, 0, :], ALU.mult,
                      after=pr.free.get(f"out_t{n}", ()))
                pr.free[f"xhat{n}"] = [m]
                SP.wait(m)
                pr.free[f"out_t{n}"] = [stored[n].inc(nc.sync.dma_start(
                    dst[bass.ds(i * 2 + n, 1)].rearrange("a p d -> p (a d)"), out_t[n][:]))]
        for s in stored:
            SP.wait(Mark(s, s.count, None))


def rotary_frequencies(np):
    half = HD // 2
    freq = np.float32(10000.0) ** (-np.arange(half, dtype=np.float32) / np.float32(half))
    return np.tile(freq.astype(np.float32), P // half)[:, None]


def kernel(**inputs):
    import numpy as np
    import concourse.bacc as bacc
    from concourse.bass_utils import run_bass_kernel_spmd

    arrays = {f"in_{name}": np.ascontiguousarray(a) for name, a in inputs.items()}
    arrays["in_inv_freq"] = rotary_frequencies(np)

    def declare(nc):
        dram = {name[3:]: nc.dram_tensor(name, a.shape, mybir.dt.from_np(a.dtype), kind="ExternalInput").ap()
                for name, a in arrays.items()}
        dram["out"] = nc.dram_tensor("out", (1, T, D), F32, kind="ExternalOutput").ap()
        return dram

    def fresh():
        return bacc.Bacc("TRN2", target_bir_lowering=False, num_devices=1)

    counting = fresh()
    plan = build(counting, declare(counting), {})
    nc = fresh()
    assert build(nc, declare(nc), plan) == plan
    r = run_bass_kernel_spmd(nc, [arrays], core_ids=[0])
    return r.results[0]["out"]
```
